# Optimizing a Trainium2 kernel written in Bass

```python
import math
import jax, jax.numpy as jnp
from jax import lax
import numpy as np

D_MODEL = 1024
BATCH = 1
SEQ = 256
DEPTH = 2

GRID_W = 64
CTX_LEN = 256
EPS = 1e-6

A_WIDTH = 512
A_GROUPS = 4
A_GROUP_DIM = A_WIDTH // A_GROUPS
A_CHUNK = 128

B_HEADS = 8
B_Q_LORA = 384
B_KV_LORA = 256
B_NOPE = 64
B_ROPE = 32
B_VDIM = 64
B_BLOCK = 128
ROPE_BASE = 10000.0
ROPE_FREQS = B_ROPE // 4
MLA_SCALE = (B_NOPE + B_ROPE) ** -0.5

C_HEADS = 8
C_HEAD = 64
C_WIDTH = C_HEADS * C_HEAD
C_DECAY_LORA = 64
C_AAA_LORA = 64
C_GATE_LORA = 128
C_N_DIR = 2
C_GN_EPS = 64e-5
DECAY_SCALE = 0.6065306597126334

B_COLS = B_Q_LORA + B_KV_LORA + B_ROPE
C_COLS = 3 * C_WIDTH + C_N_DIR * C_DECAY_LORA + C_N_DIR * C_AAA_LORA + C_GATE_LORA
A_COLS = 2 * A_WIDTH
G_COLS = 3 * D_MODEL
IN_COLS = B_COLS + C_COLS + A_COLS + G_COLS
Q_SL = slice(0, B_Q_LORA)
KV_SL = slice(B_Q_LORA, B_Q_LORA + B_KV_LORA)
KR_SL = slice(B_Q_LORA + B_KV_LORA, B_COLS)
C_SL = slice(B_COLS, B_COLS + C_COLS)
A_SL = slice(B_COLS + C_COLS, B_COLS + C_COLS + A_COLS)
G_SL = slice(B_COLS + C_COLS + A_COLS, IN_COLS)

N_EXPERTS = 16
N_GROUPS = 4
EXPERTS_PER_GROUP = N_EXPERTS // N_GROUPS
TOP_GROUPS = 1
TOP_K = 2
D_EXPERT = 512

kernel_name = 'hybrid_mla_rwkv7_gmlp_moe_dit'

def rmsnorm(x, g):
    xf = x.astype(jnp.float32)
    y = xf * lax.rsqrt(jnp.mean(xf * xf, axis=-1, keepdims=True) + EPS)
    return (y * g.astype(jnp.float32)).astype(x.dtype)

def axial_rope_tables(rows, dtype):
    row = jnp.repeat(jnp.arange(rows, dtype=jnp.float32), GRID_W)
    col = jnp.tile(jnp.arange(GRID_W, dtype=jnp.float32), rows)
    inv = jnp.power(ROPE_BASE, -jnp.arange(ROPE_FREQS, dtype=jnp.float32) / ROPE_FREQS)
    ang = jnp.stack([row[:, None] * inv, col[:, None] * inv], axis=1)
    return jnp.cos(ang).astype(dtype), jnp.sin(ang).astype(dtype)

def apply_axial_rope(x, cos, sin):
    xs = x.reshape(x.shape[:-1] + (2, 2, ROPE_FREQS))
    x1, x2 = xs[..., 0, :], xs[..., 1, :]
    out = jnp.stack([x1 * cos - x2 * sin, x2 * cos + x1 * sin], axis=-2)
    return out.reshape(x.shape)

def centred_shift(z):
    zp = jnp.pad(z, ((0, 0), (1, 1), (0, 0)))
    return 0.5 * (zp[:, :-2] + zp[:, 2:])

def chunk_gmlp(za, v_gain, w_s, b_s):
    zg = jax.nn.gelu(za)
    u, v = zg[..., :A_WIDTH], zg[..., A_WIDTH:]
    v = rmsnorm(v, v_gain)
    Bn, T, _ = v.shape
    vc = v.reshape(Bn, T // A_CHUNK, A_CHUNK, A_GROUPS, A_GROUP_DIM)
    mixed = jnp.einsum('gij,bnjgc->bnigc', w_s, vc) + b_s.T[None, None, :, :, None]
    return u * mixed.reshape(Bn, T, A_WIDTH)

def mla_queries(zq, q_norm_g, w_uq):
    Bn, T, _ = zq.shape
    q = (rmsnorm(zq, q_norm_g) @ w_uq).reshape(Bn, T, B_HEADS, B_NOPE + B_ROPE)
    return q[..., :B_NOPE], q[..., B_NOPE:]

def mla_keys_values(zkv, kv_norm_g, w_ukv):
    Bn, T, _ = zkv.shape
    kv = (rmsnorm(zkv, kv_norm_g) @ w_ukv).reshape(Bn, T, B_HEADS, B_NOPE + B_VDIM)
    return kv[..., :B_NOPE], kv[..., B_NOPE:]

def mla_attend(q_nope, q_rope, k_nope, k_rope, v):
    Bn, Tq = q_nope.shape[:2]
    nblk = Tq // B_BLOCK

    def to_blocks(t):
        return jnp.moveaxis(t.reshape((Bn, nblk, B_BLOCK) + t.shape[2:]), 1, 0)

    def one_block(qb):
        qn, qr = qb
        s = jnp.einsum('bqhd,bkhd->bhqk', qn, k_nope) + jnp.einsum('bqhr,bkr->bhqk', qr, k_rope)
        p = jax.nn.softmax(s.astype(jnp.float32) * MLA_SCALE, axis=-1).astype(v.dtype)
        return jnp.einsum('bhqk,bkhd->bqhd', p, v)

    o = lax.map(one_block, (to_blocks(q_nope), to_blocks(q_rope)))
    return jnp.moveaxis(o, 0, 1).reshape(Bn, Tq, B_HEADS * B_VDIM)

def rwkv_features(zc, mu, w0, w2, a0, a2, k_k, k_a):
    f32 = jnp.float32
    zc = zc + mu * (centred_shift(zc) - zc)
    Bn, T, _ = zc.shape
    heads = lambda t: t.reshape(Bn, T, C_HEADS, C_HEAD)
    dirs = lambda t: t.reshape(Bn, T, C_N_DIR, C_HEADS, C_HEAD)
    r = heads(zc[..., 0:C_WIDTH]).astype(f32)
    k = zc[..., C_WIDTH:2 * C_WIDTH]
    v = heads(zc[..., 2 * C_WIDTH:3 * C_WIDTH]).astype(f32)
    o = 3 * C_WIDTH
    zw = zc[..., o:o + C_N_DIR * C_DECAY_LORA].reshape(Bn, T, C_N_DIR, C_DECAY_LORA)
    o += C_N_DIR * C_DECAY_LORA
    za = zc[..., o:o + C_N_DIR * C_AAA_LORA].reshape(Bn, T, C_N_DIR, C_AAA_LORA)
    o += C_N_DIR * C_AAA_LORA
    zg = zc[..., o:]
    w_logit = w0 + jnp.einsum('btdl,dlc->btdc', jnp.tanh(zw), w2)
    w = jnp.exp(-DECAY_SCALE * jax.nn.sigmoid(w_logit.astype(f32)))
    a = jax.nn.sigmoid((a0 + jnp.einsum('btdl,dlc->btdc', za, a2)).astype(f32))
    kk = heads(k * k_k).astype(f32)
    kk = kk * lax.rsqrt(jnp.maximum(jnp.sum(kk * kk, axis=-1, keepdims=True), 1e-12))
    kd = k.astype(f32)[:, :, None, :] * (1.0 + (a - 1.0) * k_a.astype(f32))
    return r, v, kk, dirs(w), dirs(a), dirs(kd), zg

def rwkv_scan(r, w, k, v, kk, a, s0, reverse, emit):
    def step(S, inp):
        if emit:
            w_t, k_t, v_t, kk_t, a_t, r_t = inp
        else:
            w_t, k_t, v_t, kk_t, a_t = inp
        sa = jnp.einsum('bhvk,bhk->bhv', S, -kk_t)
        S = S * w_t[:, :, None, :] + sa[..., None] * (kk_t * a_t)[:, :, None, :] + v_t[..., None] * k_t[:, :, None, :]
        return S, (jnp.einsum('bhvk,bhk->bhv', S, r_t) if emit else None)

    seq = (w, k, v, kk, a, r) if emit else (w, k, v, kk, a)
    xs = tuple(jnp.moveaxis(t, 1, 0) for t in seq)
    S, out = lax.scan(step, s0, xs, reverse=reverse)
    return S, (jnp.moveaxis(out, 0, 1) if emit else None)

def rwkv_direction(feats, d, s0, emit):
    r, v, kk, w, a, kd, _ = feats
    return rwkv_scan(r, w[:, :, d], kd[:, :, d], v, kk, a[:, :, d], s0, d == 1, emit)

def rwkv_readout(o, feats, g2, r_k, gn_g, gn_b):
    r, v, kk, w, a, kd, zg = feats
    Bn, T = o.shape[:2]
    m = jnp.mean(o, axis=-1, keepdims=True)
    var = jnp.mean(jnp.square(o - m), axis=-1, keepdims=True)
    y = ((o - m) * lax.rsqrt(var + C_GN_EPS)).reshape(Bn, T, C_WIDTH) * gn_g + gn_b
    bonus = jnp.sum(r[:, :, None] * kd * r_k, axis=-1, keepdims=True) * v[:, :, None]
    y = y + jnp.sum(bonus, axis=2).reshape(Bn, T, C_WIDTH)
    g = jax.nn.sigmoid(zg) @ g2
    return y.astype(g.dtype) * g

def merge_branches(zg, y_a, y_b, y_c, w_up_a, w_up_b, w_up_c, w_o):
    g = jax.nn.sigmoid(zg)
    g_a, g_b, g_c = g[..., :D_MODEL], g[..., D_MODEL:2 * D_MODEL], g[..., 2 * D_MODEL:]
    return (g_a * (y_a @ w_up_a) + g_b * (y_b @ w_up_b) + g_c * (y_c @ w_up_c)) @ w_o

def moe(h, router_w, router_b, w1, w3, w2):
    Bn, T, D = h.shape
    t = h.reshape(Bn * T, D)
    scores = jax.nn.sigmoid((t @ router_w).astype(jnp.float32))
    sel = scores + router_b.astype(jnp.float32)
    grp_score = jnp.sum(lax.top_k(sel.reshape(-1, N_GROUPS, EXPERTS_PER_GROUP), 2)[0], axis=-1)
    _, gidx = lax.top_k(grp_score, TOP_GROUPS)
    gmask = jnp.sum(jax.nn.one_hot(gidx, N_GROUPS, dtype=jnp.float32), axis=1)
    emask = jnp.repeat(gmask, EXPERTS_PER_GROUP, axis=1)
    _, eidx = lax.top_k(jnp.where(emask > 0, sel, -jnp.inf), TOP_K)
    wsel = jnp.take_along_axis(scores, eidx, axis=-1)
    wsel = wsel / jnp.sum(wsel, axis=-1, keepdims=True)
    comb = jnp.sum(jax.nn.one_hot(eidx, N_EXPERTS, dtype=jnp.float32) * wsel[..., None], axis=1).astype(t.dtype)
    out = jnp.zeros_like(t)
    for e in range(N_EXPERTS):
        he = jax.nn.silu(t @ w1[e]) * (t @ w3[e])
        out = out + comb[:, e:e + 1] * (he @ w2[e])
    return out.reshape(Bn, T, D)

def setup_inputs(seed: int = 0) -> dict:
    key = jax.random.key(seed)
    ks = jax.random.split(key, 48)
    counter = [0]

    def nxt():
        k = ks[counter[0]]
        counter[0] += 1
        return k

    def nrm(shape, scale):
        return jax.random.normal(nxt(), shape, jnp.float32) * scale

    def gain(shape):
        return 1.0 + nrm(shape, 0.02)

    L, D = DEPTH, D_MODEL
    return {
        'x': nrm((BATCH, SEQ, D), 1.0),
        'c': nrm((BATCH, D), 1.0),
        'ctx': nrm((BATCH, CTX_LEN, D), 1.0),
        'c_ctx': nrm((D,), 1.0),
        'mod_w': nrm((L, D, 6 * D), 0.5 * D ** -0.5),
        'mod_b': nrm((L, 6 * D), 0.02),
        'norm1_g': gain((L, D)),
        'norm2_g': gain((L, D)),
        'w_in': nrm((L, D, IN_COLS), D ** -0.5),
        'a_v_gain': gain((L, A_WIDTH)),
        'a_ws': nrm((L, A_GROUPS, A_CHUNK, A_CHUNK), 0.5 * A_CHUNK ** -0.5),
        'a_bs': gain((L, A_GROUPS, A_CHUNK)),
        'b_q_norm': gain((L, B_Q_LORA)),
        'b_w_uq': nrm((L, B_Q_LORA, B_HEADS * (B_NOPE + B_ROPE)), B_Q_LORA ** -0.5),
        'b_kv_norm': gain((L, B_KV_LORA)),
        'b_w_ukv': nrm((L, B_KV_LORA, B_HEADS * (B_NOPE + B_VDIM)), B_KV_LORA ** -0.5),
        'c_mu': jax.random.uniform(nxt(), (L, C_COLS), jnp.float32),
        'c_w0': nrm((L, C_N_DIR, C_WIDTH), 0.5),
        'c_w2': nrm((L, C_N_DIR, C_DECAY_LORA, C_WIDTH), 0.5 * C_DECAY_LORA ** -0.5),
        'c_a0': nrm((L, C_N_DIR, C_WIDTH), 0.5),
        'c_a2': nrm((L, C_N_DIR, C_AAA_LORA, C_WIDTH), 0.5 * C_AAA_LORA ** -0.5),
        'c_g2': nrm((L, C_GATE_LORA, C_WIDTH), C_GATE_LORA ** -0.5),
        'c_k_k': 1.0 + nrm((L, C_WIDTH), 0.1),
        'c_k_a': 1.0 + nrm((L, C_WIDTH), 0.1),
        'c_r_k': nrm((L, C_HEADS, C_HEAD), 0.1),
        'c_gn_g': gain((L, C_WIDTH)),
        'c_gn_b': nrm((L, C_WIDTH), 0.02),
        'w_up_a': nrm((L, A_WIDTH, D), A_WIDTH ** -0.5),
        'w_up_b': nrm((L, B_HEADS * B_VDIM, D), (B_HEADS * B_VDIM) ** -0.5),
        'w_up_c': nrm((L, C_WIDTH, D), C_WIDTH ** -0.5),
        'w_o': nrm((L, D, D), D ** -0.5),
        'router_w': nrm((D, N_EXPERTS), D ** -0.5),
        'router_b': nrm((N_EXPERTS,), 0.01),
        'moe_w1': nrm((L, N_EXPERTS, D, D_EXPERT), D ** -0.5),
        'moe_w3': nrm((L, N_EXPERTS, D, D_EXPERT), D ** -0.5),
        'moe_w2': nrm((L, N_EXPERTS, D_EXPERT, D), D_EXPERT ** -0.5),
        'final_g': gain((D,)),
    }

def reference(x, c, ctx, c_ctx, mod_w, mod_b, norm1_g, norm2_g, w_in,
              a_v_gain, a_ws, a_bs, b_q_norm, b_w_uq, b_kv_norm, b_w_ukv,
              c_mu, c_w0, c_w2, c_a0, c_a2, c_g2, c_k_k, c_k_a, c_r_k, c_gn_g, c_gn_b,
              w_up_a, w_up_b, w_up_c, w_o, router_w, router_b, moe_w1, moe_w3, moe_w2, final_g):
    Bn, T, _ = x.shape
    rows = T // GRID_W
    cos, sin = axial_rope_tables(rows, x.dtype)
    c_act = jax.nn.silu(c)
    cc_act = jax.nn.silu(c_ctx)
    xc = ctx
    for l in range(DEPTH):
        last = l == DEPTH - 1
        sh1, sc1, ga1, sh2, sc2, ga2 = jnp.split((c_act @ mod_w[l] + mod_b[l])[:, None, :], 6, axis=-1)
        sh1c, sc1c, ga1c, sh2c, sc2c, ga2c = jnp.split((cc_act @ mod_w[l] + mod_b[l])[None, None, :], 6, axis=-1)

        h = rmsnorm(x, norm1_g[l]) * (1 + sc1) + sh1
        hc = rmsnorm(xc, norm1_g[l]) * (1 + sc1c) + sh1c
        z = h @ w_in[l]
        zc = hc @ (w_in[l][:, :B_COLS + C_COLS] if last else w_in[l])

        kn_c, v_c = mla_keys_values(zc[..., KV_SL], b_kv_norm[l], b_w_ukv[l])
        kr_c = zc[..., KR_SL]
        kn, v = mla_keys_values(z[..., KV_SL], b_kv_norm[l], b_w_ukv[l])
        kr = apply_axial_rope(z[..., KR_SL], cos, sin)
        qn, qr = mla_queries(z[..., Q_SL], b_q_norm[l], b_w_uq[l])
        qr = apply_axial_rope(qr, cos[:, None], sin[:, None])
        y_b = mla_attend(qn, qr, jnp.concatenate([kn_c, kn], axis=1),
                         jnp.concatenate([kr_c, kr], axis=1), jnp.concatenate([v_c, v], axis=1))

        rw = (c_mu[l], c_w0[l], c_w2[l], c_a0[l], c_a2[l], c_k_k[l], c_k_a[l])
        f_lat = rwkv_features(z[..., C_SL], *rw)
        f_ctx = rwkv_features(zc[..., C_SL], *rw)
        s0 = jnp.zeros((Bn, C_HEADS, C_HEAD, C_HEAD), jnp.float32)
        s_f, oc_f = rwkv_direction(f_ctx, 0, s0, not last)
        s_b, oc_b = rwkv_direction(f_ctx, 1, s0, not last)
        _, ol_f = rwkv_direction(f_lat, 0, s_f, True)
        _, ol_b = rwkv_direction(f_lat, 1, s_b, True)
        y_c = rwkv_readout(ol_f + ol_b, f_lat, c_g2[l], c_r_k[l], c_gn_g[l], c_gn_b[l])

        y_a = chunk_gmlp(z[..., A_SL], a_v_gain[l], a_ws[l], a_bs[l])

        x_new = x + ga1 * merge_branches(z[..., G_SL], y_a, y_b, y_c, w_up_a[l], w_up_b[l], w_up_c[l], w_o[l])
        h2 = rmsnorm(x_new, norm2_g[l]) * (1 + sc2) + sh2
        x_new = x_new + ga2 * moe(h2, router_w, router_b, moe_w1[l], moe_w3[l], moe_w2[l])

        if not last:
            qn_c, qr_c = mla_queries(zc[..., Q_SL], b_q_norm[l], b_w_uq[l])
            y_bc = mla_attend(qn_c, qr_c, kn_c, kr_c, v_c)
            y_cc = rwkv_readout(oc_f + oc_b, f_ctx, c_g2[l], c_r_k[l], c_gn_g[l], c_gn_b[l])
            y_ac = chunk_gmlp(zc[..., A_SL], a_v_gain[l], a_ws[l], a_bs[l])
            xc_new = xc + ga1c * merge_branches(zc[..., G_SL], y_ac, y_bc, y_cc, w_up_a[l], w_up_b[l], w_up_c[l], w_o[l])
            h2c = rmsnorm(xc_new, norm2_g[l]) * (1 + sc2c) + sh2c
            xc = xc_new + ga2c * moe(h2c, router_w, router_b, moe_w1[l], moe_w3[l], moe_w2[l])
        x = x_new
    return rmsnorm(x, final_g)


_drawn_inputs = setup_inputs


def setup_inputs(seed=0):
    import zlib

    import numpy as np

    out = dict(_drawn_inputs(seed))
    spreads = {}
    factors = {'a_v_gain': 8.0,
     'a_bs': 5.905,
     'b_q_norm': 8.0,
     'b_kv_norm': 8.0,
     'c_k_k': 2.966,
     'c_gn_g': 3.576,
     'c_gn_b': 4.268,
     'final_g': 2.69}
    for name, (base, spread) in spreads.items():
        noise = np.random.default_rng([zlib.crc32(name.encode()), seed]).standard_normal(out[name].shape)
        drawn = base * np.exp(spread * noise) if base else spread * noise
        out[name] = __import__('jax').numpy.asarray(drawn.astype(out[name].dtype))
    for name, factor in factors.items():
        out[name] = (out[name] * factor).astype(out[name].dtype)
    return out
```

```python
from contextlib import ExitStack

import numpy as np
import concourse.bass as bass
from concourse import mybir

F32 = mybir.dt.float32
ACT = mybir.ActivationFunctionType
ALU = mybir.AluOpType
AX = mybir.AxisListType

P = 128
DEPTH = 2
D = 1024
KT = D // P
CTX = 256
LAT = 256
TOK = CTX + LAT
NT = TOK // P
EPS = 1e-6
GN_EPS = 64e-5
DECAY = 0.6065306597126334
HEADS = 8
HD = 64
NOPE, ROPE, VD = 64, 32, 64
QK = NOPE + ROPE
QL, KVL = 384, 256
MLA_SCALE = float((NOPE + ROPE) ** -0.5)
CW = 512
CH = 64
STEPS = TOK // CH
HG = 4
NE, NG, EPG, DE = 16, 4, 4, 512
RING = 4
SLOT = 1024
XL = KT + NE * KT

V_N1, V_N2, V_MODB, V_QN, V_KVN, V_AVG, V_MU, V_KK, V_FG = 0, 8, 16, 64, 67, 69, 73, 88, 92
NVEC = 100
ZR, ZK, ZV, ZKK, ZW, ZA, ZG = 0, 4, 8, 12, 16, 17, 18
(C_ID, C_ONE, C_BONE, C_MS, C_MI, C_NDT, C_NOT, C_ND, C_NO, C_S00, C_S01, C_S10, C_S11) = range(13)
NCONST = 13


def constants():
    c = np.zeros((NCONST, P, P), np.float32)
    row = np.arange(P)
    d, t = row // CH, row % CH
    same = d[:, None] == d[None, :]
    fwd = d[:, None] == 0
    before = np.where(fwd, t[:, None] < t[None, :], t[:, None] > t[None, :]) & same
    equal = np.eye(P, dtype=bool)
    block = (t[:, None] // 16) == (t[None, :] // 16)
    c[C_ID] = equal
    c[C_ONE] = 1.0
    c[C_BONE] = same
    c[C_MS] = before
    c[C_MI] = before | equal
    c[C_NDT] = -(before & block).astype(np.float32)
    c[C_NOT] = -(before & ~block).astype(np.float32)
    c[C_ND] = c[C_NDT].T
    c[C_NO] = c[C_NOT].T
    for dd in range(2):
        for half in range(2):
            for i in range(CH):
                c[C_S00 + 2 * dd + half, dd * CH + i, half * CH + i] = 1.0
    return np.ascontiguousarray(c.transpose(1, 0, 2))


def small_constants():
    s = np.zeros((P, 2 + P + 16 + 4), np.float32)
    s[:CH, 0] = 1.0
    s[CH:, 1] = 1.0
    s[0, 2:2 + CH] = 1.0
    s[1, 2 + CH:2 + P] = 1.0
    s[:16, 2 + P:2 + P + 16] = np.eye(16)
    s[:, 2 + P + 16:] = [4.0, 3.0, 2.0, 1.0]
    return s


def rope_tables():
    nf = ROPE // 4
    tok = np.arange(LAT)
    pos = np.stack([tok // 64, tok % 64], 0).astype(np.float32)
    inv = np.power(np.float32(10000.0), -np.arange(nf, dtype=np.float32) / nf)
    out = np.zeros((P, 2, LAT), np.float32)
    for ax in range(2):
        ang = pos[ax][None, :] * inv[:, None]
        for half in range(2):
            r = ax * 2 * nf + half * nf
            out[64 + r:64 + r + nf, 0] = np.cos(ang)
            out[96 + r:96 + r + nf, 1] = np.sin(ang) * (-1.0 if half == 0 else 1.0)
    return out


SHARED = {
    "products_of_inverse": "p_nt2 p_n2 p_nt3 p_n4 p_nt4 p_x4 p_n8 p_x8 p_h p_ht p_x p_ht2 p_ht3 p_tt",
    "products_of_chain": "p_r p_u p_s p_o turned gram tokens_turned logits cums",
    "products_of_attention": "q_made k_made v_made scores prob_turned attended zb_summed",
    "products_of_rest": "norm_summed kk_summed read yc_turned mixed routed comb_turned",
    "inverse_kept_by_act": "n2_kept n4_kept h_kept x_kept ht2_kept tt_kept turned_kept",
    "chain_kept_by_act": "r_kept u_kept o_kept v_kept exps tanhed lora_half lora_in",
    "attention_by_act": "zb_kept zb_squared zb_rooted q_kept k_kept v_stored prob pt_kept yb_kept",
    "inputs_by_act": "squared norm_rooted h_done h_part raw_copied kk_rooted cond_ready zg_done",
    "readout_by_act": "var_rooted yc_kept",
    "gmlp_by_act": "u_gelu v_gelu v_sq v_rooted scored gated",
    "inverse_by_dve": "nt2_kept x1_done x1b_done x2_done nt4_kept x4_done n8_kept xt_done ht_kept w1_done w2_done w_done masked "
                      "turned_kept_v",
    "chain_by_dve": "sig_done kka kd_half kd_done bonus_a bonus_b bonus_kept operand state_sum state_new",
    "attention_by_dve": "zb_inv zb_scaled rope_sin rope_cos kr_ctx q_mid kr_made kr_spread q_roped max_raw max_done sum_inv prob_scaled",
    "inputs_by_dve": "norm_rs x_scaled mod_sum mod_step mod_ready raw_clear lora_clear state_clear z_sides z_half z_mixed kk_raw "
                     "kk_squared kk_clamped kk_inv kk_done blocks_clear eps_half eps_set out_ready",
    "readout_by_dve": "ro var_done yc_done v_inv v_normed mix_biased ya_done merged route comb_done",
    "step_by_pool": "staged operand_in",
}
SEMAPHORE = {n: g for g, names in SHARED.items() for n in names.split()}


class Signals:

    def __init__(self, ctx, nc, known):
        self.ctx, self.nc, self.known = ctx, nc, known
        self.sems, self.count, self.at = {}, {}, {}

    def sem(self, name):
        name = SEMAPHORE.get(name, name)
        if name not in self.sems:
            self.sems[name] = self.ctx.enter_context(self.nc.semaphore(name))
            self.count[name] = 0
        return self.sems[name]

    def out(self, name, *key, by=1):
        s = self.sem(name)
        shared = SEMAPHORE.get(name, name)
        self.count[shared] += by
        self.at[(name, *key)] = self.count[shared]
        return s, by

    def skip(self, name, n):
        self.sem(name)
        self.count[name] += n

    def got(self, name, *key):
        value = self.known[(name, *key)] if self.known is not None else 1
        return self.sem(name), value

    def base(self, name, *key):
        return self.known[(name, *key)] if self.known is not None else 1


def stream(l, w):
    for j in range(48):
        yield ("mod", l, j), w["mod"][l, j], SLOT
    for i in range(15):
        yield ("zc", l, i), w["zc"][l, i], SLOT
    for i in range(6):
        yield ("zb", l, i), w["zb"][l, i], SLOT
    for i in range(4):
        yield ("uq", l, i), w["uq"][l, i], 768
    yield ("uk", l, 0), w["uk"][l], SLOT
    yield ("uv", l, 0), w["uv"][l], SLOT
    for i in range(4):
        yield ("zu", l, i), w["zu"][l, i], SLOT
    for i in range(4):
        yield ("zv", l, i), w["zv"][l, i], SLOT
    for j in range(KT):
        for g in range(3):
            yield ("gate", l, j, g), w["gate"][l, g * KT + j], SLOT
        yield ("up", l, j, 0), w["up"][l, j, :, 0:1024], SLOT
        yield ("up", l, j, 1), w["up"][l, j, :, 1024:1536], 512
    for j in range(KT):
        yield ("wo", l, j), w["wo"][l, j], SLOT


def build(nc, w, out, known):
    with ExitStack() as ctx:
        def sb(name, shape):
            return ctx.enter_context(nc.sbuf_tensor(name, shape, F32))

        sg = Signals(ctx, nc, known)
        OUT, GOT = sg.out, sg.got

        x = sb("x", [P, KT, TOK])
        h = sb("h", [P, KT, TOK])
        y = sb("y", [P, 12, TOK])
        ring = sb("ring", [P, RING, SLOT])
        con = sb("con", [P, NCONST, P])
        small = sb("small", [P, 150])
        vec = sb("vec", [P, NVEC])
        rep = sb("rep", [P, 4, CW])
        lora = sb("lora", [P, 3, CW])
        misc = sb("misc", [P, 2, CW])
        bias2 = misc[0:2, :, :]
        cs = misc[:, 0, :].rearrange("p (a t) -> p a t", a=2)
        bs = sb("bs", [P, 4, P])
        ws = sb("ws", [P, 4, P])
        rw = sb("rw", [P, KT, NE])
        rb = sb("rb", [P, NE])
        cc = sb("cc", [P, KT, 2])
        ca = sb("ca", [P, KT, 2])
        mod = sb("mod", [P, 48, 2])
        gain = sb("gain", [P, 2, KT, 2])
        mu2 = sb("mu2", [P, 2, 15])
        eps = sb("eps", [P, 2])
        st = sb("st", [P, 64])
        rt = sb("rt", [P, 512])
        arena = sb("arena", [P, 24640])
        cmb = sb("cmb", [NE, TOK])
        ps = ctx.enter_context(nc.psum_tensor("ps", [P, 8, 512], F32))

        def C(i):
            return con[:, i, :]

        def view(at, *dims):
            n = int(np.prod(dims))
            a = arena[:, at:at + n]
            if len(dims) == 2:
                return a.rearrange("p (a b) -> p a b", b=dims[1])
            if len(dims) == 3:
                return a.rearrange("p (a b c) -> p a b c", b=dims[1], c=dims[2])
            return a

        sq = view(0, 8, 512)
        zc = view(0, 19, 512)
        osb = view(9728, STEPS, 520)
        state = view(13888, HEADS, HD)
        MB = 14400

        def mat(i):
            return view(MB + 512 * i, HG, P)
        m_b, m_g, m_a, m_r = (mat(i) for i in range(4))
        ar_t = view(MB + 2048, HG, 2 * P)
        b_t, g_t = mat(6), mat(7)
        n_t, n_, go_ = mat(8), mat(9), mat(11)
        bt_, qb_, qg_ = mat(12), mat(13), mat(14)
        n4_, nt4_, n8_, x_t, x_ = (mat(i) for i in range(15, 20))
        tok = y[:, 0:8, :]
        stage = y[:, 8:12, :].rearrange("p a (b c) -> p (a b) c", c=P)
        raw = view(MB, 2, 2, 258)
        shs = view(MB + 1100, 2, 2, 256)
        kks = view(MB + 2200, 2, 512)
        zq = view(0, 5, 512)
        qt = view(2560, HEADS, 512)
        kt_ = view(6656, HEADS, 512)
        vt = view(10752, 4, 512)
        pr = view(12800, 2, 2, 512)
        prt = view(14848, 2, 1024)
        rtmp = view(16896, 2, 2, 256)
        rsq = view(17920, 2, 512)
        ut = view(0, 4, 512)
        vg = view(2048, 4, 512)
        at = view(4096, 4, 512)
        vsq = view(6144, 512)
        mg = view(0, KT, 512)
        sgm = view(4096, 2, 3, 512)
        mt = view(7168, 512)
        w13 = view(0, 2, KT, 1024)
        w2 = view(16384, 2, 4, 1024)
        he = y[:, 0:8, :].rearrange("p (u f) t -> p u f t", u=2)
        sil = y[:, 8:10, :]
        cb = y[:, 10:12, :]
        cmask = rt

        loads = [q for l in range(DEPTH) for q in stream(l, w)]
        slot_of = {key: i % RING for i, (key, _, _) in enumerate(loads)}

        def t0_of(l):
            return CTX if l == DEPTH - 1 else 0

        def chunk_start(c, d):
            n = CTX // CH
            return CH * (c if d == 0 else c // n * n + n - 1 - c % n)

        def keep0(l, c):
            return l < DEPTH - 1 or c >= STEPS // 2

        def lbd(q):
            return rt[:, q * P:(q + 1) * P]

        def attention_pairs(l):
            return [(s, hh) for s in (range(2) if l < DEPTH - 1 else range(1, 2)) for hh in range(HEADS)]

        score, sel, pick, first, second, comb = \
            (y[:, 4, 64 * i:64 * i + 64].rearrange("p (t e) -> p t e", e=NE) for i in range(6))

        block = ctx.enter_context(nc.Block())

        @block.sync
        def _(sp):
            sp.dma_start(x[:, :, :], w["x"]).then_inc(*OUT("x_in", by=16))
            for dst, name in ((con[:, :, :], "con"), (small[:, :], "small"), (cs[64:P, :, :], "cs"), (rw[:, :, :], "rw"),
                              (rb[:, :], "rb"), (cc[:, :, :], "cc")):
                sp.dma_start(dst, w[name]).then_inc(*OUT("const_in", by=16))
            n = 0
            for l in range(DEPTH):
                if l:
                    sp.wait_ge(*GOT("h_done", l - 1, 1))
                for dst, name in ((vec[:, :], "vec"), (rep[:, :, :], "rep"), (lora[:, :, :], "lora"),
                                  (bias2[:, :, :], "bias2"), (bs[:, :, :], "bs"), (ws[:, :, :], "ws")):
                    sp.dma_start(dst, w[name][l]).then_inc(*OUT("param_in", l, by=16))
                while n < len(loads) and loads[n][0][1] == l:
                    key, src, size = loads[n]
                    if n >= RING:
                        sp.wait_ge(*GOT("chunk_used", *loads[n - RING][0]))
                    sp.dma_start(ring[:, n % RING, 0:size], src).then_inc(*OUT(f"slot{n % RING}", *key, by=16))
                    n += 1
                sp.wait_ge(*GOT("x_added", l, KT - 1))
                sp.wait_ge(*GOT("norm_summed", l, 1))
                for u in range(2):
                    sp.dma_start(w13[:, u, :, :], w["w13"][l, u]).then_inc(*OUT(f"w13_in{u}", l, by=16))
                    sp.dma_start(w2[:, u, :, :], w["w2"][l, u]).then_inc(*OUT(f"w2_in{u}", l, by=16))
                later13 = w["w13"][l].rearrange("(i u) p k n -> i u p k n", u=2)[1:]
                later2 = w["w2"][l].rearrange("(i u) p k n -> i u p k n", u=2)[1:]
                with sp.Fori(0, NE // 2 - 1, 1) as i:
                    for u in range(2):
                        sp.wait_ge(sg.sem("y_done"), i * 16 + (l * NE * 8 + 8 * u + 8))
                        sp.dma_start(w13[:, u, :, :], later13[i, u]).then_inc(sg.sem(f"w13_in{u}"), 16)
                        sp.dma_start(w2[:, u, :, :], later2[i, u]).then_inc(sg.sem(f"w2_in{u}"), 16)
                for u in range(2):
                    sg.skip(f"w13_in{u}", 16 * (NE // 2 - 1))
                    sg.skip(f"w2_in{u}", 16 * (NE // 2 - 1))
            sp.wait_ge(*GOT("out_ready",))
            sp.dma_start(out, h[:, :, 0:LAT]).then_inc(*OUT("out_stored", by=16))
            sp.wait_ge(*GOT("out_stored"))

        @block.tensor
        def _(pe):
            def weights(*key):
                pe.wait_ge(*GOT(f"slot{slot_of[key]}", *key))
                return ring[:, slot_of[key], :]

            def norm(l, which):
                t0 = 0 if l < DEPTH and which == 0 else CTX if l == DEPTH else t0_of(l)
                if which == 1:
                    pe.wait_ge(*GOT("x_added", l, KT - 1))
                for k in range(KT):
                    pe.wait_ge(*GOT("squared", l, which, k))
                    mm = pe.matmul(ps[:, 7, t0:], C(C_ONE), sq[:, k, t0:], start=(k == 0), stop=(k == KT - 1))
                mm.then_inc(*OUT("norm_summed", l, which))

            def full(dst, wt, rhs, n, t0):
                for k in range(n):
                    mm = pe.matmul(dst, wt[:, k * P:(k + 1) * P], rhs[:, k, t0:TOK], start=(k == 0), stop=(k == n - 1))
                return mm

            def modulation(l):
                pe.wait_ge(*GOT("cond_ready"))
                pe.wait_ge(*GOT("const_in"))
                pe.wait_ge(*GOT("param_in", l))
                for j in range(48):
                    wt = weights("mod", l, j)
                    for k in range(KT):
                        mm = pe.matmul(ps[:, 0, 2 * j:2 * j + 2], wt[:, k * P:(k + 1) * P], ca[:, k, :],
                                       start=(k == 0), stop=(k == KT - 1))
                    mm.then_inc(*OUT("chunk_used", "mod", l, j))

            def rwkv_inputs(l):
                pe.wait_ge(*GOT("h_done", l, 0))
                pe.wait_ge(*GOT("mod_ready", l))
                for i in range(15):
                    wt = weights("zc", l, i)
                    if i >= 2:
                        pe.wait_ge(*GOT("raw_copied", l, i - 2))
                    full(ps[:, i % 2, :], wt, h, KT, 0).then_inc(*OUT("chunk_used", "zc", l, i))
                for f in range(4):
                    pe.wait_ge(*GOT("kk_squared", l, f))
                    if f >= 2:
                        pe.wait_ge(*GOT("kk_rooted", l, f - 2))
                    pe.matmul(ps[:, 2 + f % 2, :], C(C_BONE), kks[:, f % 2, :], start=True, stop=True) \
                        .then_inc(*OUT("kk_summed", l, f))

            def rwkv_step(l, c):
                keep = l < DEPTH - 1 or c >= STEPS // 2
                pe.wait_ge(*GOT("staged", l, c, 1))
                if c:
                    pe.wait_ge(*GOT("o_kept" if keep0(l, c - 1) else "state_new", l, c - 1, 1))
                    pe.wait_ge(*GOT("state_new", l, c - 1, 1))
                else:
                    pe.wait_ge(*GOT("kk_done", l, 3))
                for q in range(4):
                    for f in range(4):
                        mm = pe.transpose(ps[:, q, f * P:(f + 1) * P], stage[:, 4 * q + f, :], C(C_ID))
                mm.then_inc(*OUT("tokens_turned", l, c))
                for q in range(2):
                    pe.wait_ge(*GOT("lora_in", l, c, q))
                    pe.matmul(ps[:, 4 + q, :], lbd(q), lora[:, q, :], start=True, stop=False)
                    pe.matmul(ps[:, 4 + q, :], small[0:2, 2:2 + P], bias2[:, q, :], start=False, stop=True) \
                        .then_inc(*OUT("logits", l, c, q))
                pe.wait_ge(*GOT("sig_done", l, c, 0))
                pe.matmul(ps[:, 6, :], C(C_MI), tok[:, 0, :], start=True, stop=True)
                pe.matmul(ps[:, 7, :], C(C_MS), tok[:, 0, :], start=True, stop=True)
                for hh in range(HEADS):
                    for d in range(2):
                        mm = pe.matmul(ps[d * HD:(d + 1) * HD, 4, hh:hh + 1], tok[:, 0, hh * HD:(hh + 1) * HD],
                                       small[:, d:d + 1], start=True, stop=True)
                mm.then_inc(*OUT("cums", l, c))
                for g in range(2):
                    rwkv_matrices(l, c, g)
                    rwkv_chain(l, c, g, keep)

            def rwkv_matrices(l, c, g):
                k = (l, c, g)

                def each(bank, lhs, rhs, name):
                    for i in range(HG):
                        mm = pe.matmul(ps[:, bank, i * P:(i + 1) * P], lhs[:, i, :], rhs[:, i, :], start=True, stop=True)
                    mm.then_inc(*OUT(name, *k))

                pe.wait_ge(*GOT("operand_in", *k, 3, 1))
                if g == 0:
                    pe.wait_ge(*GOT("kd_done", l, c))
                    pe.wait_ge(*GOT("exps", l, c, 3))
                    pe.wait_ge(*GOT("v_kept", l, c))
                    pe.wait_ge(*GOT("bonus_kept", l, c))
                else:
                    pe.wait_ge(*GOT("state_new", l, c, 0))
                    if keep0(l, c):
                        pe.wait_ge(*GOT("o_kept", l, c, 0))
                for q, src in enumerate((m_a, m_r, m_b, m_g)):
                    for i in range(HG):
                        mm = pe.transpose(ps[:, q, i * P:(i + 1) * P], src[:, i, :], C(C_ID))
                mm.then_inc(*OUT("turned", *k))
                pe.wait_ge(*GOT("turned_kept", *k, 1))
                pe.wait_ge(*GOT("turned_kept_v", *k, 3))
                if g == 1:
                    pe.wait_ge(*GOT("tt_kept", l, c, 0))
                for q, src in enumerate((b_t, g_t)):
                    for i in range(HG):
                        mm = pe.matmul(ps[:, 4 + 2 * q + i // 2, i % 2 * 256:i % 2 * 256 + 256], src[:, i, :],
                                       ar_t[:, i, :], start=True, stop=True)
                for i in range(HG):
                    mm = pe.matmul(ps[:, 0, i * P:(i + 1) * P], ar_t[:, i, 0:P], b_t[:, i, :], start=True, stop=True)
                mm.then_inc(*OUT("gram", *k))
                pe.wait_ge(*GOT("masked", *k, 1))
                each(1, n_, n_t, "p_nt2")
                each(2, n_t, n_, "p_n2")
                pe.wait_ge(*GOT("nt2_kept", *k))
                pe.wait_ge(*GOT("n2_kept", *k))
                each(3, g_t, n_t, "p_nt3")
                pe.wait_ge(*GOT("masked", *k, 5))
                each(4, b_t, g_t, "p_n4")
                each(5, g_t, b_t, "p_nt4")
                pe.wait_ge(*GOT("n4_kept", *k))
                pe.wait_ge(*GOT("x2_done", *k))
                each(6, n4_, m_a, "p_x4")
                pe.wait_ge(*GOT("nt4_kept", *k))
                each(7, nt4_, n4_, "p_n8")
                pe.wait_ge(*GOT("n8_kept", *k))
                pe.wait_ge(*GOT("x4_done", *k))
                each(1, n8_, m_r, "p_x8")
                pe.wait_ge(*GOT("xt_done", *k))
                each(2, x_t, go_, "p_h")
                each(3, go_, x_t, "p_ht")
                for i in range(HG):
                    mm = pe.transpose(ps[:, 4, i * P:(i + 1) * P], x_t[:, i, :], C(C_ID))
                mm.then_inc(*OUT("p_x", *k))
                pe.wait_ge(*GOT("h_kept", *k))
                pe.wait_ge(*GOT("ht_kept", *k))
                each(5, n_, n_t, "p_ht2")
                pe.wait_ge(*GOT("ht2_kept", *k))
                each(6, n_, n4_, "p_ht3")
                pe.wait_ge(*GOT("w_done", *k))
                pe.wait_ge(*GOT("x_kept", *k))
                each(7, x_, nt4_, "p_tt")

            def rwkv_chain(l, c, g, keep):
                k = (l, c, g)
                v = tok[:, 5, :].rearrange("p (h v) -> p h v", v=HD)
                h0 = g * HG
                if c == 0 and g == 0:
                    pe.wait_ge(*GOT("state_clear", l))
                for i in range(HG):
                    o = ps[:, 0, i * HD:(i + 1) * HD]
                    pe.matmul(o, ar_t[:, i, 0:P], state[:, h0 + i, :], start=True, stop=False)
                    mm = pe.matmul(o, bt_[:, i, :], v[:, h0 + i, :], start=False, stop=True)
                mm.then_inc(*OUT("p_r", *k))
                pe.wait_ge(*GOT("r_kept", *k))
                pe.wait_ge(*GOT("tt_kept", *k))
                pe.wait_ge(*GOT("xt_done", *k))
                for i in range(HG):
                    mm = pe.matmul(ps[:, 1, i * HD:(i + 1) * HD], n8_[:, i, :], n_t[:, i, 0:HD], start=True, stop=True)
                mm.then_inc(*OUT("p_u", *k))
                pe.wait_ge(*GOT("u_kept", *k))
                for i in range(HG):
                    o = ps[:, 3, i * HD:(i + 1) * HD]
                    pe.matmul(o, m_b[:, i, :], n_t[:, i, HD:P], start=True, stop=False)
                    mm = pe.matmul(o, m_g[:, i, :], v[:, h0 + i, :], start=False, stop=True)
                mm.then_inc(*OUT("p_s", *k))
                if keep:
                    for i in range(HG):
                        o = ps[:, 2, i * HD:(i + 1) * HD]
                        pe.matmul(o, ar_t[:, i, P:2 * P], state[:, h0 + i, :], start=True, stop=False)
                        pe.matmul(o, qb_[:, i, :], n_t[:, i, HD:P], start=False, stop=False)
                        mm = pe.matmul(o, qg_[:, i, :], v[:, h0 + i, :], start=False, stop=True)
                    mm.then_inc(*OUT("p_o", *k))

            def rwkv_readout(l):
                pe.wait_ge(*GOT("zg_done", l))
                for i in range(t0_of(l) // P, NT):
                    n = CTX // CH
                    if i > t0_of(l) // P:
                        pe.wait_ge(*GOT("yc_kept", l, i - 1))
                    else:
                        pe.wait_ge(*GOT("o_kept", l, STEPS - 1, 1))
                        pe.wait_ge(*GOT("state_new", l, STEPS - 1, 1))
                    parts = []
                    for half in range(2):
                        j = 2 * i + half
                        parts.append((0, half, j))
                        parts.append((1, half, j // n * n + n - 1 - j % n))
                    for bank, a, b in ((0, 0, CW), (1, CW, CW + HEADS)):
                        for q, (d, half, c) in enumerate(parts):
                            pe.matmul(ps[:, bank, 0:b - a], C(C_S00 + 2 * d + half), osb[:, c, a:b],
                                      start=(q == 0), stop=(q == 3))
                    for f in range(4):
                        pe.transpose(ps[:, 2, f * P:(f + 1) * P], zc[:, ZV + f, i * P:(i + 1) * P], C(C_ID))
                    pe.matmul(ps[:, 3, :], zc[:, ZG, i * P:(i + 1) * P], lora[:, 2, :], start=True, stop=True) \
                        .then_inc(*OUT("read", l, i))
                    pe.wait_ge(*GOT("yc_done", l, i))
                    for f in range(4):
                        mm = pe.transpose(ps[:, 4, f * P:(f + 1) * P], tok[:, 0, f * P:(f + 1) * P], C(C_ID))
                    mm.then_inc(*OUT("yc_turned", l, i))

            def attention_inputs(l):
                t0 = t0_of(l)
                for i in range(6):
                    wt = weights("zb", l, i)
                    if i >= 2:
                        pe.wait_ge(*GOT("zb_kept", l, i - 2))
                    elif i == 0:
                        pe.wait_ge(*GOT("yc_kept", l, NT - 1))
                    full(ps[:, i % 2, :], wt, h, KT, 0).then_inc(*OUT("chunk_used", "zb", l, i))
                for i in range(5):
                    pe.wait_ge(*GOT("zb_squared", l, i))
                    mm = pe.matmul(ps[:, 2 if i < 3 else 3, :], C(C_ONE), rsq[:, i % 2, :],
                                   start=(i in (0, 3)), stop=(i in (2, 4)))
                    mm.then_inc(*OUT("zb_summed", l, i))
                for i in range(5):
                    pe.wait_ge(*GOT("zb_scaled", l, i))
                n = 0
                for i in range(4):
                    wt = weights("uq", l, i)
                    for j in range(2):
                        hh = 2 * i + j
                        bank = 4 + hh % 2
                        if hh >= 2:
                            pe.wait_ge(*GOT("q_kept", l, hh - 2))
                            pe.wait_ge(*GOT("q_roped", l, hh - 2))
                        for k in range(3):
                            mm = pe.matmul(ps[:, bank, t0:TOK], wt[:, (j * 3 + k) * P:(j * 3 + k + 1) * P], zq[:, k, t0:TOK],
                                           start=(k == 0), stop=(k == 2))
                        mm.then_inc(*(OUT("q_made", l, hh) if j == 0 else OUT("chunk_used", "uq", l, i)))
                wt = weights("uk", l, 0)
                for hh in range(HEADS):
                    if hh >= 2:
                        pe.wait_ge(*GOT("k_kept", l, hh - 2))
                    else:
                        pe.wait_ge(*GOT("q_kept", l, 6 + hh))
                        pe.wait_ge(*GOT("kr_spread", l))
                    for k in range(2):
                        mm = pe.matmul(ps[0:HD, 6 + hh % 2, :], wt[:, (hh * 2 + k) * HD:(hh * 2 + k + 1) * HD], zq[:, 3 + k, :],
                                       start=(k == 0), stop=(k == 1))
                    mm.then_inc(*(OUT("k_made", l, hh) if hh < HEADS - 1 else OUT("chunk_used", "uk", l, 0)))
                wt = weights("uv", l, 0)
                pe.wait_ge(*GOT("kr_spread", l))
                pe.wait_ge(*GOT("zb_rooted", l, 1))
                for i in range(NT):
                    for k in range(2):
                        mm = pe.matmul(ps[:, i, :], zq[:, 3 + k, i * P:(i + 1) * P], wt[:, k * 512:(k + 1) * 512],
                                       start=(k == 0), stop=(k == 1))
                    mm.then_inc(*(OUT("v_made", l, i) if i < NT - 1 else OUT("chunk_used", "uv", l, 0)))

            def attention(l):
                pairs = attention_pairs(l)

                def scores(n):
                    s, hh = pairs[n]
                    nk = 4 if s else 2
                    if n >= 2:
                        pe.wait_ge(*GOT("prob", l, n - 2, 1))
                    elif n == 0:
                        pe.wait_ge(*GOT("v_stored", l, NT - 1))
                        pe.wait_ge(*GOT("k_kept", l, HEADS - 1))
                        pe.wait_ge(*GOT("q_kept", l, HEADS - 1))
                        pe.wait_ge(*GOT("q_roped", l, HEADS - 1))
                    for q in range(2):
                        tt = s * CTX + q * P
                        mm = pe.matmul(ps[:, n % 2 * 2 + q, 0:nk * P], qt[0:QK, hh, tt:tt + P], kt_[0:QK, hh, 0:nk * P],
                                       start=True, stop=True)
                    mm.then_inc(*OUT("scores", l, n))

                scores(0)
                for n, (s, hh) in enumerate(pairs):
                    nk = 4 if s else 2
                    if n + 1 < len(pairs):
                        scores(n + 1)
                    pe.wait_ge(*GOT("prob_scaled", l, n, 1))
                    if n >= 1:
                        pe.wait_ge(*GOT("pt_kept", l, n - 1))
                    for kk in range(nk):
                        for q in range(2):
                            mm = pe.transpose(ps[:, 4 + kk // 2, kk % 2 * 256 + q * P:kk % 2 * 256 + (q + 1) * P],
                                              pr[:, n % 2, q, kk * P:(kk + 1) * P], C(C_ID))
                    mm.then_inc(*OUT("prob_turned", l, n))
                    pe.wait_ge(*GOT("pt_kept", l, n))
                    if n >= 2:
                        pe.wait_ge(*GOT("yb_kept", l, n - 2))
                    for kk in range(nk):
                        mm = pe.matmul(ps[hh % 2 * HD:hh % 2 * HD + HD, 6 + n % 2, 0:256], vt[:, kk, hh * VD:(hh + 1) * VD],
                                       prt[:, n % 2, kk * 256:(kk + 1) * 256], start=(kk == 0), stop=(kk == nk - 1))
                    mm.then_inc(*OUT("attended", l, n))

            def gmlp(l):
                t0 = t0_of(l)
                pe.wait_ge(*GOT("yb_kept", l, len(attention_pairs(l)) - 1))
                pe.wait_ge(*GOT("yb_kept", l, len(attention_pairs(l)) - 2))
                for i in range(4):
                    wt = weights("zu", l, i)
                    if i >= 2:
                        pe.wait_ge(*GOT("u_gelu", l, i - 2))
                    full(ps[:, 4 + i % 2, t0:TOK], wt, h, KT, t0).then_inc(*OUT("chunk_used", "zu", l, i))
                for i in range(4):
                    wt = weights("zv", l, i)
                    for k in range(2):
                        for t in range(t0 // P, NT):
                            mm = pe.matmul(ps[:, t, :], h[:, 2 * i + k, t * P:(t + 1) * P], wt[:, k * 512:(k + 1) * 512],
                                           start=(i == 0 and k == 0), stop=(i == 3 and k == 1))
                    mm.then_inc(*OUT("chunk_used", "zv", l, i))
                pe.wait_ge(*GOT("v_normed", l, NT - 1))
                pe.wait_ge(*GOT("u_gelu", l, 3))
                for g in range(4):
                    for t in range(t0 // P, NT):
                        mm = pe.matmul(ps[:, 4 + g, t * P:(t + 1) * P], vg[:, t, g * P:(g + 1) * P], ws[:, g, :],
                                       start=True, stop=True)
                    mm.then_inc(*OUT("mixed", l, g))

            def merge(l):
                t0 = t0_of(l)
                pe.wait_ge(*GOT("ya_done", l, 3))
                pe.wait_ge(*GOT("v_normed", l, NT - 1))
                for j in range(KT):
                    for g in range(3):
                        wt = weights("gate", l, j, g)
                        if j:
                            pe.wait_ge(*GOT("gated", l, j - 1, g))
                        full(ps[:, g, t0:TOK], wt, h, KT, t0).then_inc(*OUT("chunk_used", "gate", l, j, g))
                    for g in range(3):
                        if g != 1:
                            wt = weights("up", l, j, g // 2)
                        at_ = 512 * g if g < 2 else 0
                        if j:
                            pe.wait_ge(*GOT("merged", l, j - 1, 4))
                        for k in range(4):
                            mm = pe.matmul(ps[:, 3 + g, t0:TOK], wt[:, at_ + k * P:at_ + (k + 1) * P], y[:, 4 * g + k, t0:TOK],
                                           start=(k == 0), stop=(k == 3))
                        if g:
                            mm.then_inc(*OUT("chunk_used", "up", l, j, g // 2))
                pe.wait_ge(*GOT("merged", l, KT - 1, 4))
                for j in range(KT):
                    wt = weights("wo", l, j)
                    if j >= 2:
                        pe.wait_ge(*GOT("x_added", l, j - 2))
                    full(ps[:, 6 + j % 2, t0:TOK], wt, mg, KT, t0).then_inc(*OUT("chunk_used", "wo", l, j))

            def router(l):
                t0 = t0_of(l)
                pe.wait_ge(*GOT("h_done", l, 1))
                for t in range(t0 // P, NT):
                    for k in range(KT):
                        mm = pe.matmul(ps[:, 6, t * NE:(t + 1) * NE], h[:, k, t * P:(t + 1) * P], rw[:, k, :],
                                       start=(k == 0), stop=(k == KT - 1))
                mm.then_inc(*OUT("routed", l))
                pe.wait_ge(*GOT("comb_done", l))
                for t in range(t0 // P, NT):
                    mm = pe.transpose(ps[0:NE, 7, t * P:(t + 1) * P], comb[:, t, :], C(C_ID))
                mm.then_inc(*OUT("comb_turned", l))

            def experts(l):
                t0 = t0_of(l)
                nf = l * NE * 4
                nd = l * NE * 8
                ne = l * NE
                pe.wait_ge(*GOT("comb_spread", l, "first"))
                with pe.Fori(0, NE, 2) as e:
                    for u in range(2):
                        pe.wait_ge(sg.sem(f"w13_in{u}"), e * 8 + 16 * (l * (NE // 2) + 1))
                        for f in range(4):
                            if f == 1:
                                pe.wait_ge(sg.sem("comb_masked"), e + (ne + u + 1))
                                pe.wait_ge(sg.sem("comb_spread"), e + (ne + u + l + 1))
                                pe.matmul(ps[:, 7, t0:TOK], con[0:NE, C_ONE, :], cmask[0:NE, t0:TOK], start=True,
                                          stop=True).then_inc(sg.sem("comb_rowed"), 1)
                            pe.wait_ge(sg.sem("he_gated"), e * 4 + (nf + 4 * (l + 1) + 4 * u + f - 1))
                            for q in range(2):
                                for k in range(KT):
                                    mm = pe.matmul(ps[:, 2 * q + f % 2, t0:TOK],
                                                   w13[:, u, k, q * 512 + f * P:q * 512 + (f + 1) * P], h[:, k, t0:TOK],
                                                   start=(k == 0), stop=(k == KT - 1))
                            mm.then_inc(sg.sem("h13_done"), 1)
                        pe.wait_ge(sg.sem(f"w2_in{u}"), e * 8 + 16 * (l * (NE // 2) + 1))
                        pe.wait_ge(sg.sem("he_done"), e * 4 + (nf + 4 * u + 4))
                        for d in range(KT):
                            pe.wait_ge(sg.sem("x_added"), e * 8 + (XL * l + 8 * u + 7 + d))
                            for k in range(4):
                                mm = pe.matmul(ps[:, 4 + d % 2, t0:TOK], w2[:, u, k, d * P:(d + 1) * P], he[:, u, k, t0:TOK],
                                               start=(k == 0), stop=(k == 3))
                            mm.then_inc(sg.sem("y_done"), 1)

            for l in range(DEPTH):
                modulation(l)
                norm(l, 0)
                rwkv_inputs(l)
                for c in range(STEPS):
                    rwkv_step(l, c)
                rwkv_readout(l)
                attention_inputs(l)
                attention(l)
                gmlp(l)
                merge(l)
                norm(l, 1)
                router(l)
                experts(l)
            norm(DEPTH, 0)

        @block.scalar
        def _(act):
            def A(o, i, f, **kw):
                return act.activation(o, i, f, **kw)

            def norm(l, which):
                t0 = 0 if l < DEPTH and which == 0 else CTX if l == DEPTH else t0_of(l)
                for k in range(KT):
                    if which == 1:
                        act.wait_ge(*GOT("x_added", l, k))
                        if k == 0:
                            act.wait_ge(*GOT("chunk_used", "wo", l, KT - 1))
                    elif l:
                        act.wait_ge(sg.sem("x_added"), XL * l)
                    else:
                        act.wait_ge(*GOT("x_in"))
                    A(sq[:, k, t0:], x[:, k, t0:], ACT.Square).then_inc(*OUT("squared", l, which, k))
                act.wait_ge(*GOT("norm_summed", l, which))
                act.wait_ge(*GOT("eps_set"))
                A(rt[:, t0:], ps[:, 7, t0:], ACT.Sqrt, bias=eps[:, 0:1], scale=1.0 / D).then_inc(*OUT("norm_rooted", l, which))
                if l == DEPTH:
                    return
                for k in range(KT):
                    act.wait_ge(*GOT("x_scaled", l, which, k))
                    for s in range(t0 // CTX, 2):
                        v = h[:, k, s * CTX:(s + 1) * CTX]
                        ins = A(v, v, ACT.Identity, scale=gain[:, which, k, s:s + 1],
                                bias=mod[:, 24 * which + k, s:s + 1])
                        ins.then_inc(*(OUT("h_done", l, which) if k == KT - 1 and s == 1 else OUT("h_part", l, which, k, s)))

            def copy(o, i):
                return A(o, i, ACT.Copy)

            def rwkv_inputs(l):
                for i in range(15):
                    act.wait_ge(*GOT("chunk_used", "zc", l, i))
                    if i == 0:
                        act.wait_ge(*GOT("raw_clear", l))
                    if i >= 2:
                        act.wait_ge(*GOT("z_mixed", l, i - 2))
                    copy(raw[:, i % 2, :, 1:257], ps[:, i % 2, :].rearrange("p (s t) -> p s t", s=2)) \
                        .then_inc(*OUT("raw_copied", l, i))
                for f in range(4):
                    act.wait_ge(*GOT("kk_clamped", l, f))
                    A(kks[:, f % 2, :], kks[:, f % 2, :], ACT.Sqrt).then_inc(*OUT("kk_rooted", l, f))

            def rwkv_step(l, c):
                if c == 0:
                    act.wait_ge(*GOT("lora_clear", l))
                    act.wait_ge(*GOT("z_mixed", l, 13))
                else:
                    act.wait_ge(*GOT("logits", l, c - 1, 1))
                for q in range(2):
                    for d in range(2):
                        a = chunk_start(c, d)
                        r = slice(d * 64, d * 64 + 64)
                        ins = A(lbd(q)[r, d * 64:d * 64 + 64], zc[r, ZW + q, a:a + 64], ACT.Tanh if q == 0 else ACT.Copy)
                        ins.then_inc(*(OUT("lora_in", l, c, q) if d else OUT("lora_half", l, c, q)))
                if c:
                    act.wait_ge(*GOT("bonus_kept", l, c - 1))
                    act.wait_ge(*GOT("cums", l, c - 1))
                for q in range(2):
                    act.wait_ge(*GOT("logits", l, c, q))
                    A(tok[:, q, :], ps[:, 4 + q, :], ACT.Tanh, scale=0.5).then_inc(*OUT("tanhed", l, c, q))
                act.wait_ge(*GOT("cums", l, c))
                if c:
                    act.wait_ge(*GOT("operand_in", l, c - 1, 1, 3, 1))
                A(tok[:, 2, :], ps[:, 6, :], ACT.Exp, scale=-DECAY).then_inc(*OUT("exps", l, c, 0))
                A(tok[:, 3, :], ps[:, 7, :], ACT.Exp, scale=-DECAY).then_inc(*OUT("exps", l, c, 1))
                A(tok[:, 4, :], ps[:, 6, :], ACT.Exp, scale=DECAY).then_inc(*OUT("exps", l, c, 2))
                if c:
                    act.wait_ge(*GOT("state_new", l, c - 1, 1))
                A(st[:, 0:8], ps[:, 4, 0:8], ACT.Exp, scale=-DECAY).then_inc(*OUT("exps", l, c, 3))
                if c:
                    act.wait_ge(*GOT("p_s", l, c - 1, 1))
                    if keep0(l, c - 1):
                        act.wait_ge(*GOT("p_o", l, c - 1, 1))
                act.wait_ge(*GOT("tokens_turned", l, c))
                copy(tok[:, 5, :], ps[:, 2, :]).then_inc(*OUT("v_kept", l, c))
                for g in range(2):
                    rwkv_matrices(l, c, g)

            def rwkv_matrices(l, c, g):
                k = (l, c, g)

                def keep(name, src, bank, dst):
                    act.wait_ge(*GOT(src, *k))
                    copy(dst, ps[:, bank, :].rearrange("p (h t) -> p h t", t=P)).then_inc(*OUT(name, *k))
                if c or g:
                    pl, pc, pg = (l, c, 0) if g else (l, c - 1, 1)
                    act.wait_ge(*GOT("p_s", pl, pc, pg))
                    if keep0(pl, pc):
                        act.wait_ge(*GOT("p_o", pl, pc, pg))
                act.wait_ge(*GOT("turned", *k))
                copy(ar_t[:, :, 0:P], ps[:, 0, :].rearrange("p (h t) -> p h t", t=P)).then_inc(*OUT("turned_kept", *k, 0))
                copy(ar_t[:, :, P:2 * P], ps[:, 1, :].rearrange("p (h t) -> p h t", t=P)).then_inc(*OUT("turned_kept", *k, 1))
                keep("n2_kept", "p_n2", 2, g_t)
                keep("n4_kept", "p_n4", 4, n4_)
                keep("h_kept", "p_h", 2, n_)
                keep("x_kept", "p_x", 4, x_)
                keep("ht2_kept", "p_ht2", 5, n4_)
                keep("tt_kept", "p_tt", 7, n8_)
                act.wait_ge(*GOT("p_r", *k))
                A(n_t[:, :, 0:HD], ps[:, 0, 0:HG * HD].rearrange("p (h v) -> p h v", v=HD), ACT.Copy, scale=-1.0) \
                    .then_inc(*OUT("r_kept", *k))
                act.wait_ge(*GOT("p_u", *k))
                copy(n_t[:, :, HD:P], ps[:, 1, 0:HG * HD].rearrange("p (h v) -> p h v", v=HD)).then_inc(*OUT("u_kept", *k))
                if keep0(l, c):
                    act.wait_ge(*GOT("p_o", *k))
                    copy(osb[:, c, g * 256:(g + 1) * 256], ps[:, 2, 0:256]).then_inc(*OUT("o_kept", *k))

            def rwkv_readout(l):
                A(zc[:, ZG, :], zc[:, ZG, :], ACT.Sigmoid).then_inc(*OUT("zg_done", l))
                for i in range(t0_of(l) // P, NT):
                    act.wait_ge(*GOT("var_done", l, i))
                    A(st[:, 16:24], st[:, 16:24], ACT.Sqrt, bias=eps[:, 1:2], scale=1.0 / HD).then_inc(*OUT("var_rooted", l, i))
                    act.wait_ge(*GOT("yc_turned", l, i))
                    copy(y[:, 8:12, i * P:(i + 1) * P], ps[:, 4, :].rearrange("p (f t) -> p f t", t=P)) \
                        .then_inc(*OUT("yc_kept", l, i))

            def attention_inputs(l):
                t0 = t0_of(l)
                for i in range(5):
                    act.wait_ge(*GOT("chunk_used", "zb", l, i))
                    copy(zq[:, i, :], ps[:, i % 2, :]).then_inc(*OUT("zb_kept", l, i))
                for i in range(5):
                    act.wait_ge(*GOT("zb_kept", l, i))
                    if i >= 2:
                        act.wait_ge(*GOT("zb_summed", l, i - 2))
                    A(rsq[:, i % 2, :], zq[:, i, :], ACT.Square).then_inc(*OUT("zb_squared", l, i))
                for i, (bank, n) in enumerate(((2, QL), (3, KVL))):
                    act.wait_ge(*GOT("zb_summed", l, 2 if i == 0 else 4))
                    A(pr[:, 0, i, :], ps[:, bank, :], ACT.Sqrt, bias=eps[:, 0:1], scale=1.0 / n).then_inc(*OUT("zb_rooted", l, i))
                for hh in range(HEADS):
                    act.wait_ge(*(GOT("q_made", l, hh) if hh % 2 == 0 else GOT("chunk_used", "uq", l, hh // 2)))
                    copy(qt[0:64, hh, t0:], ps[0:64, 4 + hh % 2, t0:]).then_inc(*OUT("q_kept", l, hh))
                for hh in range(HEADS):
                    act.wait_ge(*(GOT("k_made", l, hh) if hh < HEADS - 1 else GOT("chunk_used", "uk", l, 0)))
                    copy(kt_[0:64, hh, :], ps[0:64, 6 + hh % 2, :]).then_inc(*OUT("k_kept", l, hh))
                for i in range(NT):
                    act.wait_ge(*(GOT("v_made", l, i) if i < NT - 1 else GOT("chunk_used", "uv", l, 0)))
                    copy(vt[:, i, :], ps[:, i, :]).then_inc(*OUT("v_stored", l, i))

            def attention(l):
                pairs = attention_pairs(l)

                def probabilities(n):
                    s, hh = pairs[n]
                    nk = 4 if s else 2
                    act.wait_ge(*GOT("max_done", l, n))
                    if n >= 2:
                        act.wait_ge(*GOT("prob_turned", l, n - 2))
                    else:
                        act.wait_ge(*GOT("zb_scaled", l, 4))
                    for q in range(2):
                        A(pr[:, n % 2, q, 0:nk * P], ps[:, n % 2 * 2 + q, 0:nk * P], ACT.Exp, scale=MLA_SCALE,
                          bias=st[:, 32 + n % 2 * 8 + q:33 + n % 2 * 8 + q],
                          accum_out=st[:, 34 + n % 2 * 8 + q:35 + n % 2 * 8 + q]).then_inc(*OUT("prob", l, n, q))

                def keep(n):
                    s, hh = pairs[n]
                    nk = 4 if s else 2
                    act.wait_ge(*GOT("prob_turned", l, n))
                    if n >= 2:
                        act.wait_ge(*GOT("attended", l, n - 2))
                    copy(prt[:, n % 2, 0:nk * 256].rearrange("p (b k) -> p b k", k=512),
                         ps[:, 4:4 + nk // 2, :]).then_inc(*OUT("pt_kept", l, n))
                    act.wait_ge(*GOT("attended", l, n))
                    r = slice(hh % 2 * HD, hh % 2 * HD + HD)
                    copy(y[r, 4 + hh // 2, s * CTX:(s + 1) * CTX], ps[r, 6 + n % 2, 0:256]).then_inc(*OUT("yb_kept", l, n))

                probabilities(0)
                for n in range(len(pairs)):
                    if n + 1 < len(pairs):
                        probabilities(n + 1)
                    keep(n)

            def gmlp(l):
                t0 = t0_of(l)
                for i in range(4):
                    act.wait_ge(*GOT("chunk_used", "zu", l, i))
                    A(ut[:, i, t0:], ps[:, 4 + i % 2, t0:], ACT.Gelu_apprx_tanh).then_inc(*OUT("u_gelu", l, i))
                act.wait_ge(*GOT("chunk_used", "zv", l, 3))
                for t in range(t0 // P, NT):
                    A(vg[:, t, :], ps[:, t, :], ACT.Gelu_apprx_tanh).then_inc(*OUT("v_gelu", l, t))
                for t in range(t0 // P, NT):
                    act.wait_ge(*GOT("v_gelu", l, t))
                    if t > t0 // P:
                        act.wait_ge(*GOT("v_sq", l, t - 1))
                    A(vsq, vg[:, t, :], ACT.Square, accum_out=st[:, 48 + t:49 + t]).then_inc(*OUT("v_sq", l, t))
                act.wait_ge(*GOT("v_sq", l, NT - 1))
                A(st[:, 52 + t0 // P:56], st[:, 48 + t0 // P:52], ACT.Sqrt, bias=eps[:, 0:1], scale=1.0 / CW) \
                    .then_inc(*OUT("v_rooted", l))

            def merge(l):
                t0 = t0_of(l)
                for j in range(KT):
                    for g in range(3):
                        act.wait_ge(*GOT("chunk_used", "gate", l, j, g))
                        if j >= 2:
                            act.wait_ge(*GOT("merged", l, j - 2, 4))
                        elif j == 0 and g == 0:
                            act.wait_ge(*GOT("ya_done", l, 3))
                        A(sgm[:, j % 2, g, t0:], ps[:, g, t0:], ACT.Sigmoid).then_inc(*OUT("gated", l, j, g))

            def experts(l):
                t0 = t0_of(l)
                act.wait_ge(*GOT("routed", l))
                A(score[:, t0 // P:, :], ps[:, 6, t0 // P * NE:NT * NE].rearrange("p (t e) -> p t e", e=NE), ACT.Sigmoid) \
                    .then_inc(*OUT("scored", l))
                act.wait_ge(*GOT("comb_turned", l))
                copy(cmb[0:NE, t0:], ps[0:NE, 7, t0:]).then_inc(*OUT("comb_spread", l, "first"))
                sg.skip("comb_spread", NE)
                nf, ne = l * NE * 4, l * NE
                with act.Fori(0, NE, 2) as e:
                    for u in range(2):
                        for f in range(4):
                            if f == 1:
                                act.wait_ge(sg.sem("comb_rowed"), e + (ne + u + 1))
                                act.wait_ge(sg.sem("he_gated"), e * 4 + (nf + 4 * (l + 1) + 4 * u - 3))
                                copy(cb[:, u, t0:], ps[:, 7, t0:]).then_inc(sg.sem("comb_spread"), 1)
                            act.wait_ge(sg.sem("h13_done"), e * 4 + (nf + 4 * u + f + 1))
                            act.wait_ge(sg.sem("he_gated"), e * 4 + (nf + 4 * (l + 1) + 4 * u + f - 1))
                            A(sil[:, f % 2, t0:], ps[:, f % 2, t0:], ACT.Silu).then_inc(sg.sem("silu_done"), 1)

            act.wait_ge(*GOT("const_in"))
            A(ca[:, :, :], cc[:, :, :], ACT.Silu).then_inc(*OUT("cond_ready"))
            for l in range(DEPTH):
                norm(l, 0)
                rwkv_inputs(l)
                for c in range(STEPS):
                    rwkv_step(l, c)
                rwkv_readout(l)
                attention_inputs(l)
                attention(l)
                gmlp(l)
                merge(l)
                norm(l, 1)
                experts(l)
            norm(DEPTH, 0)

        @block.vector
        def _(dve):
            V = dve
            TT = V.tensor_tensor

            def heads(a, n=HEADS):
                return a.rearrange("p (h v) -> p h v", h=n)

            def norm(l, which):
                t0 = 0 if l < DEPTH and which == 0 else CTX if l == DEPTH else t0_of(l)
                V.wait_ge(*GOT("norm_rooted", l, which))
                V.reciprocal(rt[:, t0:], rt[:, t0:]).then_inc(*OUT("norm_rs", l, which))
                V.wait_ge(*GOT("norm_rs", l, which))
                for k in range(KT):
                    if l == DEPTH:
                        V.scalar_tensor_tensor(out=h[:, k, 0:LAT], in0=x[:, k, CTX:], scalar=vec[:, V_FG + k:V_FG + k + 1],
                                               in1=rt[:, t0:], op0=ALU.mult, op1=ALU.mult).then_inc(*OUT("out_ready"))
                    else:
                        TT(h[:, k, t0:], x[:, k, t0:], rt[:, t0:], ALU.mult).then_inc(*OUT("x_scaled", l, which, k))

            def modulation(l):
                V.wait_ge(*GOT("param_in", l))
                V.wait_ge(*GOT("chunk_used", "mod", l, 47))
                if l:
                    V.wait_ge(sg.sem("x_added"), XL * l)
                TT(mod[:, :, :], ps[:, 0, 0:96].rearrange("p (j s) -> p j s", s=2),
                   vec[:, V_MODB:V_MODB + 48].unsqueeze(2).to_broadcast([P, 48, 2]), ALU.add).then_inc(*OUT("mod_sum", l))
                V.wait_ge(*GOT("mod_sum", l))
                for q, (m, g) in enumerate(((8, V_N1), (32, V_N2))):
                    V.scalar_tensor_tensor(out=gain[:, q, :, :], in0=mod[:, m:m + 8, :], scalar=1.0,
                                           in1=vec[:, g:g + 8].unsqueeze(2).to_broadcast([P, 8, 2]),
                                           op0=ALU.add, op1=ALU.mult).then_inc(*OUT("mod_step", l, q))
                mu = vec[:, V_MU:V_MU + 15]
                V.tensor_scalar(mu2[:, 0, :], mu, 0.5, None, ALU.mult).then_inc(*OUT("mod_step", l, 2))
                V.tensor_scalar(mu2[:, 1, :], mu, -1.0, 1.0, ALU.mult, ALU.add).then_inc(*OUT("mod_ready", l))

            def rwkv_inputs(l):
                V.wait_ge(*GOT("x_scaled", l, 0, KT - 1))
                V.memset(view(MB, 1032), 0.0).then_inc(*OUT("raw_clear", l))
                V.memset(rt[:, 0:256], 0.0).then_inc(*OUT("lora_clear", l))
                V.memset(state, 0.0).then_inc(*OUT("state_clear", l))
                V.wait_ge(*GOT("mod_ready", l))
                where = list(range(12)) + [ZW, ZA, ZG]
                for i in range(15):
                    V.wait_ge(*GOT("raw_copied", l, i))
                    if i >= 2:
                        V.wait_ge(*GOT("z_mixed", l, i - 2))
                    r, s_ = raw[:, i % 2, :, :], shs[:, i % 2, :, :]
                    TT(s_, r[:, :, 0:256], r[:, :, 2:258], ALU.add).then_inc(*OUT("z_sides", l, i))
                    V.wait_ge(*GOT("z_sides", l, i))
                    V.tensor_scalar(s_, s_, mu2[:, 0, i:i + 1], None, ALU.mult).then_inc(*OUT("z_half", l, i))
                    V.wait_ge(*GOT("z_half", l, i))
                    V.scalar_tensor_tensor(out=zc[:, where[i], :].rearrange("p (s t) -> p s t", s=2), in0=r[:, :, 1:257],
                                           scalar=mu2[:, 1, i:i + 1], in1=s_, op0=ALU.mult, op1=ALU.add) \
                        .then_inc(*OUT("z_mixed", l, i))
                V.wait_ge(*GOT("z_mixed", l, 14))
                for f in range(4):
                    V.tensor_scalar(zc[:, ZKK + f, :], zc[:, ZK + f, :], vec[:, V_KK + f:V_KK + f + 1], None, ALU.mult) \
                        .then_inc(*OUT("kk_raw", l, f))
                for f in range(4):
                    V.wait_ge(*GOT("kk_raw", l, f))
                    if f >= 2:
                        V.wait_ge(*GOT("kk_done", l, f - 2))
                    TT(kks[:, f % 2, :], zc[:, ZKK + f, :], zc[:, ZKK + f, :], ALU.mult).then_inc(*OUT("kk_squared", l, f))
                    V.wait_ge(*GOT("kk_summed", l, f))
                    V.tensor_scalar(kks[:, f % 2, :], ps[:, 2 + f % 2, :], 1e-12, None, ALU.max) \
                        .then_inc(*OUT("kk_clamped", l, f))
                    V.wait_ge(*GOT("kk_rooted", l, f))
                    V.reciprocal(kks[:, f % 2, :], kks[:, f % 2, :]).then_inc(*OUT("kk_inv", l, f))
                    V.wait_ge(*GOT("kk_inv", l, f))
                    TT(zc[:, ZKK + f, :], zc[:, ZKK + f, :], kks[:, f % 2, :], ALU.mult).then_inc(*OUT("kk_done", l, f))
                V.wait_ge(*GOT("kk_done", l, 3))
                V.memset(view(MB, 4 * 512), 0.0).then_inc(*OUT("blocks_clear", l))

            def rwkv_step(l, c):
                T = [tok[:, i, :] for i in range(8)]
                for q in range(2):
                    V.wait_ge(*GOT("tanhed", l, c, q))
                    V.tensor_scalar(T[q], T[q], 0.5, 0.5, ALU.mult, ALU.add).then_inc(*OUT("sig_done", l, c, q))
                V.wait_ge(*GOT("sig_done", l, c, 1))
                V.wait_ge(*GOT("tokens_turned", l, c))
                if c:
                    V.wait_ge(*GOT("operand_in", l, c - 1, 1, 3, 1))
                r, k, kk = ps[:, 0, :], ps[:, 1, :], ps[:, 3, :]
                TT(T[6], kk, T[1], ALU.mult).then_inc(*OUT("kka", l, c))
                V.scalar_tensor_tensor(out=T[7], in0=T[1], scalar=1.0, in1=rep[:, 0, :], op0=ALU.subtract, op1=ALU.mult) \
                    .then_inc(*OUT("kd_half", l, c))
                V.wait_ge(*GOT("kd_half", l, c))
                V.scalar_tensor_tensor(out=T[7], in0=T[7], scalar=1.0, in1=k, op0=ALU.add, op1=ALU.mult) \
                    .then_inc(*OUT("kd_done", l, c))
                V.wait_ge(*GOT("kd_done", l, c))
                TT(T[1], r, T[7], ALU.mult).then_inc(*OUT("bonus_a", l, c))
                V.wait_ge(*GOT("bonus_a", l, c))
                TT(T[1], T[1], rep[:, 1, :], ALU.mult).then_inc(*OUT("bonus_b", l, c))
                V.wait_ge(*GOT("bonus_b", l, c))
                V.tensor_reduce(osb[:, c, CW:CW + HEADS], heads(T[1]), AX.X, ALU.add).then_inc(*OUT("bonus_kept", l, c))
                V.wait_ge(*GOT("exps", l, c, 2))
                for q, (t, a, b) in enumerate(((T[3], kk, T[3]), (T[2], r, T[2]), (T[6], T[6], T[4]), (T[7], T[7], T[4]))):
                    TT(t, a, b, ALU.mult).then_inc(*OUT("operand", l, c, q))
                for g in range(2):
                    rwkv_matrices(l, c, g)

            def rwkv_matrices(l, c, g):
                k = (l, c, g)

                def bank(b):
                    return ps[:, b, :].rearrange("p (h t) -> p h t", t=P)

                def wide(m):
                    return C(m).unsqueeze(1).to_broadcast([P, HG, P])
                V.wait_ge(*GOT("turned", *k))
                V.tensor_copy(b_t, bank(2)).then_inc(*OUT("turned_kept_v", *k, 2))
                V.tensor_copy(g_t, bank(3)).then_inc(*OUT("turned_kept_v", *k, 3))
                V.wait_ge(*GOT("gram", *k))
                gb = ps[:, 4:6, :].rearrange("p b (h t) -> p (b h) t", t=2 * P)
                gg = ps[:, 6:8, :].rearrange("p b (h t) -> p (b h) t", t=2 * P)
                for q, (o, i, m) in enumerate(((n_t, gb[:, :, 0:P], C_NDT), (n_, bank(0), C_ND), (go_, bank(0), C_NO),
                                               (qb_, gb[:, :, P:], C_MI), (bt_, gg[:, :, 0:P], C_MS),
                                               (qg_, gg[:, :, P:], C_MI))):
                    TT(o, i, wide(m), ALU.mult).then_inc(*OUT("masked", *k, q))
                V.wait_ge(*GOT("p_nt2", *k))
                V.tensor_copy(b_t, bank(1)).then_inc(*OUT("nt2_kept", *k))
                TT(x_, n_t, wide(C_ID), ALU.add).then_inc(*OUT("x1_done", *k))
                V.wait_ge(*GOT("x1_done", *k))
                TT(x_, x_, b_t, ALU.add).then_inc(*OUT("x1b_done", *k))
                V.wait_ge(*GOT("x1b_done", *k))
                V.wait_ge(*GOT("p_nt3", *k))
                TT(m_a, bank(3), x_, ALU.add).then_inc(*OUT("x2_done", *k))
                V.wait_ge(*GOT("p_nt4", *k))
                V.tensor_copy(nt4_, bank(5)).then_inc(*OUT("nt4_kept", *k))
                V.wait_ge(*GOT("x2_done", *k))
                V.wait_ge(*GOT("p_x4", *k))
                TT(m_r, bank(6), m_a, ALU.add).then_inc(*OUT("x4_done", *k))
                V.wait_ge(*GOT("p_n8", *k))
                V.tensor_copy(n8_, bank(7)).then_inc(*OUT("n8_kept", *k))
                V.wait_ge(*GOT("x4_done", *k))
                V.wait_ge(*GOT("p_x8", *k))
                TT(x_t, bank(1), m_r, ALU.add).then_inc(*OUT("xt_done", *k))
                V.wait_ge(*GOT("p_ht", *k))
                V.tensor_copy(n_t, bank(3)).then_inc(*OUT("ht_kept", *k))
                V.wait_ge(*GOT("ht_kept", *k))
                TT(nt4_, n_t, wide(C_ID), ALU.add).then_inc(*OUT("w1_done", *k))
                V.wait_ge(*GOT("ht2_kept", *k))
                V.wait_ge(*GOT("w1_done", *k))
                TT(nt4_, nt4_, n4_, ALU.add).then_inc(*OUT("w2_done", *k))
                V.wait_ge(*GOT("w2_done", *k))
                V.wait_ge(*GOT("p_ht3", *k))
                TT(nt4_, bank(6), nt4_, ALU.add).then_inc(*OUT("w_done", *k))
                h0 = g * HG
                s_ = state[:, h0:h0 + HG, :]
                V.wait_ge(*GOT("p_s", *k))
                V.wait_ge(*GOT("p_o" if keep0(l, c) else "p_s", *k))
                TT(s_, ps[:, 3, 0:HG * HD].rearrange("p (h v) -> p h v", v=HD), s_, ALU.add).then_inc(*OUT("state_sum", *k))
                V.wait_ge(*GOT("state_sum", *k))
                V.wait_ge(*GOT("exps", l, c, 3))
                TT(s_, s_, st[:, h0:h0 + HG].unsqueeze(2).to_broadcast([P, HG, HD]), ALU.mult).then_inc(*OUT("state_new", *k))

            def rwkv_readout(l):
                for i in range(t0_of(l) // P, NT):
                    def spread(a):
                        return a.unsqueeze(2).to_broadcast([P, HEADS, HD])
                    a, b = heads(tok[:, 0, :]), heads(tok[:, 1, :])
                    V.wait_ge(*GOT("read", l, i))
                    if i > t0_of(l) // P:
                        V.wait_ge(*GOT("yc_turned", l, i - 1))
                    V.tensor_reduce(st[:, 8:16], heads(ps[:, 0, :]), AX.X, ALU.add).then_inc(*OUT("ro", l, i, 0))
                    V.tensor_copy(st[:, 24:32], ps[:, 1, 0:8]).then_inc(*OUT("ro", l, i, 1))
                    V.wait_ge(*GOT("ro", l, i, 1))
                    V.tensor_scalar(st[:, 8:16], st[:, 8:16], 1.0 / HD, None, ALU.mult).then_inc(*OUT("ro", l, i, 2))
                    TT(b, heads(ps[:, 2, :]), spread(st[:, 24:32]), ALU.mult).then_inc(*OUT("ro", l, i, 3))
                    V.wait_ge(*GOT("ro", l, i, 2))
                    TT(a, heads(ps[:, 0, :]), spread(st[:, 8:16]), ALU.subtract).then_inc(*OUT("ro", l, i, 4))
                    V.wait_ge(*GOT("ro", l, i, 4))
                    TT(heads(tok[:, 2, :]), a, a, ALU.mult).then_inc(*OUT("ro", l, i, 5))
                    V.wait_ge(*GOT("ro", l, i, 5))
                    V.tensor_reduce(st[:, 16:24], heads(tok[:, 2, :]), AX.X, ALU.add).then_inc(*OUT("var_done", l, i))
                    V.wait_ge(*GOT("var_rooted", l, i))
                    V.reciprocal(st[:, 16:24], st[:, 16:24]).then_inc(*OUT("ro", l, i, 6))
                    V.wait_ge(*GOT("ro", l, i, 6))
                    TT(a, a, spread(st[:, 16:24]), ALU.mult).then_inc(*OUT("ro", l, i, 7))
                    for q, (z, op) in enumerate(((rep[:, 2, :], ALU.mult), (rep[:, 3, :], ALU.add), (tok[:, 1, :], ALU.add))):
                        V.wait_ge(*GOT("ro", l, i, 7 + q))
                        TT(tok[:, 0, :], tok[:, 0, :], z, op).then_inc(*OUT("ro", l, i, 8 + q))
                    V.wait_ge(*GOT("ro", l, i, 10))
                    TT(tok[:, 0, :], ps[:, 3, :], tok[:, 0, :], ALU.mult).then_inc(*OUT("yc_done", l, i))

            def attention_inputs(l):
                t0 = t0_of(l)
                for i in range(2):
                    V.wait_ge(*GOT("zb_rooted", l, i))
                    V.reciprocal(pr[:, 0, i, :], pr[:, 0, i, :]).then_inc(*OUT("zb_inv", l, i))
                for i in range(5):
                    V.wait_ge(*GOT("zb_inv", l, 0 if i < 3 else 1))
                    V.scalar_tensor_tensor(out=zq[:, i, :], in0=zq[:, i, :], scalar=vec[:, V_QN + i:V_QN + i + 1],
                                           in1=pr[:, 0, 0 if i < 3 else 1, :], op0=ALU.mult, op1=ALU.mult) \
                        .then_inc(*OUT("zb_scaled", l, i))

                def rope(src, dst, name, *key):
                    b = rtmp[64:96, :, :, :]
                    TT(b[:, 0, 0, :], src[96:128, CTX:], cs[96:128, 1, :], ALU.mult).then_inc(*OUT("rope_sin", name, *key))
                    TT(b[:, 1, 0, :], src[64:96, CTX:], cs[64:96, 0, :], ALU.mult).then_inc(*OUT("rope_cos", name, *key))
                    V.wait_ge(*GOT("rope_cos", name, *key))
                    return TT(dst, b[:, 0, 0, :], b[:, 1, 0, :], ALU.add)

                V.wait_ge(*GOT("chunk_used", "zb", l, 5))
                V.tensor_copy(kt_[64:96, 0, 0:CTX], ps[64:96, 1, 0:CTX]).then_inc(*OUT("kr_ctx", l))
                rope(ps[:, 1, :], kt_[64:96, 0, CTX:], "k", l).then_inc(*OUT("kr_made", l))
                V.wait_ge(*GOT("kr_made", l))
                V.wait_ge(*GOT("kr_ctx", l))
                V.tensor_copy(kt_[64:96, 1:HEADS, :], kt_[64:96, 0:1, :].to_broadcast([32, HEADS - 1, TOK])) \
                    .then_inc(*OUT("kr_spread", l))
                for hh in range(HEADS):
                    V.wait_ge(*(GOT("q_made", l, hh) if hh % 2 == 0 else GOT("chunk_used", "uq", l, hh // 2)))
                    V.wait_ge(*(GOT("kr_made", l) if hh == 0 else GOT("q_roped", l, hh - 1)))
                    if t0 == 0:
                        V.tensor_copy(qt[64:96, hh, 0:CTX], ps[64:96, 4 + hh % 2, 0:CTX]).then_inc(*OUT("q_mid", l, hh))
                    rope(ps[:, 4 + hh % 2, :], qt[64:96, hh, CTX:], "q", l, hh).then_inc(*OUT("q_roped", l, hh))

            def attention(l):
                pairs = attention_pairs(l)

                def maxima(n):
                    nk = 4 if pairs[n][0] else 2
                    c0 = 32 + n % 2 * 8
                    V.wait_ge(*GOT("scores", l, n))
                    V.tensor_reduce(st[:, c0 + 4:c0 + 6], ps[:, n % 2 * 2:n % 2 * 2 + 2, 0:nk * P], AX.X, ALU.max) \
                        .then_inc(*OUT("max_raw", l, n))
                    V.wait_ge(*GOT("max_raw", l, n))
                    V.tensor_scalar(st[:, c0:c0 + 2], st[:, c0 + 4:c0 + 6], -MLA_SCALE, None, ALU.mult) \
                        .then_inc(*OUT("max_done", l, n))

                maxima(0)
                for n in range(len(pairs)):
                    nk = 4 if pairs[n][0] else 2
                    c0 = 32 + n % 2 * 8
                    if n + 1 < len(pairs):
                        maxima(n + 1)
                    V.wait_ge(*GOT("prob", l, n, 1))
                    V.reciprocal(st[:, c0 + 2:c0 + 4], st[:, c0 + 2:c0 + 4]).then_inc(*OUT("sum_inv", l, n))
                    V.wait_ge(*GOT("sum_inv", l, n))
                    for q in range(2):
                        p_ = pr[:, n % 2, q, 0:nk * P]
                        V.tensor_scalar(p_, p_, st[:, c0 + 2 + q:c0 + 3 + q], None, ALU.mult) \
                            .then_inc(*OUT("prob_scaled", l, n, q))

            def gmlp(l):
                t0 = t0_of(l)
                V.wait_ge(*GOT("v_rooted", l))
                s_ = st[:, 52 + t0 // P:56]
                V.reciprocal(s_, s_).then_inc(*OUT("v_inv", l))
                V.wait_ge(*GOT("v_inv", l))
                for t in range(t0 // P, NT):
                    V.tensor_scalar(vg[:, t, :], vg[:, t, :], st[:, 52 + t:53 + t], None, ALU.mult) \
                        .then_inc(*OUT("v_normed", l, t))
                for g in range(4):
                    V.wait_ge(*GOT("mixed", l, g))
                    o = at[:, g, t0:].rearrange("p (t i) -> p t i", i=P)
                    n = NT - t0 // P
                    V.scalar_tensor_tensor(out=o, in0=ps[:, 4 + g, t0:].rearrange("p (t i) -> p t i", i=P),
                                           scalar=vec[:, V_AVG + g:V_AVG + g + 1],
                                           in1=bs[:, g:g + 1, :].to_broadcast([P, n, P]), op0=ALU.mult, op1=ALU.add) \
                        .then_inc(*OUT("mix_biased", l, g))
                    V.wait_ge(*GOT("mix_biased", l, g))
                    TT(y[:, g, t0:], at[:, g, t0:], ut[:, g, t0:], ALU.mult).then_inc(*OUT("ya_done", l, g))

            def merge(l):
                t0 = t0_of(l)
                for j in range(KT):
                    V.wait_ge(*GOT("chunk_used", "up", l, j, 1))
                    V.wait_ge(*GOT("gated", l, j, 2))
                    o = mg[:, j, t0:]
                    for g in range(3):
                        s_ = sgm[:, j % 2, g, t0:]
                        TT(s_ if g else o, ps[:, 3 + g, t0:], s_, ALU.mult).then_inc(*OUT("merged", l, j, g))
                    for g in (1, 2):
                        V.wait_ge(*GOT("merged", l, j, g + 1))
                        TT(o, o, sgm[:, j % 2, g, t0:], ALU.add).then_inc(*OUT("merged", l, j, 2 + g))
                for j in range(KT):
                    V.wait_ge(*GOT("chunk_used", "wo", l, j))
                    for s in range(t0 // CTX, 2):
                        r = slice(s * CTX, (s + 1) * CTX)
                        ins = V.scalar_tensor_tensor(out=x[:, j, r], in0=ps[:, 6 + j % 2, r], scalar=mod[:, 16 + j, s:s + 1],
                                                     in1=x[:, j, r], op0=ALU.mult, op1=ALU.add)
                    ins.then_inc(*OUT("x_added", l, j))

            def router(l):
                a = t0_of(l) // P
                n = NT - a
                G = n * NG

                def grp(t):
                    return t[:, a:, :].rearrange("p t (g e) -> p (t g) e", e=EPG)
                rank = small[:, 2 + P + NE:2 + P + NE + EPG]
                dec = rank.unsqueeze(1).to_broadcast([P, G, EPG])
                m = rt[:, 0:16 * 8].rearrange("p (m g) -> p m g", g=16)
                step = [0]

                def run(ins):
                    step[0] += 1
                    ins.then_inc(*OUT("route", l, step[0]))
                    V.wait_ge(*GOT("route", l, step[0]))

                def over(i, e=EPG):
                    return m[:, i, 0:G].unsqueeze(2).to_broadcast([P, G, e])

                def top(src, i, onehot):
                    run(V.tensor_reduce(m[:, i, 0:G], src, AX.X, ALU.max))
                    run(TT(onehot, src, over(i), ALU.is_equal))
                    run(TT(onehot, onehot, dec, ALU.mult))
                    run(V.tensor_reduce(m[:, 7, 0:G], onehot, AX.X, ALU.max))
                    run(TT(onehot, onehot, over(7), ALU.is_equal))

                V.wait_ge(*GOT("scored", l))
                run(TT(sel[:, a:, :], score[:, a:, :], rb[:, :].unsqueeze(1).to_broadcast([P, n, NE]), ALU.add))
                top(grp(sel), 0, grp(first))
                run(V.scalar_tensor_tensor(out=grp(pick), in0=grp(first), scalar=-1e30, in1=grp(sel), op0=ALU.mult, op1=ALU.add))
                top(grp(pick), 1, grp(second))
                run(TT(m[:, 2, 0:G], m[:, 0, 0:G], m[:, 1, 0:G], ALU.add))

                def rows(i):
                    return m[:, i, 0:G].rearrange("p (t g) -> p t g", g=NG)
                dg = rank.unsqueeze(1).to_broadcast([P, n, NG])

                def wide(i):
                    return m[:, i, 0:n].unsqueeze(2).to_broadcast([P, n, NG])
                run(V.tensor_reduce(m[:, 3, 0:n], rows(2), AX.X, ALU.max))
                run(TT(rows(4), rows(2), wide(3), ALU.is_equal))
                run(TT(rows(4), rows(4), dg, ALU.mult))
                run(V.tensor_reduce(m[:, 3, 0:n], rows(4), AX.X, ALU.max))
                run(TT(rows(4), rows(4), wide(3), ALU.is_equal))
                run(TT(grp(first), grp(first), grp(second), ALU.add))
                run(TT(grp(first), grp(first), over(4), ALU.mult))
                run(TT(first[:, a:, :], first[:, a:, :], score[:, a:, :], ALU.mult))
                run(V.tensor_reduce(m[:, 5, 0:n], first[:, a:, :], AX.X, ALU.add))
                run(V.reciprocal(m[:, 5, 0:n], m[:, 5, 0:n]))
                TT(comb[:, a:, :], first[:, a:, :], m[:, 5, 0:n].unsqueeze(2).to_broadcast([P, n, NE]), ALU.mult) \
                    .then_inc(*OUT("comb_done", l))

            def experts(l):
                t0 = t0_of(l)
                nf, nd, ne = l * NE * 4, l * NE * 8, l * NE
                V.wait_ge(*GOT("comb_spread", l, "first"))
                for i in range(4):
                    V.memset(st[:, 60:61], 0.0).then_inc(sg.sem("he_gated"), 1)
                    V.wait_ge(sg.sem("he_gated"), nf + 4 * l + i + 1)
                with V.Fori(0, NE, 2) as e:
                    for u in range(2):
                        V.wait_ge(sg.sem("comb_rowed"), e + (ne + u))
                        V.tensor_scalar(cmask[0:NE, t0:], cmb[:, t0:], small[0:NE, bass.ds(e + (2 + P + u), 1)], None, ALU.mult) \
                            .then_inc(sg.sem("comb_masked"), 1)
                        for f in range(4):
                            V.wait_ge(sg.sem("silu_done"), e * 4 + (nf + 4 * u + f + 1))
                            TT(he[:, u, f, t0:], ps[:, 2 + f % 2, t0:], sil[:, f % 2, t0:], ALU.mult) \
                                .then_inc(sg.sem("he_gated"), 1)
                            V.wait_ge(sg.sem("he_gated"), e * 4 + (nf + 4 * (l + 1) + 4 * u + f + 1))
                            V.wait_ge(sg.sem("comb_spread"), e + (ne + u + l + 2))
                            TT(he[:, u, f, t0:], he[:, u, f, t0:], cb[:, u, t0:], ALU.mult).then_inc(sg.sem("he_done"), 1)
                        for d in range(KT):
                            V.wait_ge(sg.sem("y_done"), e * 8 + (nd + 8 * u + d + 1))
                            V.wait_ge(sg.sem("x_added"), e * 8 + (XL * l + 8 * u + d + 1))
                            for s in range(t0 // CTX, 2):
                                r = slice(s * CTX, (s + 1) * CTX)
                                ins = V.scalar_tensor_tensor(out=x[:, d, r], in0=ps[:, 4 + d % 2, r],
                                                             scalar=mod[:, 40 + d, s:s + 1], in1=x[:, d, r],
                                                             op0=ALU.mult, op1=ALU.add)
                            ins.then_inc(sg.sem("x_added"), 1)
                sg.skip("x_added", NE * KT)

            V.memset(eps[:, 0:1], EPS).then_inc(*OUT("eps_half"))
            V.memset(eps[:, 1:2], GN_EPS).then_inc(*OUT("eps_set"))
            V.wait_ge(*GOT("const_in"))
            for l in range(DEPTH):
                modulation(l)
                norm(l, 0)
                rwkv_inputs(l)
                for c in range(STEPS):
                    rwkv_step(l, c)
                rwkv_readout(l)
                attention_inputs(l)
                attention(l)
                gmlp(l)
                merge(l)
                norm(l, 1)
                router(l)
                experts(l)
            norm(DEPTH, 0)

        @block.gpsimd
        def _(pool):
            last = []

            def alone():
                if last:
                    pool.wait_ge(*GOT(*last[-1]))

            for l in range(DEPTH):
                for c in range(STEPS):
                    if c == 0:
                        pool.wait_ge(*GOT("kk_done", l, 3))
                        pool.wait_ge(*GOT("z_mixed", l, 14))
                        pool.wait_ge(*GOT("blocks_clear", l))
                    for d in range(2):
                        if c:
                            pool.wait_ge(*GOT("tokens_turned", l, c - 1))
                        a = chunk_start(c, d)
                        alone()
                        pool.tensor_copy(stage[:, :, d * CH:(d + 1) * CH], zc[:, 0:16, a:a + CH]).then_inc(*OUT("staged", l, c, d))
                        last.append(("staged", l, c, d))
                    for g in range(2):
                        if c or g:
                            pl = (l, c, 0) if g else (l, c - 1, 1)
                            pool.wait_ge(*GOT("p_s", *pl))
                            pool.wait_ge(*GOT("xt_done", *pl))
                        for q, (m, t) in enumerate(((m_a, 3), (m_r, 2), (m_b, 6), (m_g, 7))):
                            pool.wait_ge(*GOT("operand", l, c, q))
                            for d in range(2):
                                r = slice(d * CH, (d + 1) * CH)
                                alone()
                                pool.tensor_copy(m[r, :, d * HD:(d + 1) * HD],
                                                 tok[r, t, g * 256:(g + 1) * 256].rearrange("p (h v) -> p h v", v=HD)) \
                                    .then_inc(*OUT("operand_in", l, c, g, q, d))
                                last.append(("operand_in", l, c, g, q, d))

        return sg.at


def layout(i):
    def chunk(wt):
        k, n = wt.shape[-2:]
        a = np.moveaxis(wt.reshape(wt.shape[:-2] + (k // P, P, n)), -3, -2)
        return a.reshape(a.shape[:-2] + (k // P * n,))

    def chunks(wt):
        L_, k, n = wt.shape
        a = wt.reshape(L_, k // P, P, n // P, P).transpose(0, 3, 2, 1, 4)
        return a.reshape(L_, n // P, P, k)

    def cols(v):
        return v.reshape(-1, P).T

    def per(f):
        return np.stack([f(l) for l in range(DEPTH)])
    swap = np.array([a * 16 + (1 - b) * 8 + f for a in range(2) for b in range(2) for f in range(8)])
    w_in = i["w_in"]
    b_cols = QL + KVL + ROPE
    c_cols = 15 * P
    kr = w_in[:, :, QL + KVL:b_cols]
    zb = np.concatenate([w_in[:, :, :QL + KVL], kr, kr, kr, kr[:, :, swap]], -1)
    a0 = b_cols + c_cols
    uq = i["b_w_uq"].reshape(DEPTH, QL, HEADS, QK)
    uq = np.concatenate([uq, uq[..., NOPE + swap]], -1).reshape(DEPTH, 3, P, 4, 2, P).transpose(0, 3, 2, 4, 1, 5)
    ukv = i["b_w_ukv"].reshape(DEPTH, 2, P, HEADS, NOPE + VD)
    up = np.stack([i["w_up_a"], i["w_up_b"], i["w_up_c"]], 1).reshape(DEPTH, 3, 4, P, KT, P)
    zv = w_in[:, :, a0 + CW:a0 + 2 * CW].reshape(DEPTH, 4, 2, P, CW).transpose(0, 1, 3, 2, 4)
    ones = np.ones((1, P, 1), np.float32)

    def spread(v):
        return np.broadcast_to(v, (P,) + v.shape)
    xs = np.concatenate([i["ctx"][0], i["x"][0]], 0)
    d = {
        "x": xs.T.reshape(KT, P, TOK).transpose(1, 0, 2),
        "cc": np.stack([i["c_ctx"], i["c"][0]], -1).reshape(KT, P, 2).transpose(1, 0, 2),
        "con": constants(), "small": small_constants(), "cs": rope_tables()[64:],
        "rw": i["router_w"].reshape(KT, P, NE).transpose(1, 0, 2),
        "rb": spread(i["router_b"]),
        "mod": chunks(i["mod_w"]),
        "zc": chunks(w_in[:, :, b_cols:a0]),
        "zb": chunks(zb),
        "uq": uq.reshape(DEPTH, 4, P, 768),
        "uk": ukv[..., :NOPE].transpose(0, 2, 3, 1, 4).reshape(DEPTH, P, SLOT),
        "uv": ukv[..., NOPE:].transpose(0, 2, 1, 3, 4).reshape(DEPTH, P, SLOT),
        "zu": chunks(w_in[:, :, a0:a0 + CW]),
        "zv": zv.reshape(DEPTH, 4, P, SLOT),
        "gate": chunks(w_in[:, :, a0 + 2 * CW:]),
        "up": up.transpose(0, 4, 3, 1, 2, 5).reshape(DEPTH, KT, P, 1536),
        "wo": chunks(i["w_o"]),
        "w13": np.concatenate([i["moe_w1"], i["moe_w3"]], -1).reshape(DEPTH, NE, KT, P, 2 * DE).transpose(0, 1, 3, 2, 4),
        "w2": i["moe_w2"].reshape(DEPTH, NE, 4, P, D).transpose(0, 1, 3, 2, 4),
        "vec": per(lambda l: np.concatenate([cols(i[n][l]) for n in ("norm1_g", "norm2_g", "mod_b", "b_q_norm", "b_kv_norm",
                                             "a_v_gain", "c_mu", "c_k_k")] + [cols(i["final_g"])], 1)),
        "rep": per(lambda l: spread(np.stack([i["c_k_a"][l], i["c_r_k"][l].reshape(-1), i["c_gn_g"][l], i["c_gn_b"][l]]))),
        "lora": per(lambda l: np.stack([i["c_w2"][l].reshape(P, CW), i["c_a2"][l].reshape(P, CW), i["c_g2"][l]], 1)),
        "bias2": per(lambda l: np.stack([i["c_w0"][l], i["c_a0"][l]], 1)),
        "bs": per(lambda l: spread(i["a_bs"][l])),
        "ws": i["a_ws"].transpose(0, 3, 1, 2),
    }
    return {k: np.ascontiguousarray(v) for k, v in d.items()}


def kernel(**inputs):
    import concourse.bacc as bacc
    from concourse.bass_utils import run_bass_kernel_spmd as run

    arrays = layout({k: np.asarray(v) for k, v in inputs.items()})
    known = None
    for _ in range(2):
        nc = bacc.Bacc("TRN2", target_bir_lowering=False, num_devices=1)
        w = {k: nc.dram_tensor(f"in_{k}", v.shape, F32, kind="ExternalInput").ap() for k, v in arrays.items()}
        out = nc.dram_tensor("out", (P, KT, LAT), F32, kind="ExternalOutput").ap()
        known = build(nc, w, out, known)
    r = run(nc, [{f"in_{k}": v for k, v in arrays.items()}], core_ids=[0])
    return r.results[0]["out"].transpose(2, 1, 0).reshape(1, LAT, D)
```

```python
from contextlib import ExitStack

import numpy as np
import concourse.bass as bass
from concourse import mybir

F32 = mybir.dt.float32
ACT = mybir.ActivationFunctionType
ALU = mybir.AluOpType
AX = mybir.AxisListType

P = 128
DEPTH = 2
D = 1024
KT = D // P
CTX = 256
LAT = 256
TOK = CTX + LAT
NT = TOK // P
EPS = 1e-6
GN_EPS = 64e-5
DECAY = 0.6065306597126334
HEADS = 8
HD = 64
NOPE, ROPE, VD = 64, 32, 64
QK = NOPE + ROPE
QL, KVL = 384, 256
MLA_SCALE = float((NOPE + ROPE) ** -0.5)
CW = 512
CH = 64
STEPS = TOK // CH
HS = 4
HU = 2
NE, NG, EPG, DE = 16, 4, 4, 512
RING = 4
SLOT = 1024
CAP = P
FAR = 4096.0

V_N1, V_N2, V_MODB, V_QN, V_KVN, V_AVG, V_MU, V_KK, V_FG = 0, 8, 16, 64, 67, 69, 73, 88, 92
NVEC = 100
ZR, ZK, ZV, ZKK, ZW, ZA, ZG = 0, 4, 8, 12, 16, 17, 18
(C_ID, C_ONE, C_BONE, C_NDT, C_MS, C_MI, C_ND, C_NO, C_S00, C_S01, C_S10, C_S11, C_TRI, C_IOTA) = range(14)
NCONST = 14


def constants():
    c = np.zeros((NCONST, P, P), np.float32)
    row = np.arange(P)
    d, t = row // CH, row % CH
    same = d[:, None] == d[None, :]
    fwd = d[:, None] == 0
    before = np.where(fwd, t[:, None] < t[None, :], t[:, None] > t[None, :]) & same
    equal = np.eye(P, dtype=bool)
    block = (t[:, None] // 16) == (t[None, :] // 16)
    c[C_ID] = equal
    c[C_ONE] = 1.0
    c[C_TRI] = row[:, None] < row[None, :]
    c[C_IOTA] = row[None, :]
    c[C_BONE] = same
    c[C_MS] = before
    c[C_MI] = before | equal
    c[C_NDT] = -(before & block).astype(np.float32)
    c[C_ND] = c[C_NDT].T
    c[C_NO] = -(before & ~block).astype(np.float32).T
    for dd in range(2):
        for half in range(2):
            for i in range(CH):
                c[C_S00 + 2 * dd + half, dd * CH + i, half * CH + i] = 1.0
    return np.ascontiguousarray(c.transpose(1, 0, 2))


def small_constants():
    s = np.zeros((P, 2 + P + 16 + 4), np.float32)
    s[:CH, 0] = 1.0
    s[CH:, 1] = 1.0
    s[0, 2:2 + CH] = 1.0
    s[1, 2 + CH:2 + P] = 1.0
    s[:16, 2 + P:2 + P + 16] = np.eye(16)
    s[:, 2 + P + 16:] = [4.0, 3.0, 2.0, 1.0]
    return s


def rope_tables():
    nf = ROPE // 4
    tok = np.arange(LAT)
    pos = np.stack([tok // 64, tok % 64], 0).astype(np.float32)
    inv = np.power(np.float32(10000.0), -np.arange(nf, dtype=np.float32) / nf)
    out = np.zeros((P, 2, LAT), np.float32)
    for ax in range(2):
        ang = pos[ax][None, :] * inv[:, None]
        for half in range(2):
            r = ax * 2 * nf + half * nf
            out[64 + r:64 + r + nf, 0] = np.cos(ang)
            out[96 + r:96 + r + nf, 1] = np.sin(ang) * (-1.0 if half == 0 else 1.0)
    return out


SHARED = {
    "products_of_inverse": "p_nt2 p_n2 p_nt3 p_n4 p_nt4 p_x4 p_n8 p_x8 p_h p_ht p_x p_ht2 p_ht3 p_tt",
    "products_of_chain": "p_r p_u p_s p_o turned gram tokens_turned logits cums",
    "products_of_attention": "q_made k_made v_made scores prob_turned attended zb_summed",
    "products_of_rest": "norm_summed kk_summed read yc_turned mixed routed mod_turned row_turned placed",
    "inverse_kept_by_act": "n2_kept n4_kept nt4_kept n8_kept h_kept x_kept ht2_kept tt_kept ar_kept bg_in",
    "chain_kept_by_act": "r_kept u_kept o_kept exps tanhed lora_in",
    "attention_by_act": "zb_kept zb_squared zb_rooted q_kept k_kept v_stored prob pt_kept yb_kept",
    "inputs_by_act": "squared norm_rooted h_done h_part raw_copied kk_rooted cond_ready zg_done mod_row",
    "readout_by_act": "var_rooted yc_kept",
    "gmlp_by_act": "u_gelu v_gelu v_sq v_rooted scored gated row_kept",
    "inverse_by_dve": "nt2_kept x2_done x4_done xt_done ht_kept w_done masked bg_kept",
    "chain_by_dve": "sig_done kka kd_half kd_done bonus_a bonus_b bonus_kept operand state_sum state_new v_kept",
    "attention_by_dve": "zb_inv zb_scaled rope_sin rope_cos kr_ctx q_mid kr_made kr_spread q_roped max_raw max_done sum_inv prob_scaled",
    "inputs_by_dve": "norm_rs x_scaled mod_sum mod_step mod_ready raw_clear lora_clear state_clear z_sides z_half z_mixed kk_raw "
                     "kk_squared kk_clamped kk_inv kk_done blocks_clear eps_half eps_set out_ready",
    "readout_by_dve": "ro var_done yc_done v_inv v_normed mix_biased ya_done merged route mask_done",
    "step_by_pool": "staged ar_in x1_done x1b_done w1_done w2_done",
}
SEMAPHORE = {n: g for g, names in SHARED.items() for n in names.split()}


class Signals:

    def __init__(self, ctx, nc, known):
        self.ctx, self.nc, self.known = ctx, nc, known
        self.sems, self.count, self.at = {}, {}, {}

    def sem(self, name):
        name = SEMAPHORE.get(name, name)
        if name not in self.sems:
            self.sems[name] = self.ctx.enter_context(self.nc.semaphore(name))
            self.count[name] = 0
        return self.sems[name]

    def out(self, name, *key, by=1):
        s = self.sem(name)
        shared = SEMAPHORE.get(name, name)
        self.count[shared] += by
        self.at[(name, *key)] = self.count[shared]
        return s, by

    def skip(self, name, n):
        self.sem(name)
        self.count[name] += n

    def got(self, name, *key):
        value = self.known[(name, *key)] if self.known is not None else 1
        return self.sem(name), value

    def base(self, name, *key):
        return self.known[(name, *key)] if self.known is not None else 1


def stream(l, w):
    for j in range(48):
        yield ("mod", l, j), w["mod"][l, j], SLOT
    for i in range(15):
        yield ("zc", l, i), w["zc"][l, i], SLOT
    for i in range(6):
        yield ("zb", l, i), w["zb"][l, i], SLOT
    for i in range(4):
        yield ("uq", l, i), w["uq"][l, i], 768
    yield ("uk", l, 0), w["uk"][l], SLOT
    yield ("uv", l, 0), w["uv"][l], SLOT
    for i in range(4):
        yield ("zu", l, i), w["zu"][l, i], SLOT
    for i in range(4):
        yield ("zv", l, i), w["zv"][l, i], SLOT
    for j in range(KT):
        for g in range(3):
            yield ("gate", l, j, g), w["gate"][l, g * KT + j], SLOT
        yield ("up", l, j, 0), w["up"][l, j, :, 0:1024], SLOT
        yield ("up", l, j, 1), w["up"][l, j, :, 1024:1536], 512
    for j in range(KT):
        yield ("wo", l, j), w["wo"][l, j], SLOT


def build(nc, w, out, known):
    with ExitStack() as ctx:
        def sb(name, shape):
            return ctx.enter_context(nc.sbuf_tensor(name, shape, F32))

        sg = Signals(ctx, nc, known)
        OUT, GOT = sg.out, sg.got

        x = sb("x", [P, KT, TOK])
        h = sb("h", [P, KT, TOK])
        y = sb("y", [P, 12, TOK])
        ring = sb("ring", [P, RING, SLOT])
        con = sb("con", [P, NCONST, P])
        small = sb("small", [P, 150])
        vec = sb("vec", [P, NVEC])
        rep = sb("rep", [P, 4, CW])
        lora = sb("lora", [P, 3, CW])
        misc = sb("misc", [P, 2, CW])
        bias2 = misc[0:2, :, :]
        cs = misc[:, 0, :].rearrange("p (a t) -> p a t", a=2)
        bs = sb("bs", [P, 4, P])
        ws = sb("ws", [P, 4, P])
        rw = sb("rw", [P, KT, NE])
        rb = sb("rb", [P, NE])
        cc = sb("cc", [P, KT, 2])
        ca = sb("ca", [P, KT, 2])
        mod = sb("mod", [P, 48, 2])
        gain = sb("gain", [P, 2, KT, 2])
        mu2 = sb("mu2", [P, 2, 15])
        eps = sb("eps", [P, 2])
        st = sb("st", [P, 64])
        rt = sb("rt", [P, 512])
        arena = sb("arena", [P, 24640])
        passes = ctx.enter_context(nc.sbuf_tensor("passes", [P, 1], mybir.dt.int32))
        ps = ctx.enter_context(nc.psum_tensor("ps", [P, 8, 512], F32))

        def C(i):
            return con[:, i, :]

        def view(at, *dims):
            n = int(np.prod(dims))
            a = arena[:, at:at + n]
            if len(dims) == 2:
                return a.rearrange("p (a b) -> p a b", b=dims[1])
            if len(dims) == 3:
                return a.rearrange("p (a b c) -> p a b c", b=dims[1], c=dims[2])
            return a

        sq = view(0, 8, 512)
        zc = view(0, 19, 512)
        osb = view(9728, STEPS, 520)
        state = view(13888, HEADS, HD)
        MB = 14400

        class Unit:

            def __init__(self, s):
                def mat(i, n=1):
                    return view(MB + (20 * s + i) * HU * P, n * HU, P)
                self.m = [mat(i) for i in range(4)]
                self.mb, self.mg, self.ma, self.mr = self.m
                self.ar = view(MB + (20 * s + 4) * HU * P, HU, 2 * P)
                self.bg = mat(6, 2)
                self.b, self.g = mat(6), mat(7)
                self.ntb, self.nt, self.bt = mat(8, 2), mat(8), mat(9)
                self.ng, self.n, self.go = mat(10, 2), mat(10), mat(11)
                self.q, self.qb, self.qg = mat(12, 2), mat(12), mat(13)
                self.n4, self.nt4, self.n8, self.xt, self.x, self.x1 = (mat(i) for i in range(14, 20))
                self.bank = 4 * s
                self.tok = [y[:, i, s * HS * HD:(s + 1) * HS * HD] for i in range(8)]
                self.stage = y[:, 8 + 2 * s:10 + 2 * s, :].rearrange("p a (b c) -> p (a b) c", c=P)
                self.low = [rt[:, (2 * s + q) * P:(2 * s + q + 1) * P] for q in range(2)]
                self.v = self.tok[5].rearrange("p (h v) -> p h v", v=HD)
                self.end = st[:, 4 * s:4 * s + 4]

        units = [Unit(s) for s in range(2)]
        tok = y[:, 0:8, :]
        raw = view(MB, 2, 2, 258)
        shs = view(MB + 1100, 2, 2, 256)
        kks = view(MB + 2200, 2, 512)
        zq = view(0, 5, 512)
        qt = view(2560, HEADS, 512)
        kt_ = view(6656, HEADS, 512)
        vt = view(10752, 4, 512)
        pr = view(12800, 2, 2, 512)
        prt = view(14848, 2, 1024)
        rtmp = view(16896, 2, 2, 256)
        rsq = view(17920, 2, 512)
        ut = view(0, 4, 512)
        vg = view(2048, 4, 512)
        at = view(4096, 4, 512)
        vsq = view(6144, 512)
        mg = view(0, KT, 512)
        sgm = view(4096, 2, 3, 512)
        mt = view(7168, 512)
        w13 = view(0, 2, KT, 1024)
        w2 = view(16384, 2, 4, 1024)
        hb = h[:, :, :].rearrange("p k t -> p (k t)")
        htok = y[:, 0:8, :].rearrange("p (n a) t -> p n (a t)", a=2)
        xg = [hb[:, u * 1024:(u + 1) * 1024] for u in range(2)]
        pk = [hb[:, 2048 + u * 512:2560 + u * 512].rearrange("p (n s) -> p n s", s=CAP) for u in range(2)]
        back = [hb[:, 3072 + u * 512:3584 + u * 512] for u in range(2)]
        het = [y[:, 8 + u, :] for u in range(2)]
        he = [y[:, 10 + u, :] for u in range(2)]
        ye = [rep[:, 2 * u:2 * u + 2, :] for u in range(2)]
        pkw = lora[:, 0, :].rearrange("p (n s) -> p n s", s=CAP)
        sil = [lora[:, 1 + u, :] for u in range(2)]
        slots = bs[:, 0, :]
        wsf = ws[:, :, :].rearrange("p g i -> p (g i)")
        score, sel, pick, first, second, comb, mask, place = \
            (wsf[:, 64 * i:64 * i + 64].rearrange("p (t e) -> p t e", e=NE) for i in range(8))
        x_final = {}

        loads = [q for l in range(DEPTH) for q in stream(l, w)]
        slot_of = {key: i % RING for i, (key, _, _) in enumerate(loads)}

        def t0_of(l):
            return CTX if l == DEPTH - 1 else 0

        def chunk_start(c, d):
            n = CTX // CH
            return CH * (c if d == 0 else c // n * n + n - 1 - c % n)

        def keep0(l, c):
            return l < DEPTH - 1 or c >= STEPS // 2

        def in_turn(make):
            flows = [make(s) for s in range(2)]
            done = False
            while not done:
                for f in flows:
                    done = next(f, True) is True
        def attention_pairs(l):
            return [(s, hh) for s in (range(2) if l < DEPTH - 1 else range(1, 2)) for hh in range(HEADS)]

        block = ctx.enter_context(nc.Block())

        @block.sync
        def _(sp):
            sp.dma_start(x[:, :, :], w["x"]).then_inc(*OUT("x_in", by=16))
            for dst, name in ((con[:, :, :], "con"), (small[:, :], "small"), (cs[64:P, :, :], "cs"), (rw[:, :, :], "rw"),
                              (rb[:, :], "rb"), (cc[:, :, :], "cc")):
                sp.dma_start(dst, w[name]).then_inc(*OUT("const_in", by=16))
            n = 0
            for l in range(DEPTH):
                while n < len(loads) and loads[n][0][1] == l:
                    key, src, size = loads[n]
                    if n >= RING:
                        sp.wait_ge(*GOT("chunk_used", *loads[n - RING][0]))
                    sp.dma_start(ring[:, n % RING, 0:size], src).then_inc(*OUT(f"slot{n % RING}", *key, by=16))
                    n += 1
                    if key == ("mod", l, 5):
                        if l:
                            sp.wait_ge(sg.sem(f"x_added{l - 1}"), x_final[l - 1, "sp"])
                            sp.wait_ge(sg.sem(f"slots_moved{l - 1}"), passes_sp)
                        for dst, name in ((vec[:, :], "vec"), (rep[:, :, :], "rep"), (lora[:, :, :], "lora"),
                                          (bias2[:, :, :], "bias2"), (bs[:, :, :], "bs"), (ws[:, :, :], "ws")):
                            sp.dma_start(dst, w[name][l]).then_inc(*OUT("param_in", l, by=16))
                sp.wait_ge(*GOT(f"x_added{l}", KT - 1))
                sp.wait_ge(*GOT("norm_summed", l, 1))
                sp.wait_ge(*GOT("passes_set", l))
                passes_sp = sp.value_load(passes[0:1, 0:1], min_val=1, max_val=TOK // CAP)
                x_final[l, "sp"] = passes_sp * (NE * KT) + KT
                pairs13 = w["w13"][l].rearrange("(i u) p k n -> i u p k n", u=2)
                pairs2 = w["w2"][l].rearrange("(i u) p k n -> i u p k n", u=2)
                with sp.Fori(0, passes_sp, 1) as p:
                    sp.wait_ge(sg.sem(f"x_added{l}"), p * (NE * KT) + KT)
                    for u in range(2):
                        sp.dma_start(w13[:, u, :, :], pairs13[0, u]).then_inc(sg.sem(f"w13_in{u}{l}"), 16)
                        sp.dma_start(w2[:, u, :, :], pairs2[0, u]).then_inc(sg.sem(f"w2_in{u}{l}"), 16)
                    with sp.Fori(0, NE // 2 - 1, 1) as i:
                        for u in range(2):
                            sp.wait_ge(sg.sem(f"y_done{l}"), p * NE + i * 2 + (u + 1))
                            sp.dma_start(w13[:, u, :, :], pairs13[1:][i, u]).then_inc(sg.sem(f"w13_in{u}{l}"), 16)
                            sp.dma_start(w2[:, u, :, :], pairs2[1:][i, u]).then_inc(sg.sem(f"w2_in{u}{l}"), 16)
            sp.wait_ge(*GOT("out_ready",))
            sp.dma_start(out, h[:, :, 0:LAT]).then_inc(*OUT("out_stored", by=16))
            sp.wait_ge(*GOT("out_stored"))

        @block.tensor
        def _(pe):
            def weights(*key):
                pe.wait_ge(*GOT(f"slot{slot_of[key]}", *key))
                return ring[:, slot_of[key], :]

            def norm(l, which):
                t0 = 0 if l < DEPTH and which == 0 else CTX if l == DEPTH else t0_of(l)
                if which == 1:
                    pe.wait_ge(*GOT(f"x_added{l}", KT - 1))
                for k in range(KT):
                    pe.wait_ge(*GOT("squared", l, which, k))
                    mm = pe.matmul(ps[:, 7, t0:], C(C_ONE), sq[:, k, t0:], start=(k == 0), stop=(k == KT - 1))
                mm.then_inc(*OUT("norm_summed", l, which))

            def full(dst, wt, rhs, n, t0):
                for k in range(n):
                    mm = pe.matmul(dst, wt[:, k * P:(k + 1) * P], rhs[:, k, t0:TOK], start=(k == 0), stop=(k == n - 1))
                return mm

            def modulation(l):
                pe.wait_ge(*GOT("cond_ready"))
                pe.wait_ge(*GOT("const_in"))
                for n in range(12):
                    if n >= 2:
                        pe.wait_ge(*GOT("mod_row", l, n - 2))
                    for q in range(4):
                        wt = weights("mod", l, 4 * n + q)
                        for i in range(2):
                            k = 2 * q + i
                            mm = pe.matmul(ps[0:2, 1 + n % 2, :], ca[:, k, :], wt[:, i * 512:(i + 1) * 512],
                                           start=(k == 0), stop=(k == KT - 1))
                        mm.then_inc(*OUT("chunk_used", "mod", l, 4 * n + q))
                for j in range(48):
                    if j % 4 == 0:
                        pe.wait_ge(*GOT("mod_row", l, j // 4))
                    mm = pe.transpose(ps[:, 0, 2 * j:2 * j + 2], y[0:2, j // 4, j % 4 * P:(j % 4 + 1) * P], con[0:2, C_ID, 0:2])
                mm.then_inc(*OUT("mod_turned", l))

            def rwkv_inputs(l):
                pe.wait_ge(*GOT("param_in", l))
                pe.wait_ge(*GOT("h_done", l, 0))
                pe.wait_ge(*GOT("mod_ready", l))
                for i in range(15):
                    wt = weights("zc", l, i)
                    if i >= 2:
                        pe.wait_ge(*GOT("raw_copied", l, i - 2))
                    full(ps[:, i % 2, :], wt, h, KT, 0).then_inc(*OUT("chunk_used", "zc", l, i))
                for f in range(4):
                    pe.wait_ge(*GOT("kk_squared", l, f))
                    if f >= 2:
                        pe.wait_ge(*GOT("kk_rooted", l, f - 2))
                    pe.matmul(ps[:, 2 + f % 2, :], C(C_BONE), kks[:, f % 2, :], start=True, stop=True) \
                        .then_inc(*OUT("kk_summed", l, f))

            def rwkv_flow(l, s):
                for c in range(STEPS):
                    yield from rwkv_step(l, c, s)
                    for u in range(HS // HU):
                        yield from rwkv_unit(l, c, s, u)

            def rwkv_step(l, c, s):
                k = (l, c, s)
                t = units[s]
                A, B, C_, D_ = (t.bank + i for i in range(4))
                pe.wait_ge(*GOT("staged", *k, 1))
                if c:
                    pe.wait_ge(*GOT("state_new", l, c - 1, s, 1))
                    if keep0(l, c - 1):
                        pe.wait_ge(*GOT("o_kept", l, c - 1, s, 1))
                else:
                    pe.wait_ge(*GOT("kk_done", l, 3))
                for q in range(4):
                    for f in range(2):
                        a = q % 2 * 256 + f * P
                        mm = pe.transpose(ps[:, A + q // 2, a:a + P], t.stage[:, 2 * q + f, :], C(C_ID))
                mm.then_inc(*OUT("tokens_turned", *k))
                pe.wait_ge(*GOT("lora_in", *k, 1))
                own = slice(s * 256, (s + 1) * 256)
                for q in range(2):
                    o = ps[:, C_, q * 256:(q + 1) * 256]
                    pe.matmul(o, t.low[q], lora[:, q, own], start=True, stop=False)
                    mm = pe.matmul(o, small[0:2, 2:2 + P], bias2[:, q, own], start=False, stop=True)
                mm.then_inc(*OUT("logits", *k))
                yield
                pe.wait_ge(*GOT("sig_done", *k))
                pe.matmul(ps[:, D_, 0:256], C(C_MI), t.tok[0], start=True, stop=True)
                pe.matmul(ps[:, D_, 256:512], C(C_MS), t.tok[0], start=True, stop=True)
                for hh in range(HS):
                    for d in range(2):
                        mm = pe.matmul(ps[d * HD:(d + 1) * HD, C_, hh:hh + 1], t.tok[0][:, hh * HD:(hh + 1) * HD],
                                       small[:, d:d + 1], start=True, stop=True)
                mm.then_inc(*OUT("cums", *k))
                yield

            def rwkv_unit(l, c, s, u):
                k = (l, c, s, u)
                t = units[s]
                A, B, C_, D_ = (t.bank + i for i in range(4))
                h0 = s * HS + u * HU

                def each(bank, lhs, rhs, name):
                    for i in range(HU):
                        mm = pe.matmul(ps[:, bank, i * P:(i + 1) * P], lhs[:, i, :], rhs[:, i, :], start=True, stop=True)
                    mm.then_inc(*OUT(name, *k))

                pe.wait_ge(*GOT("ar_in", *k, 1, 1))
                pe.wait_ge(*GOT("bg_in", *k, 1, 1))
                if u == 0:
                    pe.wait_ge(*GOT("operand", l, c, s, 3))
                    pe.wait_ge(*GOT("exps", l, c, s, 3))
                else:
                    pe.wait_ge(*GOT("state_new", l, c, s, 0))
                    if keep0(l, c):
                        pe.wait_ge(*GOT("o_kept", l, c, s, 0))
                for i in range(HU):
                    pe.transpose(ps[:, A, 2 * i * P:(2 * i + 1) * P], t.ma[:, i, :], C(C_ID))
                    pe.transpose(ps[:, A, (2 * i + 1) * P:(2 * i + 2) * P], t.mr[:, i, :], C(C_ID))
                    pe.transpose(ps[:, B, i * P:(i + 1) * P], t.mb[:, i, :], C(C_ID))
                    mm = pe.transpose(ps[:, B, (2 + i) * P:(3 + i) * P], t.mg[:, i, :], C(C_ID))
                mm.then_inc(*OUT("turned", *k))
                yield
                pe.wait_ge(*GOT("ar_kept", *k))
                pe.wait_ge(*GOT("bg_kept", *k))
                for i in range(HU):
                    pe.matmul(ps[:, A, i * P:(i + 1) * P], t.ar[:, i, 0:P], t.b[:, i, :], start=True, stop=True)
                for q, src in enumerate((t.b, t.g)):
                    for i in range(HU):
                        mm = pe.matmul(ps[:, C_ + q, i * 256:i * 256 + 256], src[:, i, :], t.ar[:, i, :], start=True, stop=True)
                mm.then_inc(*OUT("gram", *k))
                yield
                pe.wait_ge(*GOT("masked", *k, 1))
                each(B, t.n, t.nt, "p_nt2")
                each(A, t.nt, t.n, "p_n2")
                yield
                pe.wait_ge(*GOT("nt2_kept", *k))
                pe.wait_ge(*GOT("n2_kept", *k))
                each(A, t.b, t.g, "p_n4")
                each(B, t.g, t.b, "p_nt4")
                pe.wait_ge(*GOT("masked", *k, 2))
                each(C_, t.g, t.nt, "p_nt3")
                yield
                pe.wait_ge(*GOT("nt4_kept", *k))
                each(D_, t.nt4, t.n4, "p_n8")
                pe.wait_ge(*GOT("x2_done", *k))
                each(C_, t.n4, t.ma, "p_x4")
                yield
                pe.wait_ge(*GOT("n8_kept", *k))
                pe.wait_ge(*GOT("x4_done", *k))
                each(B, t.n8, t.mr, "p_x8")
                yield
                pe.wait_ge(*GOT("xt_done", *k))
                each(C_, t.go, t.xt, "p_ht")
                each(A, t.xt, t.go, "p_h")
                for i in range(HU):
                    mm = pe.transpose(ps[:, D_, i * P:(i + 1) * P], t.xt[:, i, :], C(C_ID))
                mm.then_inc(*OUT("p_x", *k))
                yield
                pe.wait_ge(*GOT("h_kept", *k))
                pe.wait_ge(*GOT("ht_kept", *k))
                each(A, t.n, t.nt, "p_ht2")
                yield
                pe.wait_ge(*GOT("ht2_kept", *k))
                each(C_, t.n, t.n4, "p_ht3")
                if c == 0:
                    pe.wait_ge(*GOT("state_clear", l))
                for i in range(HU):
                    o = ps[:, A, i * HD:(i + 1) * HD]
                    pe.matmul(o, t.ar[:, i, 0:P], state[:, h0 + i, :], start=True, stop=False)
                    mm = pe.matmul(o, t.bt[:, i, :], t.v[:, u * HU + i, :], start=False, stop=True)
                mm.then_inc(*OUT("p_r", *k))
                yield
                pe.wait_ge(*GOT("w_done", *k))
                pe.wait_ge(*GOT("x_kept", *k))
                each(D_, t.x, t.nt4, "p_tt")
                yield
                pe.wait_ge(*GOT("tt_kept", *k))
                pe.wait_ge(*GOT("r_kept", *k))
                for i in range(HU):
                    mm = pe.matmul(ps[:, D_, i * HD:(i + 1) * HD], t.n8[:, i, :], t.nt[:, i, 0:HD], start=True, stop=True)
                mm.then_inc(*OUT("p_u", *k))
                yield
                pe.wait_ge(*GOT("u_kept", *k))
                if keep0(l, c):
                    for i in range(HU):
                        o = ps[:, B, i * HD:(i + 1) * HD]
                        pe.matmul(o, t.ar[:, i, P:2 * P], state[:, h0 + i, :], start=True, stop=False)
                        pe.matmul(o, t.qb[:, i, :], t.nt[:, i, HD:P], start=False, stop=False)
                        mm = pe.matmul(o, t.qg[:, i, :], t.v[:, u * HU + i, :], start=False, stop=True)
                    mm.then_inc(*OUT("p_o", *k))
                for i in range(HU):
                    o = ps[:, C_, i * HD:(i + 1) * HD]
                    pe.matmul(o, t.mb[:, i, :], t.nt[:, i, HD:P], start=True, stop=False)
                    mm = pe.matmul(o, t.mg[:, i, :], t.v[:, u * HU + i, :], start=False, stop=True)
                mm.then_inc(*OUT("p_s", *k))
                yield

            def rwkv_readout(l):
                pe.wait_ge(*GOT("zg_done", l))
                for i in range(t0_of(l) // P, NT):
                    n = CTX // CH
                    if i > t0_of(l) // P:
                        pe.wait_ge(*GOT("yc_kept", l, i - 1))
                    else:
                        for s in range(2):
                            pe.wait_ge(*GOT("o_kept", l, STEPS - 1, s, 1))
                            pe.wait_ge(*GOT("state_new", l, STEPS - 1, s, 1))
                    parts = []
                    for half in range(2):
                        j = 2 * i + half
                        parts.append((0, half, j))
                        parts.append((1, half, j // n * n + n - 1 - j % n))
                    for bank, a, b in ((0, 0, CW), (1, CW, CW + HEADS)):
                        for q, (d, half, c) in enumerate(parts):
                            pe.matmul(ps[:, bank, 0:b - a], C(C_S00 + 2 * d + half), osb[:, c, a:b],
                                      start=(q == 0), stop=(q == 3))
                    for f in range(4):
                        pe.transpose(ps[:, 2, f * P:(f + 1) * P], zc[:, ZV + f, i * P:(i + 1) * P], C(C_ID))
                    pe.matmul(ps[:, 3, :], zc[:, ZG, i * P:(i + 1) * P], lora[:, 2, :], start=True, stop=True) \
                        .then_inc(*OUT("read", l, i))
                    pe.wait_ge(*GOT("yc_done", l, i))
                    for f in range(4):
                        mm = pe.transpose(ps[:, 4, f * P:(f + 1) * P], tok[:, 0, f * P:(f + 1) * P], C(C_ID))
                    mm.then_inc(*OUT("yc_turned", l, i))

            def attention_inputs(l):
                t0 = t0_of(l)
                for i in range(6):
                    wt = weights("zb", l, i)
                    if i >= 2:
                        pe.wait_ge(*GOT("zb_kept", l, i - 2))
                    elif i == 0:
                        pe.wait_ge(*GOT("yc_kept", l, NT - 1))
                    full(ps[:, i % 2, :], wt, h, KT, 0).then_inc(*OUT("chunk_used", "zb", l, i))
                for i in range(5):
                    pe.wait_ge(*GOT("zb_squared", l, i))
                    mm = pe.matmul(ps[:, 2 if i < 3 else 3, :], C(C_ONE), rsq[:, i % 2, :],
                                   start=(i in (0, 3)), stop=(i in (2, 4)))
                    mm.then_inc(*OUT("zb_summed", l, i))
                for i in range(5):
                    pe.wait_ge(*GOT("zb_scaled", l, i))
                n = 0
                for i in range(4):
                    wt = weights("uq", l, i)
                    for j in range(2):
                        hh = 2 * i + j
                        bank = 4 + hh % 2
                        if hh >= 2:
                            pe.wait_ge(*GOT("q_kept", l, hh - 2))
                            pe.wait_ge(*GOT("q_roped", l, hh - 2))
                        for k in range(3):
                            mm = pe.matmul(ps[:, bank, t0:TOK], wt[:, (j * 3 + k) * P:(j * 3 + k + 1) * P], zq[:, k, t0:TOK],
                                           start=(k == 0), stop=(k == 2))
                        mm.then_inc(*(OUT("q_made", l, hh) if j == 0 else OUT("chunk_used", "uq", l, i)))
                wt = weights("uk", l, 0)
                for hh in range(HEADS):
                    if hh >= 2:
                        pe.wait_ge(*GOT("k_kept", l, hh - 2))
                    else:
                        pe.wait_ge(*GOT("q_kept", l, 6 + hh))
                        pe.wait_ge(*GOT("kr_spread", l))
                    for k in range(2):
                        mm = pe.matmul(ps[0:HD, 6 + hh % 2, :], wt[:, (hh * 2 + k) * HD:(hh * 2 + k + 1) * HD], zq[:, 3 + k, :],
                                       start=(k == 0), stop=(k == 1))
                    mm.then_inc(*(OUT("k_made", l, hh) if hh < HEADS - 1 else OUT("chunk_used", "uk", l, 0)))
                wt = weights("uv", l, 0)
                pe.wait_ge(*GOT("kr_spread", l))
                pe.wait_ge(*GOT("zb_rooted", l, 1))
                for i in range(NT):
                    for k in range(2):
                        mm = pe.matmul(ps[:, i, :], zq[:, 3 + k, i * P:(i + 1) * P], wt[:, k * 512:(k + 1) * 512],
                                       start=(k == 0), stop=(k == 1))
                    mm.then_inc(*(OUT("v_made", l, i) if i < NT - 1 else OUT("chunk_used", "uv", l, 0)))

            def attention(l):
                pairs = attention_pairs(l)

                def scores(n):
                    s, hh = pairs[n]
                    nk = 4 if s else 2
                    if n >= 2:
                        pe.wait_ge(*GOT("prob", l, n - 2, 1))
                    elif n == 0:
                        pe.wait_ge(*GOT("v_stored", l, NT - 1))
                        pe.wait_ge(*GOT("k_kept", l, HEADS - 1))
                        pe.wait_ge(*GOT("q_kept", l, HEADS - 1))
                        pe.wait_ge(*GOT("q_roped", l, HEADS - 1))
                    for q in range(2):
                        tt = s * CTX + q * P
                        mm = pe.matmul(ps[:, n % 2 * 2 + q, 0:nk * P], qt[0:QK, hh, tt:tt + P], kt_[0:QK, hh, 0:nk * P],
                                       start=True, stop=True)
                    mm.then_inc(*OUT("scores", l, n))

                scores(0)
                for n, (s, hh) in enumerate(pairs):
                    nk = 4 if s else 2
                    if n + 1 < len(pairs):
                        scores(n + 1)
                    pe.wait_ge(*GOT("prob_scaled", l, n, 1))
                    if n >= 1:
                        pe.wait_ge(*GOT("pt_kept", l, n - 1))
                    for kk in range(nk):
                        for q in range(2):
                            mm = pe.transpose(ps[:, 4 + kk // 2, kk % 2 * 256 + q * P:kk % 2 * 256 + (q + 1) * P],
                                              pr[:, n % 2, q, kk * P:(kk + 1) * P], C(C_ID))
                    mm.then_inc(*OUT("prob_turned", l, n))
                    pe.wait_ge(*GOT("pt_kept", l, n))
                    if n >= 2:
                        pe.wait_ge(*GOT("yb_kept", l, n - 2))
                    for kk in range(nk):
                        mm = pe.matmul(ps[hh % 2 * HD:hh % 2 * HD + HD, 6 + n % 2, 0:256], vt[:, kk, hh * VD:(hh + 1) * VD],
                                       prt[:, n % 2, kk * 256:(kk + 1) * 256], start=(kk == 0), stop=(kk == nk - 1))
                    mm.then_inc(*OUT("attended", l, n))

            def gmlp(l):
                t0 = t0_of(l)
                pe.wait_ge(*GOT("yb_kept", l, len(attention_pairs(l)) - 1))
                pe.wait_ge(*GOT("yb_kept", l, len(attention_pairs(l)) - 2))
                for i in range(4):
                    wt = weights("zu", l, i)
                    if i >= 2:
                        pe.wait_ge(*GOT("u_gelu", l, i - 2))
                    full(ps[:, 4 + i % 2, t0:TOK], wt, h, KT, t0).then_inc(*OUT("chunk_used", "zu", l, i))
                for i in range(4):
                    wt = weights("zv", l, i)
                    for k in range(2):
                        for t in range(t0 // P, NT):
                            mm = pe.matmul(ps[:, t, :], h[:, 2 * i + k, t * P:(t + 1) * P], wt[:, k * 512:(k + 1) * 512],
                                           start=(i == 0 and k == 0), stop=(i == 3 and k == 1))
                    mm.then_inc(*OUT("chunk_used", "zv", l, i))
                pe.wait_ge(*GOT("v_normed", l, NT - 1))
                pe.wait_ge(*GOT("u_gelu", l, 3))
                for g in range(4):
                    for t in range(t0 // P, NT):
                        mm = pe.matmul(ps[:, 4 + g, t * P:(t + 1) * P], vg[:, t, g * P:(g + 1) * P], ws[:, g, :],
                                       start=True, stop=True)
                    mm.then_inc(*OUT("mixed", l, g))

            def merge(l):
                t0 = t0_of(l)
                pe.wait_ge(*GOT("ya_done", l, 3))
                pe.wait_ge(*GOT("v_normed", l, NT - 1))
                for j in range(KT):
                    for g in range(3):
                        wt = weights("gate", l, j, g)
                        if j:
                            pe.wait_ge(*GOT("gated", l, j - 1, g))
                        full(ps[:, g, t0:TOK], wt, h, KT, t0).then_inc(*OUT("chunk_used", "gate", l, j, g))
                    for g in range(3):
                        if g != 1:
                            wt = weights("up", l, j, g // 2)
                        at_ = 512 * g if g < 2 else 0
                        if j:
                            pe.wait_ge(*GOT("merged", l, j - 1, 4))
                        for k in range(4):
                            mm = pe.matmul(ps[:, 3 + g, t0:TOK], wt[:, at_ + k * P:at_ + (k + 1) * P], y[:, 4 * g + k, t0:TOK],
                                           start=(k == 0), stop=(k == 3))
                        if g:
                            mm.then_inc(*OUT("chunk_used", "up", l, j, g // 2))
                pe.wait_ge(*GOT("merged", l, KT - 1, 4))
                for j in range(KT):
                    wt = weights("wo", l, j)
                    if j >= 2:
                        pe.wait_ge(*GOT(f"x_added{l}", j - 2))
                    full(ps[:, 6 + j % 2, t0:TOK], wt, mg, KT, t0).then_inc(*OUT("chunk_used", "wo", l, j))

            def router(l):
                t0 = t0_of(l)
                pe.wait_ge(*GOT("h_done", l, 1))
                for t in range(t0 // P, NT):
                    for k in range(KT):
                        mm = pe.matmul(ps[:, 6, t * NE:(t + 1) * NE], h[:, k, t * P:(t + 1) * P], rw[:, k, :],
                                       start=(k == 0), stop=(k == KT - 1))
                mm.then_inc(*OUT("routed", l))
                for t in range(t0 // P, NT):
                    if t >= t0 // P + 2:
                        pe.wait_ge(*GOT("row_kept", l, t - 2))
                    for f in range(KT):
                        b = t % 2 * 2 + f // 4
                        mm = pe.transpose(ps[:, b, f % 4 * P:(f % 4 + 1) * P], h[:, f, t * P:(t + 1) * P], C(C_ID))
                    mm.then_inc(*OUT("row_turned", l, t))
                pe.wait_ge(*GOT("mask_done", l))
                a = t0 // P
                for t in range(a, NT):
                    for i in range(a, t + 1):
                        pe.matmul(ps[:, 6, 64 + t * NE:64 + (t + 1) * NE], C(C_ONE if i < t else C_TRI), mask[:, i, :],
                                  start=(i == a), stop=(i == t))
                for i in range(a, NT):
                    mm = pe.matmul(ps[:, 6, 128:128 + NE], C(C_ONE), mask[:, i, :], start=(i == a), stop=(i == NT - 1))
                mm.then_inc(*OUT("placed", l))

            def experts(l):
                t0 = t0_of(l)
                tiles = range(t0 // P, NT)

                def S(name):
                    return sg.sem(f"{name}{l}")
                pe.wait_ge(*GOT("passes_set", l))
                pe.wait_ge(*GOT("row_kept", l, NT - 1))
                n_passes = pe.value_load(passes[0:1, 0:1], min_val=1, max_val=TOK // CAP)
                with pe.Fori(0, n_passes, 1) as p:
                    with pe.Fori(0, NE // 2, 1) as j:
                        n = pe.snap(p * NE + j * 2)
                        for u in range(2):
                            pe.wait_ge(S("picks"), n + (u + 1))
                            pe.wait_ge(S("xg_kept"), n + u)
                            for f in range(KT):
                                for t in tiles:
                                    mm = pe.matmul(ps[:, f // 4, f % 4 * P:(f % 4 + 1) * P], htok[:, t, f * P:(f + 1) * P],
                                                   pk[u][:, t, :], start=(t == tiles[0]), stop=(t == NT - 1))
                            mm.then_inc(S("gathered"), 1)
                            pe.wait_ge(S("weighted"), n + (u + 1))
                            pe.wait_ge(S("back_kept"), n + u)
                            for t in tiles:
                                mm = pe.transpose(ps[:, 7, t * P:(t + 1) * P], pkw[:, t, :], C(C_ID))
                            mm.then_inc(S("turned_back"), 1)
                        for u in range(2):
                            pe.wait_ge(S("xg_kept"), n + (u + 1))
                            pe.wait_ge(S(f"w13_in{u}"), p * (8 * NE) + j * 16 + 16)
                            pe.wait_ge(S("he_done"), n + u)
                            pe.wait_ge(S("ye_kept"), n)
                            for q in range(2):
                                for k in range(KT):
                                    mm = pe.matmul(ps[:, 3 + q, :], xg[u][:, k * P:(k + 1) * P],
                                                   w13[:, u, k, q * 512:(q + 1) * 512], start=(k == 0), stop=(k == KT - 1))
                            mm.then_inc(S("h13_done"), 1)
                        for u in range(2):
                            pe.wait_ge(S("he_done"), n + (u + 1))
                            pe.wait_ge(S("het_kept"), n + u)
                            for k in range(4):
                                mm = pe.transpose(ps[:, 2, k * P:(k + 1) * P], he[u][:, k * P:(k + 1) * P], C(C_ID))
                            mm.then_inc(S("he_turned"), 1)
                            pe.wait_ge(S("het_kept"), n + (u + 1))
                            pe.wait_ge(S(f"w2_in{u}"), p * (8 * NE) + j * 16 + 16)
                            if u == 0:
                                pe.wait_ge(S("x_added"), n * KT + KT)
                            for q in range(2):
                                for k in range(4):
                                    mm = pe.matmul(ps[:, (5, 3)[u] + q, :], het[u][:, k * P:(k + 1) * P],
                                                   w2[:, u, k, q * 512:(q + 1) * 512], start=(k == 0), stop=(k == 3))
                            mm.then_inc(S("y_done"), 1)
                        for u in range(2):
                            pe.wait_ge(S("ye_kept"), n + (u + 1))
                            pe.wait_ge(S("back_kept"), n + (u + 1))
                            for d in range(KT):
                                if u or d >= 2:
                                    pe.wait_ge(S("x_added"), n * KT + (KT + KT * u + d - 1))
                                pe.matmul(ps[:, 5 + d % 2, t0:TOK], ye[u][:, d // 4, d % 4 * P:(d % 4 + 1) * P],
                                          back[u][:, t0:TOK], start=True, stop=True).then_inc(S("scattered"), 1)

            for l in range(DEPTH):
                modulation(l)
                norm(l, 0)
                rwkv_inputs(l)
                in_turn(lambda s: rwkv_flow(l, s))
                rwkv_readout(l)
                attention_inputs(l)
                attention(l)
                gmlp(l)
                merge(l)
                norm(l, 1)
                router(l)
                experts(l)
            norm(DEPTH, 0)

        @block.scalar
        def _(act):
            def A_(o, i, f, **kw):
                return act.activation(o, i, f, **kw)

            def norm(l, which):
                t0 = 0 if l < DEPTH and which == 0 else CTX if l == DEPTH else t0_of(l)
                for k in range(KT):
                    if which == 1:
                        act.wait_ge(*GOT(f"x_added{l}", k))
                        if k == 0:
                            act.wait_ge(*GOT("chunk_used", "wo", l, KT - 1))
                    elif l:
                        act.wait_ge(sg.sem(f"x_added{l - 1}"), x_final[l - 1, "act"])
                    else:
                        act.wait_ge(*GOT("x_in"))
                    A_(sq[:, k, t0:], x[:, k, t0:], ACT.Square).then_inc(*OUT("squared", l, which, k))
                act.wait_ge(*GOT("norm_summed", l, which))
                act.wait_ge(*GOT("eps_set"))
                A_(rt[:, t0:], ps[:, 7, t0:], ACT.Sqrt, bias=eps[:, 0:1], scale=1.0 / D).then_inc(*OUT("norm_rooted", l, which))
                if l == DEPTH:
                    return
                for k in range(KT):
                    act.wait_ge(*GOT("x_scaled", l, which, k))
                    for s in range(t0 // CTX, 2):
                        v = h[:, k, s * CTX:(s + 1) * CTX]
                        ins = A_(v, v, ACT.Identity, scale=gain[:, which, k, s:s + 1],
                                bias=mod[:, 24 * which + k, s:s + 1])
                        ins.then_inc(*(OUT("h_done", l, which) if k == KT - 1 and s == 1 else OUT("h_part", l, which, k, s)))

            def copy(o, i):
                return A_(o, i, ACT.Copy)

            def rwkv_inputs(l):
                for i in range(15):
                    act.wait_ge(*GOT("chunk_used", "zc", l, i))
                    if i == 0:
                        act.wait_ge(*GOT("raw_clear", l))
                    if i >= 2:
                        act.wait_ge(*GOT("z_mixed", l, i - 2))
                    copy(raw[:, i % 2, :, 1:257], ps[:, i % 2, :].rearrange("p (s t) -> p s t", s=2)) \
                        .then_inc(*OUT("raw_copied", l, i))
                for f in range(4):
                    act.wait_ge(*GOT("kk_clamped", l, f))
                    A_(kks[:, f % 2, :], kks[:, f % 2, :], ACT.Sqrt).then_inc(*OUT("kk_rooted", l, f))

            def rwkv_flow(l, s):
                for c in range(STEPS):
                    yield from rwkv_step(l, c, s)
                    for u in range(HS // HU):
                        yield from rwkv_unit(l, c, s, u)

            def rwkv_step(l, c, s):
                k = (l, c, s)
                t = units[s]
                A, B, C_, D_ = (t.bank + i for i in range(4))
                if c == 0:
                    act.wait_ge(*GOT("lora_clear", l))
                    act.wait_ge(*GOT("z_mixed", l, 13))
                else:
                    act.wait_ge(*GOT("logits", l, c - 1, s))
                for q in range(2):
                    for d in range(2):
                        a = chunk_start(c, d)
                        r = slice(d * 64, d * 64 + 64)
                        A_(t.low[q][r, d * 64:d * 64 + 64], zc[r, ZW + q, a:a + 64], ACT.Tanh if q == 0 else ACT.Copy) \
                            .then_inc(*OUT("lora_in", *k, q))
                if c:
                    act.wait_ge(*GOT("bonus_kept", l, c - 1, s))
                act.wait_ge(*GOT("logits", *k))
                for q in range(2):
                    A_(t.tok[q], ps[:, C_, q * 256:(q + 1) * 256], ACT.Tanh, scale=0.5).then_inc(*OUT("tanhed", *k, q))
                yield
                act.wait_ge(*GOT("cums", *k))
                if c:
                    act.wait_ge(*GOT("ar_in", l, c - 1, s, 1, 1, 1))
                    act.wait_ge(*GOT("bg_in", l, c - 1, s, 1, 1, 1))
                    act.wait_ge(*GOT("state_new", l, c - 1, s, 1))
                A_(t.tok[4], ps[:, D_, 0:256], ACT.Exp, scale=DECAY).then_inc(*OUT("exps", *k, 0))
                A_(t.tok[3], ps[:, D_, 256:512], ACT.Exp, scale=-DECAY).then_inc(*OUT("exps", *k, 1))
                A_(t.tok[2], ps[:, D_, 0:256], ACT.Exp, scale=-DECAY).then_inc(*OUT("exps", *k, 2))
                A_(t.end, ps[:, C_, 0:HS], ACT.Exp, scale=-DECAY).then_inc(*OUT("exps", *k, 3))
                yield

            def rwkv_unit(l, c, s, u):
                k = (l, c, s, u)
                t = units[s]
                A, B, C_, D_ = (t.bank + i for i in range(4))
                prev = (l, c, s, 0) if u else (l, c - 1, s, 1)

                def keep(name, src, bank, dst):
                    act.wait_ge(*GOT(src, *k))
                    copy(dst, ps[:, bank, 0:HU * P].rearrange("p (h t) -> p h t", t=P)).then_inc(*OUT(name, *k))
                if c or u:
                    act.wait_ge(*GOT("p_s", *prev))
                for q, (m, i) in enumerate(((t.mb, 6), (t.mg, 7))):
                    act.wait_ge(*GOT("operand", l, c, s, q))
                    for d in range(2):
                        r = slice(d * CH, (d + 1) * CH)
                        copy(m[r, :, d * HD:(d + 1) * HD],
                             t.tok[i][r, u * P:(u + 1) * P].rearrange("p (h v) -> p h v", v=HD)).then_inc(*OUT("bg_in", *k, q, d))
                act.wait_ge(*GOT("turned", *k))
                copy(t.ar, ps[:, A, :].rearrange("p (h t) -> p h t", t=2 * P)).then_inc(*OUT("ar_kept", *k))
                yield
                yield
                keep("n2_kept", "p_n2", A, t.g)
                yield
                keep("n4_kept", "p_n4", A, t.n4)
                keep("nt4_kept", "p_nt4", B, t.nt4)
                yield
                keep("n8_kept", "p_n8", D_, t.n8)
                yield
                yield
                keep("h_kept", "p_h", A, t.n)
                keep("x_kept", "p_x", D_, t.x)
                yield
                keep("ht2_kept", "p_ht2", A, t.n4)
                yield
                act.wait_ge(*GOT("p_r", *k))
                act.wait_ge(*GOT("w_done", *k))
                A_(t.nt[:, :, 0:HD], ps[:, A, 0:HU * HD].rearrange("p (h v) -> p h v", v=HD), ACT.Copy, scale=-1.0) \
                    .then_inc(*OUT("r_kept", *k))
                yield
                keep("tt_kept", "p_tt", D_, t.n8)
                yield
                act.wait_ge(*GOT("p_u", *k))
                copy(t.nt[:, :, HD:P], ps[:, D_, 0:HU * HD].rearrange("p (h v) -> p h v", v=HD)).then_inc(*OUT("u_kept", *k))
                yield
                if keep0(l, c):
                    act.wait_ge(*GOT("p_o", *k))
                    a = (s * HS + u * HU) * HD
                    copy(osb[:, c, a:a + HU * HD], ps[:, B, 0:HU * HD]).then_inc(*OUT("o_kept", *k))
                yield

            def rwkv_readout(l):
                A_(zc[:, ZG, :], zc[:, ZG, :], ACT.Sigmoid).then_inc(*OUT("zg_done", l))
                for i in range(t0_of(l) // P, NT):
                    act.wait_ge(*GOT("var_done", l, i))
                    A_(st[:, 16:24], st[:, 16:24], ACT.Sqrt, bias=eps[:, 1:2], scale=1.0 / HD).then_inc(*OUT("var_rooted", l, i))
                    act.wait_ge(*GOT("yc_turned", l, i))
                    copy(y[:, 8:12, i * P:(i + 1) * P], ps[:, 4, :].rearrange("p (f t) -> p f t", t=P)) \
                        .then_inc(*OUT("yc_kept", l, i))

            def attention_inputs(l):
                t0 = t0_of(l)
                for i in range(5):
                    act.wait_ge(*GOT("chunk_used", "zb", l, i))
                    copy(zq[:, i, :], ps[:, i % 2, :]).then_inc(*OUT("zb_kept", l, i))
                for i in range(5):
                    act.wait_ge(*GOT("zb_kept", l, i))
                    if i >= 2:
                        act.wait_ge(*GOT("zb_summed", l, i - 2))
                    A_(rsq[:, i % 2, :], zq[:, i, :], ACT.Square).then_inc(*OUT("zb_squared", l, i))
                for i, (bank, n) in enumerate(((2, QL), (3, KVL))):
                    act.wait_ge(*GOT("zb_summed", l, 2 if i == 0 else 4))
                    A_(pr[:, 0, i, :], ps[:, bank, :], ACT.Sqrt, bias=eps[:, 0:1], scale=1.0 / n).then_inc(*OUT("zb_rooted", l, i))
                for hh in range(HEADS):
                    act.wait_ge(*(GOT("q_made", l, hh) if hh % 2 == 0 else GOT("chunk_used", "uq", l, hh // 2)))
                    copy(qt[0:64, hh, t0:], ps[0:64, 4 + hh % 2, t0:]).then_inc(*OUT("q_kept", l, hh))
                for hh in range(HEADS):
                    act.wait_ge(*(GOT("k_made", l, hh) if hh < HEADS - 1 else GOT("chunk_used", "uk", l, 0)))
                    copy(kt_[0:64, hh, :], ps[0:64, 6 + hh % 2, :]).then_inc(*OUT("k_kept", l, hh))
                for i in range(NT):
                    act.wait_ge(*(GOT("v_made", l, i) if i < NT - 1 else GOT("chunk_used", "uv", l, 0)))
                    copy(vt[:, i, :], ps[:, i, :]).then_inc(*OUT("v_stored", l, i))

            def attention(l):
                pairs = attention_pairs(l)

                def probabilities(n):
                    s, hh = pairs[n]
                    nk = 4 if s else 2
                    act.wait_ge(*GOT("max_done", l, n))
                    if n >= 2:
                        act.wait_ge(*GOT("prob_turned", l, n - 2))
                    else:
                        act.wait_ge(*GOT("zb_scaled", l, 4))
                    for q in range(2):
                        A_(pr[:, n % 2, q, 0:nk * P], ps[:, n % 2 * 2 + q, 0:nk * P], ACT.Exp, scale=MLA_SCALE,
                          bias=st[:, 32 + n % 2 * 8 + q:33 + n % 2 * 8 + q],
                          accum_out=st[:, 34 + n % 2 * 8 + q:35 + n % 2 * 8 + q]).then_inc(*OUT("prob", l, n, q))

                def keep(n):
                    s, hh = pairs[n]
                    nk = 4 if s else 2
                    act.wait_ge(*GOT("prob_turned", l, n))
                    if n >= 2:
                        act.wait_ge(*GOT("attended", l, n - 2))
                    copy(prt[:, n % 2, 0:nk * 256].rearrange("p (b k) -> p b k", k=512),
                         ps[:, 4:4 + nk // 2, :]).then_inc(*OUT("pt_kept", l, n))
                    act.wait_ge(*GOT("attended", l, n))
                    r = slice(hh % 2 * HD, hh % 2 * HD + HD)
                    copy(y[r, 4 + hh // 2, s * CTX:(s + 1) * CTX], ps[r, 6 + n % 2, 0:256]).then_inc(*OUT("yb_kept", l, n))

                probabilities(0)
                for n in range(len(pairs)):
                    if n + 1 < len(pairs):
                        probabilities(n + 1)
                    keep(n)

            def gmlp(l):
                t0 = t0_of(l)
                for i in range(4):
                    act.wait_ge(*GOT("chunk_used", "zu", l, i))
                    A_(ut[:, i, t0:], ps[:, 4 + i % 2, t0:], ACT.Gelu_apprx_tanh).then_inc(*OUT("u_gelu", l, i))
                act.wait_ge(*GOT("chunk_used", "zv", l, 3))
                for t in range(t0 // P, NT):
                    A_(vg[:, t, :], ps[:, t, :], ACT.Gelu_apprx_tanh).then_inc(*OUT("v_gelu", l, t))
                for t in range(t0 // P, NT):
                    act.wait_ge(*GOT("v_gelu", l, t))
                    if t > t0 // P:
                        act.wait_ge(*GOT("v_sq", l, t - 1))
                    A_(vsq, vg[:, t, :], ACT.Square, accum_out=st[:, 48 + t:49 + t]).then_inc(*OUT("v_sq", l, t))
                act.wait_ge(*GOT("v_sq", l, NT - 1))
                A_(st[:, 52 + t0 // P:56], st[:, 48 + t0 // P:52], ACT.Sqrt, bias=eps[:, 0:1], scale=1.0 / CW) \
                    .then_inc(*OUT("v_rooted", l))

            def merge(l):
                t0 = t0_of(l)
                for j in range(KT):
                    for g in range(3):
                        act.wait_ge(*GOT("chunk_used", "gate", l, j, g))
                        if j >= 2:
                            act.wait_ge(*GOT("merged", l, j - 2, 4))
                        elif j == 0 and g == 0:
                            act.wait_ge(*GOT("ya_done", l, 3))
                        A_(sgm[:, j % 2, g, t0:], ps[:, g, t0:], ACT.Sigmoid).then_inc(*OUT("gated", l, j, g))

            def experts(l):
                t0 = t0_of(l)

                def S(name):
                    return sg.sem(f"{name}{l}")
                act.wait_ge(*GOT("routed", l))
                A_(score[:, t0 // P:, :], ps[:, 6, t0 // P * NE:NT * NE].rearrange("p (t e) -> p t e", e=NE), ACT.Sigmoid) \
                    .then_inc(*OUT("scored", l))
                for t in range(t0 // P, NT):
                    act.wait_ge(*GOT("row_turned", l, t))
                    b = t % 2 * 2
                    copy(htok[:, t, :].rearrange("p (b k) -> p b k", b=2), ps[:, b:b + 2, :]).then_inc(*OUT("row_kept", l, t))
                act.wait_ge(*GOT("passes_set", l))
                n_passes = act.value_load(passes[0:1, 0:1], min_val=1, max_val=TOK // CAP)
                x_final[l, "act"] = n_passes * (NE * KT) + KT
                with act.Fori(0, n_passes, 1) as p:
                    with act.Fori(0, NE // 2, 1) as j:
                        n = act.snap(p * NE + j * 2)
                        act.wait_ge(S("scattered"), n * KT)
                        for u in range(2):
                            act.wait_ge(S("gathered"), n + (u + 1))
                            copy(xg[u].rearrange("p (b k) -> p b k", b=2), ps[:, 0:2, :]).then_inc(S("xg_kept"), 1)
                            act.wait_ge(S("turned_back"), n + (u + 1))
                            copy(back[u][:, t0:], ps[:, 7, t0:]).then_inc(S("back_kept"), 1)
                        for u in range(2):
                            act.wait_ge(S("h13_done"), n + (u + 1))
                            A_(sil[u], ps[:, 3, :], ACT.Silu).then_inc(S("silu_done"), 1)
                        for u in range(2):
                            act.wait_ge(S("he_turned"), n + (u + 1))
                            copy(het[u], ps[:, 2, :]).then_inc(S("het_kept"), 1)
                            act.wait_ge(S("y_done"), n + (u + 1))
                            b = (5, 3)[u]
                            copy(ye[u], ps[:, b:b + 2, :]).then_inc(S("ye_kept"), 1)

            def modulation(l):
                if l:
                    act.wait_ge(sg.sem(f"x_added{l - 1}"), x_final[l - 1, "act"])
                for n in range(12):
                    act.wait_ge(*GOT("chunk_used", "mod", l, 4 * n + 3))
                    copy(y[0:2, n, :], ps[0:2, 1 + n % 2, :]).then_inc(*OUT("mod_row", l, n))

            act.wait_ge(*GOT("const_in"))
            A_(ca[:, :, :], cc[:, :, :], ACT.Silu).then_inc(*OUT("cond_ready"))
            for l in range(DEPTH):
                modulation(l)
                norm(l, 0)
                rwkv_inputs(l)
                in_turn(lambda s: rwkv_flow(l, s))
                rwkv_readout(l)
                attention_inputs(l)
                attention(l)
                gmlp(l)
                merge(l)
                norm(l, 1)
                experts(l)
            norm(DEPTH, 0)

        @block.vector
        def _(dve):
            V = dve
            TT = V.tensor_tensor

            def heads(a, n=HEADS):
                return a.rearrange("p (h v) -> p h v", h=n)

            def norm(l, which):
                t0 = 0 if l < DEPTH and which == 0 else CTX if l == DEPTH else t0_of(l)
                V.wait_ge(*GOT("norm_rooted", l, which))
                V.reciprocal(rt[:, t0:], rt[:, t0:]).then_inc(*OUT("norm_rs", l, which))
                V.wait_ge(*GOT("norm_rs", l, which))
                for k in range(KT):
                    if l == DEPTH:
                        V.scalar_tensor_tensor(out=h[:, k, 0:LAT], in0=x[:, k, CTX:], scalar=vec[:, V_FG + k:V_FG + k + 1],
                                               in1=rt[:, t0:], op0=ALU.mult, op1=ALU.mult).then_inc(*OUT("out_ready"))
                    else:
                        TT(h[:, k, t0:], x[:, k, t0:], rt[:, t0:], ALU.mult).then_inc(*OUT("x_scaled", l, which, k))

            def modulation(l):
                V.wait_ge(*GOT("param_in", l))
                V.wait_ge(*GOT("mod_turned", l))
                if l:
                    V.wait_ge(sg.sem(f"x_added{l - 1}"), x_final[l - 1, "dve"])
                TT(mod[:, :, :], ps[:, 0, 0:96].rearrange("p (j s) -> p j s", s=2),
                   vec[:, V_MODB:V_MODB + 48].unsqueeze(2).to_broadcast([P, 48, 2]), ALU.add).then_inc(*OUT("mod_sum", l))
                V.wait_ge(*GOT("mod_sum", l))
                for q, (m, g) in enumerate(((8, V_N1), (32, V_N2))):
                    V.scalar_tensor_tensor(out=gain[:, q, :, :], in0=mod[:, m:m + 8, :], scalar=1.0,
                                           in1=vec[:, g:g + 8].unsqueeze(2).to_broadcast([P, 8, 2]),
                                           op0=ALU.add, op1=ALU.mult).then_inc(*OUT("mod_step", l, q))
                mu = vec[:, V_MU:V_MU + 15]
                V.tensor_scalar(mu2[:, 0, :], mu, 0.5, None, ALU.mult).then_inc(*OUT("mod_step", l, 2))
                V.tensor_scalar(mu2[:, 1, :], mu, -1.0, 1.0, ALU.mult, ALU.add).then_inc(*OUT("mod_ready", l))

            def rwkv_inputs(l):
                V.wait_ge(*GOT("x_scaled", l, 0, KT - 1))
                V.memset(view(MB, 1032), 0.0).then_inc(*OUT("raw_clear", l))
                V.memset(rt[:, :], 0.0).then_inc(*OUT("lora_clear", l))
                V.memset(state, 0.0).then_inc(*OUT("state_clear", l))
                V.wait_ge(*GOT("mod_ready", l))
                where = list(range(12)) + [ZW, ZA, ZG]
                for i in range(15):
                    V.wait_ge(*GOT("raw_copied", l, i))
                    if i >= 2:
                        V.wait_ge(*GOT("z_mixed", l, i - 2))
                    r, s_ = raw[:, i % 2, :, :], shs[:, i % 2, :, :]
                    TT(s_, r[:, :, 0:256], r[:, :, 2:258], ALU.add).then_inc(*OUT("z_sides", l, i))
                    V.wait_ge(*GOT("z_sides", l, i))
                    V.tensor_scalar(s_, s_, mu2[:, 0, i:i + 1], None, ALU.mult).then_inc(*OUT("z_half", l, i))
                    V.wait_ge(*GOT("z_half", l, i))
                    V.scalar_tensor_tensor(out=zc[:, where[i], :].rearrange("p (s t) -> p s t", s=2), in0=r[:, :, 1:257],
                                           scalar=mu2[:, 1, i:i + 1], in1=s_, op0=ALU.mult, op1=ALU.add) \
                        .then_inc(*OUT("z_mixed", l, i))
                V.wait_ge(*GOT("z_mixed", l, 14))
                for f in range(4):
                    V.tensor_scalar(zc[:, ZKK + f, :], zc[:, ZK + f, :], vec[:, V_KK + f:V_KK + f + 1], None, ALU.mult) \
                        .then_inc(*OUT("kk_raw", l, f))
                for f in range(4):
                    V.wait_ge(*GOT("kk_raw", l, f))
                    if f >= 2:
                        V.wait_ge(*GOT("kk_done", l, f - 2))
                    TT(kks[:, f % 2, :], zc[:, ZKK + f, :], zc[:, ZKK + f, :], ALU.mult).then_inc(*OUT("kk_squared", l, f))
                    V.wait_ge(*GOT("kk_summed", l, f))
                    V.tensor_scalar(kks[:, f % 2, :], ps[:, 2 + f % 2, :], 1e-12, None, ALU.max) \
                        .then_inc(*OUT("kk_clamped", l, f))
                    V.wait_ge(*GOT("kk_rooted", l, f))
                    V.reciprocal(kks[:, f % 2, :], kks[:, f % 2, :]).then_inc(*OUT("kk_inv", l, f))
                    V.wait_ge(*GOT("kk_inv", l, f))
                    TT(zc[:, ZKK + f, :], zc[:, ZKK + f, :], kks[:, f % 2, :], ALU.mult).then_inc(*OUT("kk_done", l, f))
                V.wait_ge(*GOT("kk_done", l, 3))
                for s in range(2):
                    V.memset(view(MB + 20 * s * HU * P, 4 * HU * P), 0.0).then_inc(*OUT("blocks_clear", l))

            def rwkv_flow(l, s):
                for c in range(STEPS):
                    yield from rwkv_step(l, c, s)
                    for u in range(HS // HU):
                        yield from rwkv_unit(l, c, s, u)

            def rwkv_step(l, c, s):
                k = (l, c, s)
                t = units[s]
                T = t.tok
                own = slice(s * 256, (s + 1) * 256)
                r, k_ = ps[:, t.bank, 0:256], ps[:, t.bank, 256:512]
                v, kk = ps[:, t.bank + 1, 0:256], ps[:, t.bank + 1, 256:512]
                if c:
                    V.wait_ge(*GOT("p_s", l, c - 1, s, 1))
                    V.wait_ge(*GOT("bg_in", l, c - 1, s, 1, 1, 1))
                V.wait_ge(*GOT("tokens_turned", *k))
                V.tensor_copy(T[5], v).then_inc(*OUT("v_kept", *k))
                V.wait_ge(*GOT("tanhed", *k, 1))
                both = y[:, 0:2, own]
                V.tensor_scalar(both, both, 0.5, 0.5, ALU.mult, ALU.add).then_inc(*OUT("sig_done", *k))
                yield
                V.wait_ge(*GOT("sig_done", *k))
                TT(T[6], kk, T[1], ALU.mult).then_inc(*OUT("kka", *k))
                V.scalar_tensor_tensor(out=T[7], in0=T[1], scalar=1.0, in1=rep[:, 0, own], op0=ALU.subtract, op1=ALU.mult) \
                    .then_inc(*OUT("kd_half", *k))
                V.wait_ge(*GOT("kd_half", *k))
                V.scalar_tensor_tensor(out=T[7], in0=T[7], scalar=1.0, in1=k_, op0=ALU.add, op1=ALU.mult) \
                    .then_inc(*OUT("kd_done", *k))
                V.wait_ge(*GOT("kd_done", *k))
                TT(T[1], r, T[7], ALU.mult).then_inc(*OUT("bonus_a", *k))
                V.wait_ge(*GOT("bonus_a", *k))
                V.wait_ge(*GOT("exps", *k, 0))
                TT(T[6], T[6], T[4], ALU.mult).then_inc(*OUT("operand", *k, 0))
                TT(T[7], T[7], T[4], ALU.mult).then_inc(*OUT("operand", *k, 1))
                V.wait_ge(*GOT("exps", *k, 2))
                TT(T[3], kk, T[3], ALU.mult).then_inc(*OUT("operand", *k, 2))
                TT(T[2], r, T[2], ALU.mult).then_inc(*OUT("operand", *k, 3))
                TT(T[1], T[1], rep[:, 1, own], ALU.mult).then_inc(*OUT("bonus_b", *k))
                V.wait_ge(*GOT("bonus_b", *k))
                V.tensor_reduce(osb[:, c, CW + s * HS:CW + (s + 1) * HS], heads(T[1], HS), AX.X, ALU.add) \
                    .then_inc(*OUT("bonus_kept", *k))
                yield

            def rwkv_unit(l, c, s, u):
                k = (l, c, s, u)
                t = units[s]
                A, B, C_, D_ = (t.bank + i for i in range(4))

                def bank(b, n=HU):
                    return ps[:, b, 0:n * P].rearrange("p (h t) -> p h t", t=P)

                V.wait_ge(*GOT("turned", *k))
                V.tensor_copy(t.bg, bank(B, 2 * HU)).then_inc(*OUT("bg_kept", *k))
                yield
                V.wait_ge(*GOT("gram", *k))

                def pair(a, lo):
                    return a.rearrange("p b (h t) -> p b h t", t=2 * P)[:, :, :, lo:lo + P]

                def per(m):
                    return con[:, m:m + 2, :].unsqueeze(2).to_broadcast([P, 2, HU, P])
                TT(t.ng.rearrange("p (m h) t -> p m h t", m=2), bank(A).unsqueeze(1).to_broadcast([P, 2, HU, P]), per(C_ND),
                   ALU.mult).then_inc(*OUT("masked", *k, 0))
                TT(t.ntb.rearrange("p (m h) t -> p m h t", m=2), pair(ps[:, C_:C_ + 2, :], 0), per(C_NDT), ALU.mult) \
                    .then_inc(*OUT("masked", *k, 1))
                TT(t.q, ps[:, C_:C_ + 2, :].rearrange("p b (h t) -> p (b h) t", t=2 * P)[:, :, P:],
                   C(C_MI).unsqueeze(1).to_broadcast([P, 2 * HU, P]), ALU.mult).then_inc(*OUT("masked", *k, 2))
                yield
                V.wait_ge(*GOT("p_nt2", *k))
                V.tensor_copy(t.b, bank(B)).then_inc(*OUT("nt2_kept", *k))
                yield
                V.wait_ge(*GOT("x1b_done", *k))
                V.wait_ge(*GOT("p_nt3", *k))
                TT(t.ma, bank(C_), t.x1, ALU.add).then_inc(*OUT("x2_done", *k))
                yield
                V.wait_ge(*GOT("x2_done", *k))
                V.wait_ge(*GOT("p_x4", *k))
                TT(t.mr, bank(C_), t.ma, ALU.add).then_inc(*OUT("x4_done", *k))
                yield
                V.wait_ge(*GOT("x4_done", *k))
                V.wait_ge(*GOT("p_x8", *k))
                TT(t.xt, bank(B), t.mr, ALU.add).then_inc(*OUT("xt_done", *k))
                yield
                V.wait_ge(*GOT("p_ht", *k))
                V.tensor_copy(t.nt, bank(C_)).then_inc(*OUT("ht_kept", *k))
                yield
                yield
                V.wait_ge(*GOT("w2_done", *k))
                V.wait_ge(*GOT("p_ht3", *k))
                TT(t.nt4, bank(C_), t.nt4, ALU.add).then_inc(*OUT("w_done", *k))
                yield
                yield
                yield
                h0 = s * HS + u * HU
                s_ = state[:, h0:h0 + HU, :]
                V.wait_ge(*GOT("p_s", *k))
                TT(s_, ps[:, C_, 0:HU * HD].rearrange("p (h v) -> p h v", v=HD), s_, ALU.add).then_inc(*OUT("state_sum", *k))
                V.wait_ge(*GOT("state_sum", *k))
                V.wait_ge(*GOT("exps", l, c, s, 3))
                TT(s_, s_, t.end[:, u * HU:(u + 1) * HU].unsqueeze(2).to_broadcast([P, HU, HD]), ALU.mult) \
                    .then_inc(*OUT("state_new", *k))
                yield

            def rwkv_readout(l):
                for i in range(t0_of(l) // P, NT):
                    def spread(a):
                        return a.unsqueeze(2).to_broadcast([P, HEADS, HD])
                    a, b = heads(tok[:, 0, :]), heads(tok[:, 1, :])
                    V.wait_ge(*GOT("read", l, i))
                    if i > t0_of(l) // P:
                        V.wait_ge(*GOT("yc_turned", l, i - 1))
                    V.tensor_reduce(st[:, 8:16], heads(ps[:, 0, :]), AX.X, ALU.add).then_inc(*OUT("ro", l, i, 0))
                    V.tensor_copy(st[:, 24:32], ps[:, 1, 0:8]).then_inc(*OUT("ro", l, i, 1))
                    V.wait_ge(*GOT("ro", l, i, 1))
                    V.tensor_scalar(st[:, 8:16], st[:, 8:16], 1.0 / HD, None, ALU.mult).then_inc(*OUT("ro", l, i, 2))
                    TT(b, heads(ps[:, 2, :]), spread(st[:, 24:32]), ALU.mult).then_inc(*OUT("ro", l, i, 3))
                    V.wait_ge(*GOT("ro", l, i, 2))
                    TT(a, heads(ps[:, 0, :]), spread(st[:, 8:16]), ALU.subtract).then_inc(*OUT("ro", l, i, 4))
                    V.wait_ge(*GOT("ro", l, i, 4))
                    TT(heads(tok[:, 2, :]), a, a, ALU.mult).then_inc(*OUT("ro", l, i, 5))
                    V.wait_ge(*GOT("ro", l, i, 5))
                    V.tensor_reduce(st[:, 16:24], heads(tok[:, 2, :]), AX.X, ALU.add).then_inc(*OUT("var_done", l, i))
                    V.wait_ge(*GOT("var_rooted", l, i))
                    V.reciprocal(st[:, 16:24], st[:, 16:24]).then_inc(*OUT("ro", l, i, 6))
                    V.wait_ge(*GOT("ro", l, i, 6))
                    TT(a, a, spread(st[:, 16:24]), ALU.mult).then_inc(*OUT("ro", l, i, 7))
                    for q, (z, op) in enumerate(((rep[:, 2, :], ALU.mult), (rep[:, 3, :], ALU.add), (tok[:, 1, :], ALU.add))):
                        V.wait_ge(*GOT("ro", l, i, 7 + q))
                        TT(tok[:, 0, :], tok[:, 0, :], z, op).then_inc(*OUT("ro", l, i, 8 + q))
                    V.wait_ge(*GOT("ro", l, i, 10))
                    TT(tok[:, 0, :], ps[:, 3, :], tok[:, 0, :], ALU.mult).then_inc(*OUT("yc_done", l, i))

            def attention_inputs(l):
                t0 = t0_of(l)
                for i in range(2):
                    V.wait_ge(*GOT("zb_rooted", l, i))
                    V.reciprocal(pr[:, 0, i, :], pr[:, 0, i, :]).then_inc(*OUT("zb_inv", l, i))
                for i in range(5):
                    V.wait_ge(*GOT("zb_inv", l, 0 if i < 3 else 1))
                    V.scalar_tensor_tensor(out=zq[:, i, :], in0=zq[:, i, :], scalar=vec[:, V_QN + i:V_QN + i + 1],
                                           in1=pr[:, 0, 0 if i < 3 else 1, :], op0=ALU.mult, op1=ALU.mult) \
                        .then_inc(*OUT("zb_scaled", l, i))

                def rope(src, dst, name, *key):
                    b = rtmp[64:96, :, :, :]
                    TT(b[:, 0, 0, :], src[96:128, CTX:], cs[96:128, 1, :], ALU.mult).then_inc(*OUT("rope_sin", name, *key))
                    TT(b[:, 1, 0, :], src[64:96, CTX:], cs[64:96, 0, :], ALU.mult).then_inc(*OUT("rope_cos", name, *key))
                    V.wait_ge(*GOT("rope_cos", name, *key))
                    return TT(dst, b[:, 0, 0, :], b[:, 1, 0, :], ALU.add)

                V.wait_ge(*GOT("chunk_used", "zb", l, 5))
                V.tensor_copy(kt_[64:96, 0, 0:CTX], ps[64:96, 1, 0:CTX]).then_inc(*OUT("kr_ctx", l))
                rope(ps[:, 1, :], kt_[64:96, 0, CTX:], "k", l).then_inc(*OUT("kr_made", l))
                V.wait_ge(*GOT("kr_made", l))
                V.wait_ge(*GOT("kr_ctx", l))
                V.tensor_copy(kt_[64:96, 1:HEADS, :], kt_[64:96, 0:1, :].to_broadcast([32, HEADS - 1, TOK])) \
                    .then_inc(*OUT("kr_spread", l))
                for hh in range(HEADS):
                    V.wait_ge(*(GOT("q_made", l, hh) if hh % 2 == 0 else GOT("chunk_used", "uq", l, hh // 2)))
                    V.wait_ge(*(GOT("kr_made", l) if hh == 0 else GOT("q_roped", l, hh - 1)))
                    if t0 == 0:
                        V.tensor_copy(qt[64:96, hh, 0:CTX], ps[64:96, 4 + hh % 2, 0:CTX]).then_inc(*OUT("q_mid", l, hh))
                    rope(ps[:, 4 + hh % 2, :], qt[64:96, hh, CTX:], "q", l, hh).then_inc(*OUT("q_roped", l, hh))

            def attention(l):
                pairs = attention_pairs(l)

                def maxima(n):
                    nk = 4 if pairs[n][0] else 2
                    c0 = 32 + n % 2 * 8
                    V.wait_ge(*GOT("scores", l, n))
                    V.tensor_reduce(st[:, c0 + 4:c0 + 6], ps[:, n % 2 * 2:n % 2 * 2 + 2, 0:nk * P], AX.X, ALU.max) \
                        .then_inc(*OUT("max_raw", l, n))
                    V.wait_ge(*GOT("max_raw", l, n))
                    V.tensor_scalar(st[:, c0:c0 + 2], st[:, c0 + 4:c0 + 6], -MLA_SCALE, None, ALU.mult) \
                        .then_inc(*OUT("max_done", l, n))

                maxima(0)
                for n in range(len(pairs)):
                    nk = 4 if pairs[n][0] else 2
                    c0 = 32 + n % 2 * 8
                    if n + 1 < len(pairs):
                        maxima(n + 1)
                    V.wait_ge(*GOT("prob", l, n, 1))
                    V.reciprocal(st[:, c0 + 2:c0 + 4], st[:, c0 + 2:c0 + 4]).then_inc(*OUT("sum_inv", l, n))
                    V.wait_ge(*GOT("sum_inv", l, n))
                    for q in range(2):
                        p_ = pr[:, n % 2, q, 0:nk * P]
                        V.tensor_scalar(p_, p_, st[:, c0 + 2 + q:c0 + 3 + q], None, ALU.mult) \
                            .then_inc(*OUT("prob_scaled", l, n, q))

            def gmlp(l):
                t0 = t0_of(l)
                V.wait_ge(*GOT("v_rooted", l))
                s_ = st[:, 52 + t0 // P:56]
                V.reciprocal(s_, s_).then_inc(*OUT("v_inv", l))
                V.wait_ge(*GOT("v_inv", l))
                for t in range(t0 // P, NT):
                    V.tensor_scalar(vg[:, t, :], vg[:, t, :], st[:, 52 + t:53 + t], None, ALU.mult) \
                        .then_inc(*OUT("v_normed", l, t))
                for g in range(4):
                    V.wait_ge(*GOT("mixed", l, g))
                    o = at[:, g, t0:].rearrange("p (t i) -> p t i", i=P)
                    n = NT - t0 // P
                    V.scalar_tensor_tensor(out=o, in0=ps[:, 4 + g, t0:].rearrange("p (t i) -> p t i", i=P),
                                           scalar=vec[:, V_AVG + g:V_AVG + g + 1],
                                           in1=bs[:, g:g + 1, :].to_broadcast([P, n, P]), op0=ALU.mult, op1=ALU.add) \
                        .then_inc(*OUT("mix_biased", l, g))
                    V.wait_ge(*GOT("mix_biased", l, g))
                    TT(y[:, g, t0:], at[:, g, t0:], ut[:, g, t0:], ALU.mult).then_inc(*OUT("ya_done", l, g))

            def merge(l):
                t0 = t0_of(l)
                for j in range(KT):
                    V.wait_ge(*GOT("chunk_used", "up", l, j, 1))
                    V.wait_ge(*GOT("gated", l, j, 2))
                    o = mg[:, j, t0:]
                    for g in range(3):
                        s_ = sgm[:, j % 2, g, t0:]
                        TT(s_ if g else o, ps[:, 3 + g, t0:], s_, ALU.mult).then_inc(*OUT("merged", l, j, g))
                    for g in (1, 2):
                        V.wait_ge(*GOT("merged", l, j, g + 1))
                        TT(o, o, sgm[:, j % 2, g, t0:], ALU.add).then_inc(*OUT("merged", l, j, 2 + g))
                for j in range(KT):
                    V.wait_ge(*GOT("chunk_used", "wo", l, j))
                    for s in range(t0 // CTX, 2):
                        r = slice(s * CTX, (s + 1) * CTX)
                        ins = V.scalar_tensor_tensor(out=x[:, j, r], in0=ps[:, 6 + j % 2, r], scalar=mod[:, 16 + j, s:s + 1],
                                                     in1=x[:, j, r], op0=ALU.mult, op1=ALU.add)
                    ins.then_inc(*OUT(f"x_added{l}", j))

            def router(l):
                a = t0_of(l) // P
                n = NT - a
                G = n * NG

                def grp(t):
                    return t[:, a:, :].rearrange("p t (g e) -> p (t g) e", e=EPG)
                rank = small[:, 2 + P + NE:2 + P + NE + EPG]
                dec = rank.unsqueeze(1).to_broadcast([P, G, EPG])
                m = rt[:, 0:16 * 8].rearrange("p (m g) -> p m g", g=16)
                step = [0]

                def run(ins):
                    step[0] += 1
                    ins.then_inc(*OUT("route", l, step[0]))
                    V.wait_ge(*GOT("route", l, step[0]))

                def over(i, e=EPG):
                    return m[:, i, 0:G].unsqueeze(2).to_broadcast([P, G, e])

                def top(src, i, onehot):
                    run(V.tensor_reduce(m[:, i, 0:G], src, AX.X, ALU.max))
                    run(TT(onehot, src, over(i), ALU.is_equal))
                    run(TT(onehot, onehot, dec, ALU.mult))
                    run(V.tensor_reduce(m[:, 7, 0:G], onehot, AX.X, ALU.max))
                    run(TT(onehot, onehot, over(7), ALU.is_equal))

                V.wait_ge(*GOT("scored", l))
                run(TT(sel[:, a:, :], score[:, a:, :], rb[:, :].unsqueeze(1).to_broadcast([P, n, NE]), ALU.add))
                top(grp(sel), 0, grp(first))
                run(V.scalar_tensor_tensor(out=grp(pick), in0=grp(first), scalar=-1e30, in1=grp(sel), op0=ALU.mult, op1=ALU.add))
                top(grp(pick), 1, grp(second))
                run(TT(m[:, 2, 0:G], m[:, 0, 0:G], m[:, 1, 0:G], ALU.add))

                def rows(i):
                    return m[:, i, 0:G].rearrange("p (t g) -> p t g", g=NG)
                dg = rank.unsqueeze(1).to_broadcast([P, n, NG])

                def wide(i):
                    return m[:, i, 0:n].unsqueeze(2).to_broadcast([P, n, NG])
                run(V.tensor_reduce(m[:, 3, 0:n], rows(2), AX.X, ALU.max))
                run(TT(rows(4), rows(2), wide(3), ALU.is_equal))
                run(TT(rows(4), rows(4), dg, ALU.mult))
                run(V.tensor_reduce(m[:, 3, 0:n], rows(4), AX.X, ALU.max))
                run(TT(rows(4), rows(4), wide(3), ALU.is_equal))
                run(TT(grp(first), grp(first), grp(second), ALU.add))
                TT(grp(mask), grp(first), over(4), ALU.mult).then_inc(*OUT("mask_done", l))
                V.wait_ge(*GOT("mask_done", l))
                run(TT(first[:, a:, :], mask[:, a:, :], score[:, a:, :], ALU.mult))
                run(V.tensor_reduce(m[:, 5, 0:n], first[:, a:, :], AX.X, ALU.add))
                run(V.reciprocal(m[:, 5, 0:n], m[:, 5, 0:n]))
                run(TT(comb[:, a:, :], first[:, a:, :], m[:, 5, 0:n].unsqueeze(2).to_broadcast([P, n, NE]), ALU.mult))
                V.wait_ge(*GOT("placed", l))
                pos = ps[:, 6, 64 + a * NE:64 + NT * NE].rearrange("p (t e) -> p t e", e=NE)
                run(V.scalar_tensor_tensor(out=place[:, a:, :], in0=pos, scalar=-FAR, in1=mask[:, a:, :], op0=ALU.add, op1=ALU.mult))
                run(V.tensor_scalar(place[:, a:, :], place[:, a:, :], FAR, None, ALU.add))
                run(V.tensor_reduce(m[:, 6, 0:1], ps[:, 6, 128:128 + NE], AX.X, ALU.max))
                run(V.tensor_scalar(m[:, 6, 1:2], m[:, 6, 0:1], float(CAP), 1.0, ALU.is_gt, ALU.add))
                for i in range(2, TOK // CAP):
                    run(V.tensor_scalar(m[:, 6, 2:3], m[:, 6, 0:1], float(i * CAP), None, ALU.is_gt))
                    run(TT(m[:, 6, 1:2], m[:, 6, 1:2], m[:, 6, 2:3], ALU.add))
                run(V.tensor_copy(slots, C(C_IOTA)))
                V.tensor_copy(passes[:, :], m[:, 6, 1:2]).then_inc(*OUT("passes_set", l))

            def experts(l):
                t0 = t0_of(l)
                a = t0 // P
                nt = NT - a

                def S(name):
                    return sg.sem(f"{name}{l}")
                V.wait_ge(*GOT("passes_set", l))
                V.wait_ge(*GOT("row_turned", l, NT - 1))
                n_passes = V.value_load(passes[0:1, 0:1], min_val=1, max_val=TOK // CAP)
                x_final[l, "dve"] = n_passes * (NE * KT) + KT
                sl = slots.unsqueeze(1).to_broadcast([P, nt, CAP])
                with V.Fori(0, n_passes, 1) as p:
                    with V.Fori(0, NE // 2, 1) as j:
                        n = V.snap(p * NE + j * 2)
                        for u in range(2):
                            def of_expert(t):
                                e = wsf[:, (5 if t == "comb" else 7) * 64 + a * NE:][:, 0:nt * NE]
                                return e.rearrange("p (t e) -> p t e", e=NE)[:, :, bass.ds(j * 2 + u, 1)].to_broadcast([P, nt, CAP])
                            V.wait_ge(S("slots_moved"), p)
                            TT(pk[u][:, a:, :], sl, of_expert("place"), ALU.is_equal).then_inc(S("picks"), 1)
                            V.wait_ge(S("picks"), n + (u + 1))
                            V.wait_ge(S("turned_back"), n + u)
                            TT(pkw[:, a:, :], pk[u][:, a:, :], of_expert("comb"), ALU.mult).then_inc(S("weighted"), 1)
                        for u in range(2):
                            V.wait_ge(S("silu_done"), n + (u + 1))
                            TT(he[u], ps[:, 4, :], sil[u], ALU.mult).then_inc(S("he_done"), 1)
                        for u in range(2):
                            for d in range(KT):
                                V.wait_ge(S("scattered"), n * KT + (KT * u + d + 1))
                                V.wait_ge(S("x_added"), n * KT + (KT * u + d + 1))
                                for s in range(t0 // CTX, 2):
                                    r = slice(s * CTX, (s + 1) * CTX)
                                    ins = V.scalar_tensor_tensor(out=x[:, d, r], in0=ps[:, 5 + d % 2, r],
                                                                 scalar=mod[:, 40 + d, s:s + 1], in1=x[:, d, r],
                                                                 op0=ALU.mult, op1=ALU.add)
                                ins.then_inc(S("x_added"), 1)
                    V.wait_ge(S("weighted"), p * NE + NE)
                    V.tensor_scalar(slots, slots, float(CAP), None, ALU.add).then_inc(S("slots_moved"), 1)

            V.memset(eps[:, 0:1], EPS).then_inc(*OUT("eps_half"))
            V.memset(eps[:, 1:2], GN_EPS).then_inc(*OUT("eps_set"))
            V.wait_ge(*GOT("const_in"))
            for l in range(DEPTH):
                modulation(l)
                norm(l, 0)
                rwkv_inputs(l)
                in_turn(lambda s: rwkv_flow(l, s))
                rwkv_readout(l)
                attention_inputs(l)
                attention(l)
                gmlp(l)
                merge(l)
                norm(l, 1)
                router(l)
                experts(l)
            norm(DEPTH, 0)

        @block.gpsimd
        def _(pool):
            last = []

            def alone():
                if last:
                    pool.wait_ge(*GOT(*last[-1]))

            def run(ins, *key):
                ins.then_inc(*OUT(*key))
                last.append(key)

            def rwkv_flow(l, s):
                for c in range(STEPS):
                    yield from rwkv_step(l, c, s)
                    for u in range(HS // HU):
                        yield from rwkv_unit(l, c, s, u)

            def rwkv_step(l, c, s):
                t = units[s]
                if c == 0:
                    pool.wait_ge(*GOT("kk_done", l, 3))
                    pool.wait_ge(*GOT("blocks_clear", l))
                else:
                    pool.wait_ge(*GOT("tokens_turned", l, c - 1, s))
                for d in range(2):
                    a = chunk_start(c, d)
                    alone()
                    run(pool.tensor_copy(t.stage[:, :, d * CH:(d + 1) * CH].rearrange("p (q f) t -> p q f t", f=2),
                                         zc[:, 0:16, a:a + CH].rearrange("p (q f) t -> p q f t", f=4)[:, :, 2 * s:2 * s + 2, :]),
                        "staged", l, c, s, d)
                yield
                yield

            def rwkv_unit(l, c, s, u):
                k = (l, c, s, u)
                t = units[s]
                prev = (l, c, s, 0) if u else (l, c - 1, s, 1)
                if c or u:
                    pool.wait_ge(*GOT("xt_done", *prev))
                for q, (m, i) in enumerate(((t.ma, 3), (t.mr, 2))):
                    pool.wait_ge(*GOT("operand", l, c, s, 2 + q))
                    for d in range(2):
                        r = slice(d * CH, (d + 1) * CH)
                        alone()
                        run(pool.tensor_copy(m[r, :, d * HD:(d + 1) * HD],
                                             t.tok[i][r, u * P:(u + 1) * P].rearrange("p (h v) -> p h v", v=HD)),
                            "ar_in", *k, q, d)
                yield
                eye = C(C_ID).unsqueeze(1).to_broadcast([P, HU, P])
                pool.wait_ge(*GOT("masked", *k, 1))
                alone()
                run(pool.tensor_tensor(t.x1, t.nt, eye, ALU.add), "x1_done", *k)
                yield
                pool.wait_ge(*GOT("nt2_kept", *k))
                alone()
                run(pool.tensor_tensor(t.x1, t.x1, t.b, ALU.add), "x1b_done", *k)
                yield
                yield
                yield
                yield
                pool.wait_ge(*GOT("ht_kept", *k))
                alone()
                run(pool.tensor_tensor(t.nt4, t.nt, eye, ALU.add), "w1_done", *k)
                yield
                pool.wait_ge(*GOT("ht2_kept", *k))
                alone()
                run(pool.tensor_tensor(t.nt4, t.nt4, t.n4, ALU.add), "w2_done", *k)
                yield
                yield
                yield
                yield
                yield

            for l in range(DEPTH):
                in_turn(lambda s: rwkv_flow(l, s))

        return sg.at


def layout(i):
    def chunk(wt):
        k, n = wt.shape[-2:]
        a = np.moveaxis(wt.reshape(wt.shape[:-2] + (k // P, P, n)), -3, -2)
        return a.reshape(a.shape[:-2] + (k // P * n,))

    def chunks(wt):
        L_, k, n = wt.shape
        a = wt.reshape(L_, k // P, P, n // P, P).transpose(0, 3, 2, 1, 4)
        return a.reshape(L_, n // P, P, k)

    def cols(v):
        return v.reshape(-1, P).T

    def per(f):
        return np.stack([f(l) for l in range(DEPTH)])
    swap = np.array([a * 16 + (1 - b) * 8 + f for a in range(2) for b in range(2) for f in range(8)])
    w_in = i["w_in"]
    b_cols = QL + KVL + ROPE
    c_cols = 15 * P
    kr = w_in[:, :, QL + KVL:b_cols]
    zb = np.concatenate([w_in[:, :, :QL + KVL], kr, kr, kr, kr[:, :, swap]], -1)
    a0 = b_cols + c_cols
    uq = i["b_w_uq"].reshape(DEPTH, QL, HEADS, QK)
    uq = np.concatenate([uq, uq[..., NOPE + swap]], -1).reshape(DEPTH, 3, P, 4, 2, P).transpose(0, 3, 2, 4, 1, 5)
    ukv = i["b_w_ukv"].reshape(DEPTH, 2, P, HEADS, NOPE + VD)
    up = np.stack([i["w_up_a"], i["w_up_b"], i["w_up_c"]], 1).reshape(DEPTH, 3, 4, P, KT, P)
    zv = w_in[:, :, a0 + CW:a0 + 2 * CW].reshape(DEPTH, 4, 2, P, CW).transpose(0, 1, 3, 2, 4)
    ones = np.ones((1, P, 1), np.float32)

    def spread(v):
        return np.broadcast_to(v, (P,) + v.shape)
    xs = np.concatenate([i["ctx"][0], i["x"][0]], 0)
    d = {
        "x": xs.T.reshape(KT, P, TOK).transpose(1, 0, 2),
        "cc": np.stack([i["c_ctx"], i["c"][0]], -1).reshape(KT, P, 2).transpose(1, 0, 2),
        "con": constants(), "small": small_constants(), "cs": rope_tables()[64:],
        "rw": i["router_w"].reshape(KT, P, NE).transpose(1, 0, 2),
        "rb": spread(i["router_b"]),
        "mod": i["mod_w"].reshape(DEPTH, 4, 2, P, 12, 512).transpose(0, 4, 1, 3, 2, 5).reshape(DEPTH, 48, P, SLOT),
        "zc": chunks(w_in[:, :, b_cols:a0]),
        "zb": chunks(zb),
        "uq": uq.reshape(DEPTH, 4, P, 768),
        "uk": ukv[..., :NOPE].transpose(0, 2, 3, 1, 4).reshape(DEPTH, P, SLOT),
        "uv": ukv[..., NOPE:].transpose(0, 2, 1, 3, 4).reshape(DEPTH, P, SLOT),
        "zu": chunks(w_in[:, :, a0:a0 + CW]),
        "zv": zv.reshape(DEPTH, 4, P, SLOT),
        "gate": chunks(w_in[:, :, a0 + 2 * CW:]),
        "up": up.transpose(0, 4, 3, 1, 2, 5).reshape(DEPTH, KT, P, 1536),
        "wo": chunks(i["w_o"]),
        "w13": np.concatenate([i["moe_w1"], i["moe_w3"]], -1).reshape(DEPTH, NE, KT, P, 2 * DE).transpose(0, 1, 3, 2, 4),
        "w2": i["moe_w2"].reshape(DEPTH, NE, 4, P, D).transpose(0, 1, 3, 2, 4),
        "vec": per(lambda l: np.concatenate([cols(i[n][l]) for n in ("norm1_g", "norm2_g", "mod_b", "b_q_norm", "b_kv_norm",
                                             "a_v_gain", "c_mu", "c_k_k")] + [cols(i["final_g"])], 1)),
        "rep": per(lambda l: spread(np.stack([i["c_k_a"][l], i["c_r_k"][l].reshape(-1), i["c_gn_g"][l], i["c_gn_b"][l]]))),
        "lora": per(lambda l: np.stack([i["c_w2"][l].reshape(P, CW), i["c_a2"][l].reshape(P, CW), i["c_g2"][l]], 1)),
        "bias2": per(lambda l: np.stack([i["c_w0"][l], i["c_a0"][l]], 1)),
        "bs": per(lambda l: spread(i["a_bs"][l])),
        "ws": i["a_ws"].transpose(0, 3, 1, 2),
    }
    return {k: np.ascontiguousarray(v) for k, v in d.items()}


def kernel(**inputs):
    import concourse.bacc as bacc
    from concourse.bass_utils import run_bass_kernel_spmd as run

    arrays = layout({k: np.asarray(v) for k, v in inputs.items()})
    known = None
    for _ in range(2):
        nc = bacc.Bacc("TRN2", target_bir_lowering=False, num_devices=1)
        w = {k: nc.dram_tensor(f"in_{k}", v.shape, F32, kind="ExternalInput").ap() for k, v in arrays.items()}
        out = nc.dram_tensor("out", (P, KT, LAT), F32, kind="ExternalOutput").ap()
        known = build(nc, w, out, known)
    r = run(nc, [{f"in_{k}": v for k, v in arrays.items()}], core_ids=[0])
    return r.results[0]["out"].transpose(2, 1, 0).reshape(1, LAT, D)
```

```python
from contextlib import ExitStack

import numpy as np
import concourse.bass as bass
from concourse import mybir

F32 = mybir.dt.float32
ACT = mybir.ActivationFunctionType
ALU = mybir.AluOpType
AX = mybir.AxisListType

P = 128
DEPTH = 2
D = 1024
KT = D // P
CTX = 256
LAT = 256
TOK = CTX + LAT
NT = TOK // P
EPS = 1e-6
GN_EPS = 64e-5
DECAY = 0.6065306597126334
HEADS = 8
HD = 64
NOPE, ROPE, VD = 64, 32, 64
QK = NOPE + ROPE
QL, KVL = 384, 256
MLA_SCALE = float((NOPE + ROPE) ** -0.5)
CW = 512
CH = 64
STEPS = TOK // CH
HS = 4
HU = 2
NE, NG, EPG, DE = 16, 4, 4, 512
PAIRS = NE // 2
RING = 4
SLOT = 1024
CAP = P
MOD_ROWS = 16 + 16 + 48
KK_AT = 8
FAR = 4096.0

V_N1, V_N2, V_MODB, V_QN, V_KVN, V_AVG, V_MU, V_KK, V_FG = 0, 8, 16, 64, 67, 69, 73, 88, 92
NVEC = 100
ZR, ZK, ZV, ZKK, ZW, ZA, ZG = 0, 4, 8, 12, 16, 17, 18
(C_ID, C_ONE, C_BONE, C_NDT, C_MS, C_MI, C_ND, C_NO, C_S00, C_S01, C_S10, C_S11, C_TRI, C_IOTA) = range(14)
NCONST = 14


def constants():
    c = np.zeros((NCONST, P, P), np.float32)
    row = np.arange(P)
    d, t = row // CH, row % CH
    same = d[:, None] == d[None, :]
    fwd = d[:, None] == 0
    before = np.where(fwd, t[:, None] < t[None, :], t[:, None] > t[None, :]) & same
    equal = np.eye(P, dtype=bool)
    block = (t[:, None] // 16) == (t[None, :] // 16)
    c[C_ID] = equal
    c[C_ONE] = 1.0
    c[C_TRI] = row[:, None] < row[None, :]
    c[C_IOTA] = row[None, :]
    c[C_BONE] = same
    c[C_MS] = before
    c[C_MI] = before | equal
    c[C_NDT] = -(before & block).astype(np.float32)
    c[C_ND] = c[C_NDT].T
    c[C_NO] = -(before & ~block).astype(np.float32).T
    for dd in range(2):
        for half in range(2):
            for i in range(CH):
                c[C_S00 + 2 * dd + half, dd * CH + i, half * CH + i] = 1.0
    return np.ascontiguousarray(c.transpose(1, 0, 2))


def small_constants():
    s = np.zeros((P, 2 + P + 16 + 4), np.float32)
    s[:CH, 0] = 1.0
    s[CH:, 1] = 1.0
    s[0, 2:2 + CH] = 1.0
    s[1, 2 + CH:2 + P] = 1.0
    s[:16, 2 + P:2 + P + 16] = np.eye(16)
    s[:, 2 + P + 16:] = [4.0, 3.0, 2.0, 1.0]
    return s


def rope_tables():
    nf = ROPE // 4
    tok = np.arange(LAT)
    pos = np.stack([tok // 64, tok % 64], 0).astype(np.float32)
    inv = np.power(np.float32(10000.0), -np.arange(nf, dtype=np.float32) / nf)
    out = np.zeros((P, 2, LAT), np.float32)
    for ax in range(2):
        ang = pos[ax][None, :] * inv[:, None]
        for half in range(2):
            r = ax * 2 * nf + half * nf
            out[64 + r:64 + r + nf, 0] = np.cos(ang)
            out[96 + r:96 + r + nf, 1] = np.sin(ang) * (-1.0 if half == 0 else 1.0)
    return out


SHARED = {
    "products_of_inverse": "p_nt2 p_n2 p_nt3 p_n4 p_nt4 p_x4 p_n8 p_x8 p_h p_ht p_x p_ht2 p_ht3 p_tt",
    "products_of_chain": "p_r p_u p_s p_o turned gram tokens_turned logits cums",
    "products_of_attention": "q_made k_made v_made scores prob_turned attended zb_summed",
    "products_of_rest": "norm_summed kk_summed read yc_turned mixed routed mod_turned row_turned placed",
    "inverse_kept_by_act": "n2_kept n4_kept nt4_kept n8_kept h_kept x_kept ht2_kept tt_kept ar_kept bg_in",
    "chain_kept_by_act": "r_kept u_kept o_kept exps tanhed lora_in",
    "attention_by_act": "zb_kept zb_squared zb_rooted q_kept k_kept v_stored prob pt_kept yb_kept",
    "inputs_by_act": "squared norm_rooted h_done h_part raw_copied kk_rooted cond_ready crow_ready zg_done mod_row",
    "readout_by_act": "var_rooted yc_kept",
    "gmlp_by_act": "u_gelu v_gelu v_sq v_rooted scored gated row_kept",
    "inverse_by_dve": "nt2_kept x2_done x4_done xt_done ht_kept w_done masked bg_kept",
    "chain_by_dve": "sig_done kka kd_half kd_done bonus_a bonus_b bonus_kept operand state_sum state_new v_kept",
    "attention_by_dve": "zb_inv zb_scaled rope_sin rope_cos kr_ctx q_mid kr_made kr_spread q_roped max_raw max_done sum_inv prob_scaled",
    "inputs_by_dve": "norm_rs x_scaled mod_sum mod_step mod_rest mod_ready raw_clear lora_clear state_clear z_sides z_half z_mixed kk_raw "
                     "kk_squared kk_clamped kk_inv kk_done blocks_clear eps_half eps_set out_ready",
    "readout_by_dve": "ro var_done yc_done v_inv v_normed mix_biased ya_done merged route mask_done",
    "step_by_pool": "staged ar_in x1_done x1b_done w1_done w2_done",
}
SEMAPHORE = {n: g for g, names in SHARED.items() for n in names.split()}


class Signals:

    def __init__(self, ctx, nc, known):
        self.ctx, self.nc, self.known = ctx, nc, known
        self.sems, self.count, self.at = {}, {}, {}

    def sem(self, name):
        name = SEMAPHORE.get(name, name)
        if name not in self.sems:
            self.sems[name] = self.ctx.enter_context(self.nc.semaphore(name))
            self.count[name] = 0
        return self.sems[name]

    def out(self, name, *key, by=1):
        s = self.sem(name)
        shared = SEMAPHORE.get(name, name)
        self.count[shared] += by
        self.at[(name, *key)] = self.count[shared]
        return s, by

    def got(self, name, *key):
        value = self.known[(name, *key)] if self.known is not None else 1
        return self.sem(name), value


def stream(l, w):
    if l == 0:
        for j in range(16):
            yield ("mod", l, j), w["mod"][j], SLOT
    for i in range(15):
        yield ("zc", l, i), w["zc"][l, i], SLOT
    for i in range(6):
        yield ("zb", l, i), w["zb"][l, i], SLOT
    for i in range(4):
        yield ("uq", l, i), w["uq"][l, i], 768
    yield ("uk", l, 0), w["uk"][l], SLOT
    yield ("uv", l, 0), w["uv"][l], SLOT
    for i in range(4):
        yield ("zu", l, i), w["zu"][l, i], SLOT
    for i in range(4):
        yield ("zv", l, i), w["zv"][l, i], SLOT
    for j in range(KT):
        for g in range(3):
            yield ("gate", l, j, g), w["gate"][l, g * KT + j], SLOT
        yield ("up", l, j, 0), w["up"][l, j, :, 0:1024], SLOT
        yield ("up", l, j, 1), w["up"][l, j, :, 1024:1536], 512
    for j in range(KT):
        yield ("wo", l, j), w["wo"][l, j], SLOT


def build(nc, w, out, known):
    with ExitStack() as ctx:
        def sb(name, shape):
            return ctx.enter_context(nc.sbuf_tensor(name, shape, F32))

        sg = Signals(ctx, nc, known)
        OUT, GOT = sg.out, sg.got

        x = sb("x", [P, KT, TOK])
        h = sb("h", [P, KT, TOK])
        y = sb("y", [P, 12, TOK])
        ring = sb("ring", [P, RING, SLOT])
        con = sb("con", [P, NCONST, P])
        small = sb("small", [P, 150])
        vec = sb("vec", [P, NVEC])
        rep = sb("rep", [P, 4, CW])
        lora = sb("lora", [P, 3, CW])
        misc = sb("misc", [P, 2, CW])
        bias2 = misc[0:2, :, :]
        cs = misc[:, 0, :].rearrange("p (a t) -> p a t", a=2)
        bs = sb("bs", [P, 4, P])
        ws = sb("ws", [P, 4, P])
        rw = sb("rw", [P, KT, NE])
        rb = sb("rb", [P, NE])
        cc = sb("cc", [P, KT, 2])
        ca = sb("ca", [P, KT, 2])
        mod = sb("mod", [P, 48, 2])
        mod_next = sb("mod_next", [P, 48, 2])
        gain = sb("gain", [P, 2, KT, 2])
        mu2 = sb("mu2", [P, 2, 15])
        eps = sb("eps", [P, 2])
        st = sb("st", [P, 64])
        rt = sb("rt", [P, 512])
        arena = sb("arena", [P, 24640])
        passes = ctx.enter_context(nc.sbuf_tensor("passes", [P, 1], mybir.dt.int32))
        ps = ctx.enter_context(nc.psum_tensor("ps", [P, 8, 512], F32))

        def C(i):
            return con[:, i, :]

        def view(at, *dims):
            n = int(np.prod(dims))
            a = arena[:, at:at + n]
            if len(dims) == 2:
                return a.rearrange("p (a b) -> p a b", b=dims[1])
            if len(dims) == 3:
                return a.rearrange("p (a b c) -> p a b c", b=dims[1], c=dims[2])
            return a

        sq = view(0, 8, 512)
        zc = view(0, 19, 512)
        osb = view(9728, STEPS, 520)
        state = view(13888, HEADS, HD)
        MB = 14400

        class Unit:

            def __init__(self, s):
                def mat(i, n=1):
                    return view(MB + (20 * s + i) * HU * P, n * HU, P)
                self.mb, self.mg, self.ma, self.mr = (mat(i) for i in range(4))
                self.ar = view(MB + (20 * s + 4) * HU * P, HU, 2 * P)
                self.bg = mat(6, 2)
                self.b, self.g = mat(6), mat(7)
                self.ntb, self.nt, self.bt = mat(8, 2), mat(8), mat(9)
                self.ng, self.n, self.go = mat(10, 2), mat(10), mat(11)
                self.q, self.qb, self.qg = mat(12, 2), mat(12), mat(13)
                self.n4, self.nt4, self.n8 = (mat(i) for i in range(14, 17))
                self.xt = self.x1 = mat(17)
                self.x = self.b
                self.mbs, self.mgs = [self.mb, mat(18)], [self.mg, mat(19)]
                self.bank = 4 * s
                self.tok = [y[:, i, s * HS * HD:(s + 1) * HS * HD] for i in range(8)]
                self.stage = y[:, 8 + 2 * s:10 + 2 * s, :].rearrange("p a (b c) -> p (a b) c", c=P)
                self.low = [rt[:, (2 * s + q) * P:(2 * s + q + 1) * P] for q in range(2)]
                self.v = self.tok[5].rearrange("p (h v) -> p h v", v=HD)
                self.end = st[:, 4 * s:4 * s + 4]

        units = [Unit(s) for s in range(2)]
        tok = y[:, 0:8, :]
        raw = view(MB, 2, 2, 258)
        shs = view(MB + 1100, 2, 2, 256)
        kks = view(MB + 2200, 2, 512)
        zq = view(0, 5, 512)
        qt = view(2560, HEADS, 512)
        kt_ = view(6656, HEADS, 512)
        vt = view(10752, 4, 512)
        pr = view(12800, 2, 2, 512)
        prt = view(14848, 2, 1024)
        rtmp = view(16896, 2, 2, 256)
        rsq = view(17920, 2, 512)
        ut = view(0, 4, 512)
        vg = view(2048, 4, 512)
        at = view(4096, 4, 512)
        vsq = view(6144, 512)
        mg = view(0, KT, 512)
        sgm = view(4096, 2, 3, 512)
        mring = view(8192, 4, 1024)
        crow = view(12288, 2, 1024)
        mprod = view(14336, 2, 1024)
        w13 = view(0, 2, KT, 1024)
        w2 = view(16384, 2, 4, 1024)
        hb = h[:, :, :].rearrange("p k t -> p (k t)")
        htok = y[:, 0:8, :].rearrange("p (n a) t -> p n (a t)", a=2)
        xg = [hb[:, u * 1024:(u + 1) * 1024] for u in range(2)]
        pk = [hb[:, 2048 + u * 512:2560 + u * 512].rearrange("p (n s) -> p n s", s=CAP) for u in range(2)]
        back = [hb[:, 3072 + u * 512:3584 + u * 512] for u in range(2)]
        het = [y[:, 8 + u, :] for u in range(2)]
        he = [y[:, 10 + u, :] for u in range(2)]
        ye = [rep[:, 2 * u:2 * u + 2, :] for u in range(2)]
        pkw = [t_.rearrange("p (n s) -> p n s", s=CAP) for t_ in (lora[:, 0, :], rt[:, :])]
        sil = [lora[:, 1 + u, :] for u in range(2)]
        slots = bs[:, 0, :]
        wsf = ws[:, :, :].rearrange("p g i -> p (g i)")
        score, sel, pick, first, second, comb, mask, place = \
            (wsf[:, 64 * i:64 * i + 64].rearrange("p (t e) -> p t e", e=NE) for i in range(8))
        x_final = {}

        loads = [q for l in range(DEPTH) for q in stream(l, w)]
        slot_of = {key: i % RING for i, (key, _, _) in enumerate(loads)}

        def t0_of(l):
            return CTX if l == DEPTH - 1 else 0

        def chunk_start(c, d):
            n = CTX // CH
            return CH * (c if d == 0 else c // n * n + n - 1 - c % n)

        def keep0(l, c):
            return l < DEPTH - 1 or c >= STEPS // 2


        def in_turn(make):
            flows = [make(s) for s in range(2)]
            done = False
            while not done:
                for f in flows:
                    done = next(f, True) is True

        def zb_share(l, i):
            n, i = NT - t0_of(l) // P, i - t0_of(l) // P
            return range(6 * i // n, 6 * (i + 1) // n)

        def attention_pairs(l):
            return [(s, hh) for hh in range(HEADS) for s in (range(2) if l < DEPTH - 1 else range(1, 2))]

        block = ctx.enter_context(nc.Block())

        @block.sync
        def _(sp):
            sp.dma_start(x[:, :, :], w["x"]).then_inc(*OUT("x_in", by=16))
            for dst, name in ((con[:, :, :], "con"), (small[:, :], "small"), (cs[64:P, :, :], "cs"), (rw[:, :, :], "rw"),
                              (rb[:, :], "rb"), (cc[:, :, :], "cc")):
                sp.dma_start(dst, w[name]).then_inc(*OUT("const_in", by=16))
            n = 0
            row = 0
            for l in range(DEPTH):
                while n < len(loads) and loads[n][0][1] == l:
                    key, src, size = loads[n]
                    if key == ("gate", 0, 0, 0):
                        sp.wait_ge(*GOT("yb_kept", 0, len(attention_pairs(0)) - 1))
                        sp.dma_start(crow, w["crow"]).then_inc(*OUT("crow_in", by=16))
                    if l == 0 and key[0] in ("gate", "up"):
                        for _ in range(MOD_ROWS // (5 * KT)):
                            if row >= 4:
                                sp.wait_ge(*GOT("mod_row_used", row - 4, 1))
                            sp.dma_start(mring[:, row % 4, :], w["mrow"][row]).then_inc(*OUT(f"mod_row_in{row % 4}", row, by=16))
                            row += 1
                    if n >= RING:
                        sp.wait_ge(*GOT("chunk_used", *loads[n - RING][0]))
                    sp.dma_start(ring[:, n % RING, 0:size], src).then_inc(*OUT(f"slot{n % RING}", *key, by=16))
                    n += 1
                    if key == (("mod", 0, 5) if l == 0 else ("zc", l, 3)):
                        if l:
                            sp.wait_ge(sg.sem(f"x_added{l - 1}"), x_final[l - 1, "sp"])
                            sp.wait_ge(sg.sem(f"slots_moved{l - 1}"), n_passes)
                        for dst, name in ((vec[:, :], "vec"), (rep[:, :, :], "rep"), (lora[:, :, :], "lora"),
                                          (bias2[:, :, :], "bias2"), (bs[:, :, :], "bs"), (ws[:, :, :], "ws")):
                            sp.dma_start(dst, w[name][l]).then_inc(*OUT("param_in", l, by=16))
                sp.wait_ge(*GOT(f"x_added{l}", KT - 1))
                sp.wait_ge(*GOT("norm_summed", l, 1))
                pairs13 = w["w13"][l].rearrange("(i u) p k n -> i u p k n", u=2)
                pairs2 = w["w2"][l].rearrange("(i u) p k n -> i u p k n", u=2)

                def load_pair(i, used):
                    for u in range(2):
                        if used is not None:
                            sp.wait_ge(sg.sem(f"y_done{l}"), used + u)
                        sp.dma_start(w13[:, u, :, :], pairs13[i, u]).then_inc(sg.sem(f"w13_in{u}{l}"), 16)
                        sp.dma_start(w2[:, u, :, :], pairs2[i, u]).then_inc(sg.sem(f"w2_in{u}{l}"), 16)

                load_pair(0, None)
                with sp.Fori(0, PAIRS - 1, 1) as i:
                    load_pair(i + 1, i * 2 + 1)
                sp.wait_ge(*GOT("passes_set", l))
                n_passes = sp.value_load(passes[0:1, 0:1], min_val=1, max_val=TOK // CAP)
                x_final[l, "sp"] = n_passes * (PAIRS * KT) + KT
                with sp.If(n_passes > 1):
                    with sp.Fori(0, n_passes - 1, 1) as p:
                        with sp.Fori(0, PAIRS, 1) as i:
                            load_pair(i, p * NE + i * 2 + (NE - 1))
            sp.wait_ge(*GOT("out_ready",))
            sp.dma_start(out, h[:, :, 0:LAT]).then_inc(*OUT("out_stored", by=16))
            sp.wait_ge(*GOT("out_stored"))

        @block.tensor
        def _(pe):
            def weights(*key):
                pe.wait_ge(*GOT(f"slot{slot_of[key]}", *key))
                return ring[:, slot_of[key], :]

            def norm(l, which):
                t0 = 0 if l < DEPTH and which == 0 else CTX if l == DEPTH else t0_of(l)
                if which == 1:
                    pe.wait_ge(*GOT(f"x_added{l}", KT - 1))
                for k in range(KT):
                    pe.wait_ge(*GOT("squared", l, which, k))
                    mm = pe.matmul(ps[:, 7, t0:], C(C_ONE), sq[:, k, t0:], start=(k == 0), stop=(k == KT - 1))
                mm.then_inc(*OUT("norm_summed", l, which))

            def full(dst, wt, rhs, n, t0):
                for k in range(n):
                    mm = pe.matmul(dst, wt[:, k * P:(k + 1) * P], rhs[:, k, t0:TOK], start=(k == 0), stop=(k == n - 1))
                return mm

            def modulation(l):
                pe.wait_ge(*GOT("cond_ready"))
                pe.wait_ge(*GOT("const_in"))
                for n in range(4):
                    if n >= 2:
                        pe.wait_ge(*GOT("mod_row", l, n - 2))
                    for q in range(4):
                        wt = weights("mod", l, 4 * n + q)
                        for i in range(2):
                            k = 2 * q + i
                            mm = pe.matmul(ps[0:2, 1 + n % 2, :], ca[:, k, :], wt[:, i * 512:(i + 1) * 512],
                                           start=(k == 0), stop=(k == KT - 1))
                        mm.then_inc(*OUT("chunk_used", "mod", l, 4 * n + q))
                for j in range(16):
                    if j % 4 == 0:
                        pe.wait_ge(*GOT("mod_row", l, j // 4))
                    mm = pe.transpose(ps[:, 0, 2 * j:2 * j + 2], y[0:2, j // 4, j % 4 * P:(j % 4 + 1) * P], con[0:2, C_ID, 0:2])
                mm.then_inc(*OUT("mod_turned", l))

            def rwkv_inputs(l):
                pe.wait_ge(*GOT("param_in", l))
                pe.wait_ge(*GOT("h_done", l, 0))
                pe.wait_ge(*GOT("mod_ready", l))
                for i in range(15):
                    wt = weights("zc", l, i)
                    if i >= 2:
                        pe.wait_ge(*GOT("raw_copied", l, i - 2))
                    full(ps[:, i % 2, :], wt, h, KT, 0).then_inc(*OUT("chunk_used", "zc", l, i))
                    f = i - KK_AT - 1
                    if 0 <= f < 4:
                        pe.wait_ge(*GOT("kk_squared", l, f))
                        pe.matmul(ps[:, 2 + f % 2, :], C(C_BONE), kks[:, f % 2, :], start=True, stop=True) \
                            .then_inc(*OUT("kk_summed", l, f))

            def rwkv_flow(l, s):
                for c in range(STEPS):
                    yield from rwkv_step(l, c, s)
                    for u in range(HS // HU):
                        yield from rwkv_unit(l, c, s, u)

            def rwkv_step(l, c, s):
                k = (l, c, s)
                t = units[s]
                A, B, C_, D_ = (t.bank + i for i in range(4))
                pe.wait_ge(*GOT("staged", *k, 1))
                if c:
                    pe.wait_ge(*GOT("state_new", l, c - 1, s, 1))
                    if keep0(l, c - 1):
                        pe.wait_ge(*GOT("o_kept", l, c - 1, s, 1))
                else:
                    pe.wait_ge(*GOT("kk_done", l, 3))
                for q in range(4):
                    for f in range(2):
                        a = q % 2 * 256 + f * P
                        mm = pe.transpose(ps[:, A + q // 2, a:a + P], t.stage[:, 2 * q + f, :], C(C_ID))
                mm.then_inc(*OUT("tokens_turned", *k))
                pe.wait_ge(*GOT("lora_in", *k, 1))
                own = slice(s * 256, (s + 1) * 256)
                for q in range(2):
                    o = ps[:, C_, q * 256:(q + 1) * 256]
                    pe.matmul(o, t.low[q], lora[:, q, own], start=True, stop=False)
                    mm = pe.matmul(o, small[0:2, 2:2 + P], bias2[:, q, own], start=False, stop=True)
                mm.then_inc(*OUT("logits", *k))
                yield
                pe.wait_ge(*GOT("sig_done", *k))
                pe.matmul(ps[:, D_, 0:256], C(C_MI), t.tok[0], start=True, stop=True)
                pe.matmul(ps[:, D_, 256:512], C(C_MS), t.tok[0], start=True, stop=True)
                for hh in range(HS):
                    for d in range(2):
                        mm = pe.matmul(ps[d * HD:(d + 1) * HD, C_, hh:hh + 1], t.tok[0][:, hh * HD:(hh + 1) * HD],
                                       small[:, d:d + 1], start=True, stop=True)
                mm.then_inc(*OUT("cums", *k))
                yield

            def rwkv_unit(l, c, s, u):
                k = (l, c, s, u)
                t = units[s]
                A, B, C_, D_ = (t.bank + i for i in range(4))
                h0 = s * HS + u * HU

                def each(bank, lhs, rhs, name):
                    for i in range(HU):
                        mm = pe.matmul(ps[:, bank, i * P:(i + 1) * P], lhs[:, i, :], rhs[:, i, :], start=True, stop=True)
                    mm.then_inc(*OUT(name, *k))

                pe.wait_ge(*GOT("ar_in", *k, 1, 1))
                pe.wait_ge(*GOT("bg_in", *k, 2 if u else 1, 1))
                if u == 0:
                    pe.wait_ge(*GOT("operand", l, c, s, 1))
                    pe.wait_ge(*GOT("exps", l, c, s, 3))
                else:
                    pe.wait_ge(*GOT("state_new", l, c, s, 0))
                    if keep0(l, c):
                        pe.wait_ge(*GOT("o_kept", l, c, s, 0))
                for i in range(HU):
                    pe.transpose(ps[:, A, 2 * i * P:(2 * i + 1) * P], t.ma[:, i, :], C(C_ID))
                    pe.transpose(ps[:, A, (2 * i + 1) * P:(2 * i + 2) * P], t.mr[:, i, :], C(C_ID))
                    pe.transpose(ps[:, B, i * P:(i + 1) * P], t.mbs[u][:, i, :], C(C_ID))
                    mm = pe.transpose(ps[:, B, (2 + i) * P:(3 + i) * P], t.mgs[u][:, i, :], C(C_ID))
                mm.then_inc(*OUT("turned", *k))
                yield
                pe.wait_ge(*GOT("ar_kept", *k))
                pe.wait_ge(*GOT("bg_kept", *k))
                for i in range(HU):
                    pe.matmul(ps[:, A, i * P:(i + 1) * P], t.ar[:, i, 0:P], t.b[:, i, :], start=True, stop=True)
                for q, src in enumerate((t.b, t.g)):
                    for i in range(HU):
                        mm = pe.matmul(ps[:, C_ + q, i * 256:i * 256 + 256], src[:, i, :], t.ar[:, i, :], start=True, stop=True)
                mm.then_inc(*OUT("gram", *k))
                yield
                pe.wait_ge(*GOT("masked", *k, 1))
                each(B, t.n, t.nt, "p_nt2")
                each(A, t.nt, t.n, "p_n2")
                yield
                pe.wait_ge(*GOT("nt2_kept", *k))
                pe.wait_ge(*GOT("n2_kept", *k))
                each(A, t.b, t.g, "p_n4")
                each(B, t.g, t.b, "p_nt4")
                pe.wait_ge(*GOT("masked", *k, 2))
                each(C_, t.g, t.nt, "p_nt3")
                yield
                pe.wait_ge(*GOT("nt4_kept", *k))
                each(D_, t.nt4, t.n4, "p_n8")
                pe.wait_ge(*GOT("x2_done", *k))
                each(C_, t.n4, t.ma, "p_x4")
                yield
                pe.wait_ge(*GOT("n8_kept", *k))
                pe.wait_ge(*GOT("x4_done", *k))
                each(B, t.n8, t.mr, "p_x8")
                yield
                pe.wait_ge(*GOT("xt_done", *k))
                each(C_, t.go, t.xt, "p_ht")
                each(A, t.xt, t.go, "p_h")
                for i in range(HU):
                    mm = pe.transpose(ps[:, D_, i * P:(i + 1) * P], t.xt[:, i, :], C(C_ID))
                mm.then_inc(*OUT("p_x", *k))
                yield
                pe.wait_ge(*GOT("h_kept", *k))
                pe.wait_ge(*GOT("ht_kept", *k))
                each(A, t.n, t.nt, "p_ht2")
                yield
                pe.wait_ge(*GOT("ht2_kept", *k))
                each(C_, t.n, t.n4, "p_ht3")
                if c == 0:
                    pe.wait_ge(*GOT("state_clear", l))
                for i in range(HU):
                    o = ps[:, A, i * HD:(i + 1) * HD]
                    pe.matmul(o, t.ar[:, i, 0:P], state[:, h0 + i, :], start=True, stop=False)
                    mm = pe.matmul(o, t.bt[:, i, :], t.v[:, u * HU + i, :], start=False, stop=True)
                mm.then_inc(*OUT("p_r", *k))
                yield
                pe.wait_ge(*GOT("w_done", *k))
                pe.wait_ge(*GOT("x_kept", *k))
                each(D_, t.x, t.nt4, "p_tt")
                yield
                pe.wait_ge(*GOT("tt_kept", *k))
                pe.wait_ge(*GOT("r_kept", *k))
                for i in range(HU):
                    mm = pe.matmul(ps[:, D_, i * HD:(i + 1) * HD], t.n8[:, i, :], t.nt[:, i, 0:HD], start=True, stop=True)
                mm.then_inc(*OUT("p_u", *k))
                yield
                pe.wait_ge(*GOT("u_kept", *k))
                if keep0(l, c):
                    for i in range(HU):
                        o = ps[:, B, i * HD:(i + 1) * HD]
                        pe.matmul(o, t.ar[:, i, P:2 * P], state[:, h0 + i, :], start=True, stop=False)
                        pe.matmul(o, t.qb[:, i, :], t.nt[:, i, HD:P], start=False, stop=False)
                        mm = pe.matmul(o, t.qg[:, i, :], t.v[:, u * HU + i, :], start=False, stop=True)
                    mm.then_inc(*OUT("p_o", *k))
                for i in range(HU):
                    o = ps[:, C_, i * HD:(i + 1) * HD]
                    pe.matmul(o, t.mbs[u][:, i, :], t.nt[:, i, HD:P], start=True, stop=False)
                    mm = pe.matmul(o, t.mgs[u][:, i, :], t.v[:, u * HU + i, :], start=False, stop=True)
                mm.then_inc(*OUT("p_s", *k))
                yield

            def rwkv_readout(l):
                pe.wait_ge(*GOT("zg_done", l))
                for i in range(t0_of(l) // P, NT):
                    n = CTX // CH
                    if i > t0_of(l) // P:
                        pe.wait_ge(*GOT("yc_kept", l, i - 1))
                    else:
                        for s in range(2):
                            pe.wait_ge(*GOT("o_kept", l, STEPS - 1, s, 1))
                            pe.wait_ge(*GOT("state_new", l, STEPS - 1, s, 1))
                    parts = []
                    for half in range(2):
                        j = 2 * i + half
                        parts.append((0, half, j))
                        parts.append((1, half, j // n * n + n - 1 - j % n))
                    for bank, a, b in ((0, 0, CW), (1, CW, CW + HEADS)):
                        for q, (d, half, c) in enumerate(parts):
                            pe.matmul(ps[:, bank, 0:b - a], C(C_S00 + 2 * d + half), osb[:, c, a:b],
                                      start=(q == 0), stop=(q == 3))
                    for f in range(4):
                        pe.transpose(ps[:, 2, f * P:(f + 1) * P], zc[:, ZV + f, i * P:(i + 1) * P], C(C_ID))
                    pe.matmul(ps[:, 3, :], zc[:, ZG, i * P:(i + 1) * P], lora[:, 2, :], start=True, stop=True) \
                        .then_inc(*OUT("read", l, i))
                    for j in zb_share(l, i):
                        wt = weights("zb", l, j)
                        if j >= 2:
                            pe.wait_ge(*GOT("zb_kept", l, j - 2))
                        full(ps[:, 5 + j % 2, :], wt, h, KT, 0).then_inc(*OUT("chunk_used", "zb", l, j))
                    pe.wait_ge(*GOT("yc_done", l, i))
                    for f in range(4):
                        mm = pe.transpose(ps[:, 4, f * P:(f + 1) * P], tok[:, 0, f * P:(f + 1) * P], C(C_ID))
                    mm.then_inc(*OUT("yc_turned", l, i))

            def attention_inputs(l):
                t0 = t0_of(l)
                pe.wait_ge(*GOT("yc_kept", l, NT - 1))
                for i in range(5):
                    pe.wait_ge(*GOT("zb_squared", l, i))
                    mm = pe.matmul(ps[:, 2 if i < 3 else 3, :], C(C_ONE), rsq[:, i % 2, :],
                                   start=(i in (0, 3)), stop=(i in (2, 4)))
                    mm.then_inc(*OUT("zb_summed", l, i))
                for i in range(5):
                    pe.wait_ge(*GOT("zb_scaled", l, i))
                n = 0
                for i in range(4):
                    wt = weights("uq", l, i)
                    for j in range(2):
                        hh = 2 * i + j
                        bank = 4 + hh % 2
                        if hh >= 2:
                            pe.wait_ge(*GOT("q_kept", l, hh - 2))
                            pe.wait_ge(*GOT("q_roped", l, hh - 2))
                        for k in range(3):
                            mm = pe.matmul(ps[:, bank, t0:TOK], wt[:, (j * 3 + k) * P:(j * 3 + k + 1) * P], zq[:, k, t0:TOK],
                                           start=(k == 0), stop=(k == 2))
                        mm.then_inc(*(OUT("q_made", l, hh) if j == 0 else OUT("chunk_used", "uq", l, i)))
                wt = weights("uk", l, 0)
                for hh in range(HEADS):
                    if hh >= 2:
                        pe.wait_ge(*GOT("k_kept", l, hh - 2))
                    else:
                        pe.wait_ge(*GOT("q_kept", l, 6 + hh))
                        pe.wait_ge(*GOT("kr_spread", l))
                    for k in range(2):
                        mm = pe.matmul(ps[0:HD, 6 + hh % 2, :], wt[:, (hh * 2 + k) * HD:(hh * 2 + k + 1) * HD], zq[:, 3 + k, :],
                                       start=(k == 0), stop=(k == 1))
                    mm.then_inc(*(OUT("k_made", l, hh) if hh < HEADS - 1 else OUT("chunk_used", "uk", l, 0)))
                wt = weights("uv", l, 0)
                pe.wait_ge(*GOT("kr_spread", l))
                pe.wait_ge(*GOT("zb_rooted", l, 1))
                for i in range(NT):
                    for k in range(2):
                        mm = pe.matmul(ps[:, i, :], zq[:, 3 + k, i * P:(i + 1) * P], wt[:, k * 512:(k + 1) * 512],
                                       start=(k == 0), stop=(k == 1))
                    mm.then_inc(*(OUT("v_made", l, i) if i < NT - 1 else OUT("chunk_used", "uv", l, 0)))

            def attention(l):
                pairs = attention_pairs(l)

                def scores(n):
                    s, hh = pairs[n]
                    nk = 4 if s else 2
                    if n >= 2:
                        pe.wait_ge(*GOT("prob", l, n - 2, 1))
                    elif n == 0:
                        pe.wait_ge(*GOT("v_stored", l, NT - 1))
                        pe.wait_ge(*GOT("k_kept", l, HEADS - 1))
                        pe.wait_ge(*GOT("q_kept", l, HEADS - 1))
                        pe.wait_ge(*GOT("q_roped", l, HEADS - 1))
                    for q in range(2):
                        tt = s * CTX + q * P
                        mm = pe.matmul(ps[:, n % 2 * 2 + q, 0:nk * P], qt[0:QK, hh, tt:tt + P], kt_[0:QK, hh, 0:nk * P],
                                       start=True, stop=True)
                    mm.then_inc(*OUT("scores", l, n))

                def turn(n):
                    nk = 4 if pairs[n][0] else 2
                    pe.wait_ge(*GOT("prob_scaled", l, n, 1))
                    if n >= 1:
                        pe.wait_ge(*GOT("pt_kept", l, n - 1))
                    for kk in range(nk):
                        for q in range(2):
                            mm = pe.transpose(ps[:, 4 + kk // 2, kk % 2 * 256 + q * P:kk % 2 * 256 + (q + 1) * P],
                                              pr[:, n % 2, q, kk * P:(kk + 1) * P], C(C_ID))
                    mm.then_inc(*OUT("prob_turned", l, n))

                def attend(n):
                    s, hh = pairs[n]
                    nk = 4 if s else 2
                    pe.wait_ge(*GOT("pt_kept", l, n))
                    if n >= 2:
                        pe.wait_ge(*GOT("yb_kept", l, n - 2))
                    for kk in range(nk):
                        mm = pe.matmul(ps[hh % 2 * HD:hh % 2 * HD + HD, 6 + n % 2, 0:256], vt[:, kk, hh * VD:(hh + 1) * VD],
                                       prt[:, n % 2, kk * 256:(kk + 1) * 256], start=(kk == 0), stop=(kk == nk - 1))
                    mm.then_inc(*OUT("attended", l, n))

                scores(0)
                for n in range(len(pairs)):
                    if n + 1 < len(pairs):
                        scores(n + 1)
                    turn(n)
                    if n:
                        attend(n - 1)
                attend(len(pairs) - 1)

            def gmlp(l):
                t0 = t0_of(l)
                pe.wait_ge(*GOT("yb_kept", l, len(attention_pairs(l)) - 1))
                pe.wait_ge(*GOT("yb_kept", l, len(attention_pairs(l)) - 2))
                for i in range(4):
                    wt = weights("zu", l, i)
                    if i >= 2:
                        pe.wait_ge(*GOT("u_gelu", l, i - 2))
                    full(ps[:, 4 + i % 2, t0:TOK], wt, h, KT, t0).then_inc(*OUT("chunk_used", "zu", l, i))
                for i in range(4):
                    wt = weights("zv", l, i)
                    for k in range(2):
                        for t in range(t0 // P, NT):
                            mm = pe.matmul(ps[:, t, :], h[:, 2 * i + k, t * P:(t + 1) * P], wt[:, k * 512:(k + 1) * 512],
                                           start=(i == 0 and k == 0), stop=(i == 3 and k == 1))
                    mm.then_inc(*OUT("chunk_used", "zv", l, i))
                pe.wait_ge(*GOT("v_normed", l, NT - 1))
                pe.wait_ge(*GOT("u_gelu", l, 3))
                for g in range(4):
                    for t in range(t0 // P, NT):
                        mm = pe.matmul(ps[:, 4 + g, t * P:(t + 1) * P], vg[:, t, g * P:(g + 1) * P], ws[:, g, :],
                                       start=True, stop=True)
                    mm.then_inc(*OUT("mixed", l, g))

            def merge(l):
                t0 = t0_of(l)
                pe.wait_ge(*GOT("ya_done", l, 3))
                pe.wait_ge(*GOT("v_normed", l, NT - 1))
                for j in range(KT):
                    for g in range(3):
                        wt = weights("gate", l, j, g)
                        if j:
                            pe.wait_ge(*GOT("gated", l, j - 1, g))
                        full(ps[:, g, t0:TOK], wt, h, KT, t0).then_inc(*OUT("chunk_used", "gate", l, j, g))
                    for g in range(3):
                        if g != 1:
                            wt = weights("up", l, j, g // 2)
                        at_ = 512 * g if g < 2 else 0
                        if j:
                            pe.wait_ge(*GOT("merged", l, j - 1, 4))
                        for k in range(4):
                            mm = pe.matmul(ps[:, 3 + g, t0:TOK], wt[:, at_ + k * P:at_ + (k + 1) * P], y[:, 4 * g + k, t0:TOK],
                                           start=(k == 0), stop=(k == 3))
                        if g:
                            mm.then_inc(*OUT("chunk_used", "up", l, j, g // 2))
                pe.wait_ge(*GOT("merged", l, KT - 1, 4))
                for j in range(KT):
                    wt = weights("wo", l, j)
                    if j >= 2:
                        pe.wait_ge(*GOT(f"x_added{l}", j - 2))
                    full(ps[:, 6 + j % 2, t0:TOK], wt, mg, KT, t0).then_inc(*OUT("chunk_used", "wo", l, j))

            def router(l):
                t0 = t0_of(l)
                pe.wait_ge(*GOT("h_done", l, 1))
                for t in range(t0 // P, NT):
                    for k in range(KT):
                        mm = pe.matmul(ps[:, 6, t * NE:(t + 1) * NE], h[:, k, t * P:(t + 1) * P], rw[:, k, :],
                                       start=(k == 0), stop=(k == KT - 1))
                mm.then_inc(*OUT("routed", l))
                for t in range(t0 // P, NT):
                    if t >= t0 // P + 2:
                        pe.wait_ge(*GOT("row_kept", l, t - 2))
                    for f in range(KT):
                        b = t % 2 * 2 + f // 4
                        mm = pe.transpose(ps[:, b, f % 4 * P:(f % 4 + 1) * P], h[:, f, t * P:(t + 1) * P], C(C_ID))
                    mm.then_inc(*OUT("row_turned", l, t))
                pe.wait_ge(*GOT("mask_done", l))
                a = t0 // P
                for t in range(a, NT):
                    for i in range(a, t + 1):
                        pe.matmul(ps[:, 6, 64 + t * NE:64 + (t + 1) * NE], C(C_ONE if i < t else C_TRI), mask[:, i, :],
                                  start=(i == a), stop=(i == t))
                for i in range(a, NT):
                    mm = pe.matmul(ps[:, 6, 128:128 + NE], C(C_ONE), mask[:, i, :], start=(i == a), stop=(i == NT - 1))
                mm.then_inc(*OUT("placed", l))

            def experts(l):
                t0 = t0_of(l)
                tiles = range(t0 // P, NT)

                def S(name):
                    return sg.sem(f"{name}{l}")

                def gather(u, n):
                    pe.wait_ge(S("picks"), n + (u + 1))
                    if u:
                        pe.wait_ge(S("xg_kept"), n + 1)
                    for f in range(KT):
                        for t in tiles:
                            mm = pe.matmul(ps[:, f // 4, f % 4 * P:(f % 4 + 1) * P], htok[:, t, f * P:(f + 1) * P],
                                           pk[u][:, t, :], start=(t == tiles[0]), stop=(t == NT - 1))
                    mm.then_inc(S("gathered"), 1)

                def up(u, n, j_loads):
                    pe.wait_ge(S("xg_kept"), n + (u + 1))
                    pe.wait_ge(S(f"w13_in{u}"), j_loads)
                    if u:
                        pe.wait_ge(S("he_done"), n + 1)
                    for q in range(2):
                        for k in range(KT):
                            mm = pe.matmul(ps[:, 3 + q, :], xg[u][:, k * P:(k + 1) * P],
                                           w13[:, u, k, q * 512:(q + 1) * 512], start=(k == 0), stop=(k == KT - 1))
                    mm.then_inc(S("h13_done"), 1)

                def turn_back(u, n):
                    pe.wait_ge(S("weighted"), n + (u + 1))
                    if u:
                        pe.wait_ge(S("back_kept"), n + 1)
                    for t in tiles:
                        mm = pe.transpose(ps[:, 7, t * P:(t + 1) * P], pkw[u][:, t, :], C(C_ID))
                    mm.then_inc(S("turned_back"), 1)

                def turn_he(u, n):
                    pe.wait_ge(S("he_done"), n + (u + 1))
                    if u:
                        pe.wait_ge(S("back_kept"), n + 2)
                    for k in range(4):
                        mm = pe.transpose(ps[:, (2, 7)[u], k * P:(k + 1) * P], he[u][:, k * P:(k + 1) * P], C(C_ID))
                    mm.then_inc(S("he_turned"), 1)

                def down(u, n, j_loads):
                    pe.wait_ge(S("het_kept"), n + (u + 1))
                    pe.wait_ge(S(f"w2_in{u}"), j_loads)
                    for q in range(2):
                        for k in range(4):
                            mm = pe.matmul(ps[:, (5, 3)[u] + q, :], het[u][:, k * P:(k + 1) * P],
                                           w2[:, u, k, q * 512:(q + 1) * 512], start=(k == 0), stop=(k == 3))
                    mm.then_inc(S("y_done"), 1)

                def pair(n, m, j_loads, following):
                    pe.wait_ge(S("x_added"), m * KT + (KT - 2))
                    up(0, n, j_loads)
                    turn_back(0, n)
                    up(1, n, j_loads)
                    turn_he(0, n)
                    turn_back(1, n)
                    if following:
                        gather(0, n + 2)
                    turn_he(1, n)
                    pe.wait_ge(S("x_added"), m * KT + KT)
                    down(0, n, j_loads)
                    down(1, n, j_loads)
                    if following:
                        gather(1, n + 2)
                    pe.wait_ge(S("ye_kept"), n + 2)
                    for d in range(KT):
                        if d >= 4:
                            pe.wait_ge(S("x_added"), m * KT + (KT + d - 3))
                        for u in range(2):
                            mm = pe.matmul(ps[:, 3 + d % 4, t0:TOK], ye[u][:, d // 4, d % 4 * P:(d % 4 + 1) * P],
                                           back[u][:, t0:TOK], start=(u == 0), stop=(u == 1))
                        mm.then_inc(S("scattered"), 1)

                pe.wait_ge(*GOT("passes_set", l))
                pe.wait_ge(*GOT("row_kept", l, NT - 1))
                n_passes = pe.value_load(passes[0:1, 0:1], min_val=1, max_val=TOK // CAP)
                with pe.Fori(0, n_passes, 1) as p:
                    for u in range(2):
                        gather(u, p * NE)
                    with pe.Fori(0, PAIRS - 1, 1) as j:
                        m = pe.snap(p * PAIRS + j)
                        pair(pe.snap(m * 2), m, m * 16 + 16, True)
                    last = pe.snap(p * PAIRS + (PAIRS - 1))
                    pair(pe.snap(last * 2), last, last * 16 + 16, False)

            for l in range(DEPTH):
                if l == 0:
                    modulation(l)
                norm(l, 0)
                rwkv_inputs(l)
                in_turn(lambda s: rwkv_flow(l, s))
                rwkv_readout(l)
                attention_inputs(l)
                attention(l)
                gmlp(l)
                merge(l)
                norm(l, 1)
                router(l)
                experts(l)
            norm(DEPTH, 0)

        @block.scalar
        def _(act):
            def A_(o, i, f, **kw):
                return act.activation(o, i, f, **kw)

            def norm(l, which):
                t0 = 0 if l < DEPTH and which == 0 else CTX if l == DEPTH else t0_of(l)
                for k in range(KT):
                    if which == 1:
                        act.wait_ge(*GOT(f"x_added{l}", k))
                        if k == 0:
                            act.wait_ge(*GOT("chunk_used", "wo", l, KT - 1))
                    elif l:
                        act.wait_ge(sg.sem(f"x_added{l - 1}"), x_final[l - 1, "act"])
                    else:
                        act.wait_ge(*GOT("x_in"))
                    A_(sq[:, k, t0:], x[:, k, t0:], ACT.Square).then_inc(*OUT("squared", l, which, k))
                act.wait_ge(*GOT("norm_summed", l, which))
                act.wait_ge(*GOT("eps_set"))
                A_(rt[:, t0:], ps[:, 7, t0:], ACT.Sqrt, bias=eps[:, 0:1], scale=1.0 / D).then_inc(*OUT("norm_rooted", l, which))
                if l == DEPTH:
                    return
                for k in range(KT):
                    act.wait_ge(*GOT("x_scaled", l, which, k))
                    for s in range(t0 // CTX, 2):
                        v = h[:, k, s * CTX:(s + 1) * CTX]
                        ins = A_(v, v, ACT.Identity, scale=gain[:, which, k, s:s + 1],
                                bias=mod[:, 24 * which + k, s:s + 1])
                        ins.then_inc(*(OUT("h_done", l, which) if k == KT - 1 and s == 1 else OUT("h_part", l, which, k, s)))

            def copy(o, i):
                return A_(o, i, ACT.Copy)

            def rwkv_inputs(l):
                for i in range(15):
                    act.wait_ge(*GOT("chunk_used", "zc", l, i))
                    if i == 0:
                        act.wait_ge(*GOT("raw_clear", l))
                    if i >= 2:
                        act.wait_ge(*GOT("z_mixed", l, i - 2))
                    copy(raw[:, i % 2, :, 1:257], ps[:, i % 2, :].rearrange("p (s t) -> p s t", s=2)) \
                        .then_inc(*OUT("raw_copied", l, i))
                    f = i - KK_AT - 1
                    if 0 <= f < 4:
                        act.wait_ge(*GOT("kk_clamped", l, f))
                        A_(kks[:, f % 2, :], kks[:, f % 2, :], ACT.Sqrt).then_inc(*OUT("kk_rooted", l, f))

            def rwkv_flow(l, s):
                for c in range(STEPS):
                    yield from rwkv_step(l, c, s)
                    for u in range(HS // HU):
                        yield from rwkv_unit(l, c, s, u)

            def rwkv_step(l, c, s):
                k = (l, c, s)
                t = units[s]
                A, B, C_, D_ = (t.bank + i for i in range(4))
                if c == 0:
                    act.wait_ge(*GOT("lora_clear", l))
                    act.wait_ge(*GOT("z_mixed", l, 13))
                else:
                    act.wait_ge(*GOT("logits", l, c - 1, s))
                for q in range(2):
                    for d in range(2):
                        a = chunk_start(c, d)
                        r = slice(d * 64, d * 64 + 64)
                        A_(t.low[q][r, d * 64:d * 64 + 64], zc[r, ZW + q, a:a + 64], ACT.Tanh if q == 0 else ACT.Copy) \
                            .then_inc(*OUT("lora_in", *k, q))
                if c:
                    act.wait_ge(*GOT("bonus_kept", l, c - 1, s))
                act.wait_ge(*GOT("logits", *k))
                for q in range(2):
                    A_(t.tok[q], ps[:, C_, q * 256:(q + 1) * 256], ACT.Tanh, scale=0.5).then_inc(*OUT("tanhed", *k, q))
                yield
                act.wait_ge(*GOT("cums", *k))
                if c:
                    act.wait_ge(*GOT("ar_in", l, c - 1, s, 1, 1, 1))
                    act.wait_ge(*GOT("bg_in", l, c - 1, s, 1, 2, 1))
                    act.wait_ge(*GOT("state_new", l, c - 1, s, 1))
                A_(t.tok[2], ps[:, D_, 0:256], ACT.Exp, scale=-DECAY).then_inc(*OUT("exps", *k, 0))
                A_(t.tok[3], ps[:, D_, 256:512], ACT.Exp, scale=-DECAY).then_inc(*OUT("exps", *k, 1))
                A_(t.tok[4], ps[:, D_, 0:256], ACT.Exp, scale=DECAY).then_inc(*OUT("exps", *k, 2))
                A_(t.end, ps[:, C_, 0:HS], ACT.Exp, scale=-DECAY).then_inc(*OUT("exps", *k, 3))
                yield

            def rwkv_unit(l, c, s, u):
                k = (l, c, s, u)
                t = units[s]
                A, B, C_, D_ = (t.bank + i for i in range(4))
                prev = (l, c, s, 0) if u else (l, c - 1, s, 1)

                def keep(name, src, bank, dst):
                    act.wait_ge(*GOT(src, *k))
                    copy(dst, ps[:, bank, 0:HU * P].rearrange("p (h t) -> p h t", t=P)).then_inc(*OUT(name, *k))
                def blocks(u, q):
                    m, i, made = ((t.mbs[u], 6, 0), (t.mgs[u], 7, 1), (t.ma, 3, 2))[q]
                    act.wait_ge(*GOT("operand", l, c, s, made))
                    for d in range(2):
                        r = slice(d * CH, (d + 1) * CH)
                        copy(m[r, :, d * HD:(d + 1) * HD], t.tok[i][r, u * P:(u + 1) * P].rearrange("p (h v) -> p h v", v=HD)) \
                            .then_inc(*OUT("bg_in", l, c, s, u, q, d))
                if u == 0:
                    if c:
                        act.wait_ge(*GOT("p_s", l, c - 1, s, 0))
                        act.wait_ge(*GOT("xt_done", *prev))
                    for q in (2, 0, 1):
                        blocks(0, q)
                act.wait_ge(*GOT("turned", *k))
                copy(t.ar, ps[:, A, :].rearrange("p (h t) -> p h t", t=2 * P)).then_inc(*OUT("ar_kept", *k))
                yield
                if u == 0:
                    blocks(1, 0)
                yield
                keep("n2_kept", "p_n2", A, t.g)
                yield
                keep("n4_kept", "p_n4", A, t.n4)
                keep("nt4_kept", "p_nt4", B, t.nt4)
                yield
                keep("n8_kept", "p_n8", D_, t.n8)
                yield
                if u == 0:
                    blocks(1, 1)
                yield
                keep("h_kept", "p_h", A, t.n)
                keep("x_kept", "p_x", D_, t.x)
                yield
                keep("ht2_kept", "p_ht2", A, t.n4)
                yield
                act.wait_ge(*GOT("p_r", *k))
                act.wait_ge(*GOT("w_done", *k))
                A_(t.nt[:, :, 0:HD], ps[:, A, 0:HU * HD].rearrange("p (h v) -> p h v", v=HD), ACT.Copy, scale=-1.0) \
                    .then_inc(*OUT("r_kept", *k))
                yield
                keep("tt_kept", "p_tt", D_, t.n8)
                if u == 0:
                    act.wait_ge(*GOT("xt_done", *k))
                    blocks(1, 2)
                yield
                act.wait_ge(*GOT("p_u", *k))
                copy(t.nt[:, :, HD:P], ps[:, D_, 0:HU * HD].rearrange("p (h v) -> p h v", v=HD)).then_inc(*OUT("u_kept", *k))
                yield
                if keep0(l, c):
                    act.wait_ge(*GOT("p_o", *k))
                    a = (s * HS + u * HU) * HD
                    copy(osb[:, c, a:a + HU * HD], ps[:, B, 0:HU * HD]).then_inc(*OUT("o_kept", *k))
                yield

            def rwkv_readout(l):
                A_(zc[:, ZG, :], zc[:, ZG, :], ACT.Sigmoid).then_inc(*OUT("zg_done", l))
                for i in range(t0_of(l) // P, NT):
                    act.wait_ge(*GOT("var_done", l, i))
                    A_(st[:, 16:24], st[:, 16:24], ACT.Sqrt, bias=eps[:, 1:2], scale=1.0 / HD).then_inc(*OUT("var_rooted", l, i))
                    for j in zb_share(l, i):
                        if j < 5:
                            act.wait_ge(*GOT("chunk_used", "zb", l, j))
                            copy(zq[:, j, :], ps[:, 5 + j % 2, :]).then_inc(*OUT("zb_kept", l, j))
                    act.wait_ge(*GOT("yc_turned", l, i))
                    copy(y[:, 8:12, i * P:(i + 1) * P], ps[:, 4, :].rearrange("p (f t) -> p f t", t=P)) \
                        .then_inc(*OUT("yc_kept", l, i))

            def attention_inputs(l):
                t0 = t0_of(l)
                for i in range(5):
                    act.wait_ge(*GOT("zb_kept", l, i))
                    if i >= 2:
                        act.wait_ge(*GOT("zb_summed", l, i - 2))
                    A_(rsq[:, i % 2, :], zq[:, i, :], ACT.Square).then_inc(*OUT("zb_squared", l, i))
                for i, (bank, n) in enumerate(((2, QL), (3, KVL))):
                    act.wait_ge(*GOT("zb_summed", l, 2 if i == 0 else 4))
                    A_(pr[:, 0, i, :], ps[:, bank, :], ACT.Sqrt, bias=eps[:, 0:1], scale=1.0 / n).then_inc(*OUT("zb_rooted", l, i))
                for hh in range(HEADS):
                    act.wait_ge(*(GOT("q_made", l, hh) if hh % 2 == 0 else GOT("chunk_used", "uq", l, hh // 2)))
                    copy(qt[0:64, hh, t0:], ps[0:64, 4 + hh % 2, t0:]).then_inc(*OUT("q_kept", l, hh))
                for hh in range(HEADS):
                    act.wait_ge(*(GOT("k_made", l, hh) if hh < HEADS - 1 else GOT("chunk_used", "uk", l, 0)))
                    copy(kt_[0:64, hh, :], ps[0:64, 6 + hh % 2, :]).then_inc(*OUT("k_kept", l, hh))
                for i in range(NT):
                    act.wait_ge(*(GOT("v_made", l, i) if i < NT - 1 else GOT("chunk_used", "uv", l, 0)))
                    copy(vt[:, i, :], ps[:, i, :]).then_inc(*OUT("v_stored", l, i))

            def attention(l):
                pairs = attention_pairs(l)

                def probabilities(n):
                    s, hh = pairs[n]
                    nk = 4 if s else 2
                    act.wait_ge(*GOT("max_done", l, n))
                    if n >= 2:
                        act.wait_ge(*GOT("prob_turned", l, n - 2))
                    else:
                        act.wait_ge(*GOT("zb_scaled", l, 4))
                    for q in range(2):
                        A_(pr[:, n % 2, q, 0:nk * P], ps[:, n % 2 * 2 + q, 0:nk * P], ACT.Exp, scale=MLA_SCALE,
                          bias=st[:, 32 + n % 2 * 8 + q:33 + n % 2 * 8 + q],
                          accum_out=st[:, 34 + n % 2 * 8 + q:35 + n % 2 * 8 + q]).then_inc(*OUT("prob", l, n, q))

                def keep_turned(n):
                    nk = 4 if pairs[n][0] else 2
                    act.wait_ge(*GOT("prob_turned", l, n))
                    if n >= 2:
                        act.wait_ge(*GOT("attended", l, n - 2))
                    copy(prt[:, n % 2, 0:nk * 256].rearrange("p (b k) -> p b k", k=512),
                         ps[:, 4:4 + nk // 2, :]).then_inc(*OUT("pt_kept", l, n))

                def keep_attended(n):
                    s, hh = pairs[n]
                    act.wait_ge(*GOT("attended", l, n))
                    r = slice(hh % 2 * HD, hh % 2 * HD + HD)
                    copy(y[r, 4 + hh // 2, s * CTX:(s + 1) * CTX], ps[r, 6 + n % 2, 0:256]).then_inc(*OUT("yb_kept", l, n))

                probabilities(0)
                for n in range(len(pairs)):
                    if n + 1 < len(pairs):
                        probabilities(n + 1)
                    keep_turned(n)
                    if n:
                        keep_attended(n - 1)
                keep_attended(len(pairs) - 1)

            def gmlp(l):
                t0 = t0_of(l)
                for i in range(4):
                    act.wait_ge(*GOT("chunk_used", "zu", l, i))
                    A_(ut[:, i, t0:], ps[:, 4 + i % 2, t0:], ACT.Gelu_apprx_tanh).then_inc(*OUT("u_gelu", l, i))
                act.wait_ge(*GOT("chunk_used", "zv", l, 3))
                for t in range(t0 // P, NT):
                    A_(vg[:, t, :], ps[:, t, :], ACT.Gelu_apprx_tanh).then_inc(*OUT("v_gelu", l, t))
                for t in range(t0 // P, NT):
                    act.wait_ge(*GOT("v_gelu", l, t))
                    if t > t0 // P:
                        act.wait_ge(*GOT("v_sq", l, t - 1))
                    A_(vsq, vg[:, t, :], ACT.Square, accum_out=st[:, 48 + t:49 + t]).then_inc(*OUT("v_sq", l, t))
                act.wait_ge(*GOT("v_sq", l, NT - 1))
                A_(st[:, 52 + t0 // P:56], st[:, 48 + t0 // P:52], ACT.Sqrt, bias=eps[:, 0:1], scale=1.0 / CW) \
                    .then_inc(*OUT("v_rooted", l))

            def merge(l):
                t0 = t0_of(l)
                if l == 0:
                    act.wait_ge(*GOT("crow_in"))
                    A_(crow, crow, ACT.Silu).then_inc(*OUT("crow_ready"))
                for j in range(KT):
                    for g in range(3):
                        act.wait_ge(*GOT("chunk_used", "gate", l, j, g))
                        if j >= 2:
                            act.wait_ge(*GOT("merged", l, j - 2, 4))
                        elif j == 0 and g == 0:
                            act.wait_ge(*GOT("ya_done", l, 3))
                        A_(sgm[:, j % 2, g, t0:], ps[:, g, t0:], ACT.Sigmoid).then_inc(*OUT("gated", l, j, g))

            def experts(l):
                t0 = t0_of(l)

                def S(name):
                    return sg.sem(f"{name}{l}")
                act.wait_ge(*GOT("routed", l))
                A_(score[:, t0 // P:, :], ps[:, 6, t0 // P * NE:NT * NE].rearrange("p (t e) -> p t e", e=NE), ACT.Sigmoid) \
                    .then_inc(*OUT("scored", l))
                for t in range(t0 // P, NT):
                    act.wait_ge(*GOT("row_turned", l, t))
                    b = t % 2 * 2
                    copy(htok[:, t, :].rearrange("p (b k) -> p b k", b=2), ps[:, b:b + 2, :]).then_inc(*OUT("row_kept", l, t))
                act.wait_ge(*GOT("passes_set", l))
                n_passes = act.value_load(passes[0:1, 0:1], min_val=1, max_val=TOK // CAP)
                x_final[l, "act"] = n_passes * (PAIRS * KT) + KT

                def keep_tokens(u, n):
                    act.wait_ge(S("gathered"), n + (u + 1))
                    copy(xg[u].rearrange("p (b k) -> p b k", b=2), ps[:, 0:2, :]).then_inc(S("xg_kept"), 1)

                def keep_back(u, n):
                    act.wait_ge(S("turned_back"), n + (u + 1))
                    copy(back[u][:, t0:], ps[:, 7, t0:]).then_inc(S("back_kept"), 1)

                def keep_he(u, n):
                    act.wait_ge(S("he_turned"), n + (u + 1))
                    copy(het[u], ps[:, (2, 7)[u], :]).then_inc(S("het_kept"), 1)

                def pair(n, following):
                    for u in range(2):
                        act.wait_ge(S("h13_done"), n + (u + 1))
                        A_(sil[u], ps[:, 3, :], ACT.Silu).then_inc(S("silu_done"), 1)
                        if u == 0:
                            keep_back(0, n)
                    keep_he(0, n)
                    keep_back(1, n)
                    if following:
                        keep_tokens(0, n + 2)
                    keep_he(1, n)
                    for u in range(2):
                        act.wait_ge(S("y_done"), n + (u + 1))
                        b = (5, 3)[u]
                        copy(ye[u], ps[:, b:b + 2, :]).then_inc(S("ye_kept"), 1)
                    if following:
                        keep_tokens(1, n + 2)

                with act.Fori(0, n_passes, 1) as p:
                    for u in range(2):
                        keep_tokens(u, p * NE)
                    with act.Fori(0, PAIRS - 1, 1) as j:
                        pair(act.snap(p * NE + j * 2), True)
                    pair(act.snap(p * NE + (NE - 2)), False)

            def modulation(l):
                for n in range(4):
                    act.wait_ge(*GOT("chunk_used", "mod", l, 4 * n + 3))
                    copy(y[0:2, n, :], ps[0:2, 1 + n % 2, :]).then_inc(*OUT("mod_row", l, n))

            act.wait_ge(*GOT("const_in"))
            A_(ca[:, :, :], cc[:, :, :], ACT.Silu).then_inc(*OUT("cond_ready"))
            for l in range(DEPTH):
                if l == 0:
                    modulation(l)
                norm(l, 0)
                rwkv_inputs(l)
                in_turn(lambda s: rwkv_flow(l, s))
                rwkv_readout(l)
                attention_inputs(l)
                attention(l)
                gmlp(l)
                merge(l)
                norm(l, 1)
                experts(l)
            norm(DEPTH, 0)

        @block.vector
        def _(dve):
            V = dve
            TT = V.tensor_tensor

            def heads(a, n=HEADS):
                return a.rearrange("p (h v) -> p h v", h=n)

            def norm(l, which):
                t0 = 0 if l < DEPTH and which == 0 else CTX if l == DEPTH else t0_of(l)
                V.wait_ge(*GOT("norm_rooted", l, which))
                V.reciprocal(rt[:, t0:], rt[:, t0:]).then_inc(*OUT("norm_rs", l, which))
                V.wait_ge(*GOT("norm_rs", l, which))
                for k in range(KT):
                    if l == DEPTH:
                        V.scalar_tensor_tensor(out=h[:, k, 0:LAT], in0=x[:, k, CTX:], scalar=vec[:, V_FG + k:V_FG + k + 1],
                                               in1=rt[:, t0:], op0=ALU.mult, op1=ALU.mult).then_inc(*OUT("out_ready"))
                    else:
                        TT(h[:, k, t0:], x[:, k, t0:], rt[:, t0:], ALU.mult).then_inc(*OUT("x_scaled", l, which, k))

            def mod_bias(a, b):
                return vec[:, V_MODB + a:V_MODB + b].unsqueeze(2).to_broadcast([P, b - a, 2])

            def norm_gain(q):
                m, g = ((8, V_N1), (32, V_N2))[q]
                return V.scalar_tensor_tensor(out=gain[:, q, :, :], in0=mod[:, m:m + 8, :], scalar=1.0,
                                              in1=vec[:, g:g + 8].unsqueeze(2).to_broadcast([P, 8, 2]),
                                              op0=ALU.add, op1=ALU.mult)

            def modulation_rows(j):
                share = MOD_ROWS // KT
                for row in range(j * share, (j + 1) * share):
                    dst = mod[:, 16 + row, :] if row < 32 else mod_next[:, row - 32, :]
                    V.wait_ge(*GOT(f"mod_row_in{row % 4}", row))
                    for s in range(2):
                        if row:
                            V.wait_ge(*GOT("mod_row_used", row - 1, s))
                        V.tensor_tensor_reduce(mprod[:, s, :], mring[:, row % 4, :], crow[:, s, :], 1.0, 0.0,
                                               ALU.mult, ALU.add, dst[:, s:s + 1]).then_inc(*OUT("mod_row_used", row, s))
                    if row == 31:
                        V.wait_ge(*GOT("mod_row_used", row, 1))
                        TT(mod[:, 16:48, :], mod[:, 16:48, :], mod_bias(16, 48), ALU.add).then_inc(*OUT("mod_rest"))
                        V.wait_ge(*GOT("mod_rest"))
                        norm_gain(1).then_inc(*OUT("mod_step", 0, 1))

            def modulation(l):
                V.wait_ge(*GOT("param_in", l))
                if l:
                    V.wait_ge(sg.sem(f"x_added{l - 1}"), x_final[l - 1, "dve"])
                    TT(mod[:, :, :], mod_next[:, :, :], mod_bias(0, 48), ALU.add).then_inc(*OUT("mod_sum", l))
                else:
                    V.wait_ge(*GOT("mod_turned", l))
                    TT(mod[:, 0:16, :], ps[:, 0, 0:32].rearrange("p (j s) -> p j s", s=2), mod_bias(0, 16),
                       ALU.add).then_inc(*OUT("mod_sum", l))
                V.wait_ge(*GOT("mod_sum", l))
                for q in range(1 if l == 0 else 2):
                    norm_gain(q).then_inc(*OUT("mod_step", l, q))
                mu = vec[:, V_MU:V_MU + 15]
                V.tensor_scalar(mu2[:, 0, :], mu, 0.5, None, ALU.mult).then_inc(*OUT("mod_step", l, 2))
                V.tensor_scalar(mu2[:, 1, :], mu, -1.0, 1.0, ALU.mult, ALU.add).then_inc(*OUT("mod_ready", l))

            def rwkv_inputs(l):
                V.wait_ge(*GOT("x_scaled", l, 0, KT - 1))
                V.memset(view(MB, 1032), 0.0).then_inc(*OUT("raw_clear", l))
                V.memset(rt[:, :], 0.0).then_inc(*OUT("lora_clear", l))
                V.memset(state, 0.0).then_inc(*OUT("state_clear", l))
                V.wait_ge(*GOT("mod_ready", l))
                where = list(range(12)) + [ZW, ZA, ZG]
                for i in range(15):
                    V.wait_ge(*GOT("raw_copied", l, i))
                    if i >= 2:
                        V.wait_ge(*GOT("z_mixed", l, i - 2))
                    r, s_ = raw[:, i % 2, :, :], shs[:, i % 2, :, :]
                    TT(s_, r[:, :, 0:256], r[:, :, 2:258], ALU.add).then_inc(*OUT("z_sides", l, i))
                    V.wait_ge(*GOT("z_sides", l, i))
                    V.tensor_scalar(s_, s_, mu2[:, 0, i:i + 1], None, ALU.mult).then_inc(*OUT("z_half", l, i))
                    V.wait_ge(*GOT("z_half", l, i))
                    V.scalar_tensor_tensor(out=zc[:, where[i], :].rearrange("p (s t) -> p s t", s=2), in0=r[:, :, 1:257],
                                           scalar=mu2[:, 1, i:i + 1], in1=s_, op0=ALU.mult, op1=ALU.add) \
                        .then_inc(*OUT("z_mixed", l, i))
                    f = i - KK_AT - 1
                    if 0 <= f < 4:
                        V.wait_ge(*GOT("kk_summed", l, f))
                        V.tensor_scalar(kks[:, f % 2, :], ps[:, 2 + f % 2, :], 1e-12, None, ALU.max) \
                            .then_inc(*OUT("kk_clamped", l, f))
                        V.wait_ge(*GOT("kk_rooted", l, f))
                        V.reciprocal(kks[:, f % 2, :], kks[:, f % 2, :]).then_inc(*OUT("kk_inv", l, f))
                        V.wait_ge(*GOT("kk_inv", l, f))
                        TT(zc[:, ZKK + f, :], zc[:, ZKK + f, :], kks[:, f % 2, :], ALU.mult).then_inc(*OUT("kk_done", l, f))
                    f = i - KK_AT
                    if 0 <= f < 4:
                        V.wait_ge(*GOT("z_mixed", l, 4 + f))
                        V.tensor_scalar(zc[:, ZKK + f, :], zc[:, ZK + f, :], vec[:, V_KK + f:V_KK + f + 1], None, ALU.mult) \
                            .then_inc(*OUT("kk_raw", l, f))
                        V.wait_ge(*GOT("kk_raw", l, f))
                        if f >= 2:
                            V.wait_ge(*GOT("kk_done", l, f - 2))
                        TT(kks[:, f % 2, :], zc[:, ZKK + f, :], zc[:, ZKK + f, :], ALU.mult).then_inc(*OUT("kk_squared", l, f))
                V.wait_ge(*GOT("kk_done", l, 3))
                V.wait_ge(*GOT("z_mixed", l, 14))
                for s in range(2):
                    V.memset(view(MB + 20 * s * HU * P, 4 * HU * P), 0.0).then_inc(*OUT("blocks_clear", l))
                    V.memset(view(MB + (20 * s + 18) * HU * P, 2 * HU * P), 0.0).then_inc(*OUT("blocks_clear", l))

            def rwkv_flow(l, s):
                for c in range(STEPS):
                    yield from rwkv_step(l, c, s)
                    for u in range(HS // HU):
                        yield from rwkv_unit(l, c, s, u)

            def rwkv_step(l, c, s):
                k = (l, c, s)
                t = units[s]
                T = t.tok
                own = slice(s * 256, (s + 1) * 256)
                r, k_ = ps[:, t.bank, 0:256], ps[:, t.bank, 256:512]
                v, kk = ps[:, t.bank + 1, 0:256], ps[:, t.bank + 1, 256:512]
                if c:
                    V.wait_ge(*GOT("p_s", l, c - 1, s, 1))
                    V.wait_ge(*GOT("bg_in", l, c - 1, s, 1, 2, 1))
                V.wait_ge(*GOT("tokens_turned", *k))
                V.tensor_copy(T[5], v).then_inc(*OUT("v_kept", *k))
                V.wait_ge(*GOT("tanhed", *k, 1))
                both = y[:, 0:2, own]
                V.tensor_scalar(both, both, 0.5, 0.5, ALU.mult, ALU.add).then_inc(*OUT("sig_done", *k))
                yield
                V.wait_ge(*GOT("sig_done", *k))
                TT(T[6], kk, T[1], ALU.mult).then_inc(*OUT("kka", *k))
                V.scalar_tensor_tensor(out=T[7], in0=T[1], scalar=1.0, in1=rep[:, 0, own], op0=ALU.subtract, op1=ALU.mult) \
                    .then_inc(*OUT("kd_half", *k))
                V.wait_ge(*GOT("kd_half", *k))
                V.scalar_tensor_tensor(out=T[7], in0=T[7], scalar=1.0, in1=k_, op0=ALU.add, op1=ALU.mult) \
                    .then_inc(*OUT("kd_done", *k))
                V.wait_ge(*GOT("kd_done", *k))
                TT(T[1], r, T[7], ALU.mult).then_inc(*OUT("bonus_a", *k))
                V.wait_ge(*GOT("bonus_a", *k))
                V.wait_ge(*GOT("exps", *k, 0))
                TT(T[2], r, T[2], ALU.mult).then_inc(*OUT("operand", *k, 3))
                V.wait_ge(*GOT("exps", *k, 1))
                TT(T[3], kk, T[3], ALU.mult).then_inc(*OUT("operand", *k, 2))
                V.wait_ge(*GOT("exps", *k, 2))
                TT(T[6], T[6], T[4], ALU.mult).then_inc(*OUT("operand", *k, 0))
                TT(T[7], T[7], T[4], ALU.mult).then_inc(*OUT("operand", *k, 1))
                yield

            def rwkv_unit(l, c, s, u):
                k = (l, c, s, u)
                t = units[s]
                A, B, C_, D_ = (t.bank + i for i in range(4))

                def bank(b, n=HU):
                    return ps[:, b, 0:n * P].rearrange("p (h t) -> p h t", t=P)

                V.wait_ge(*GOT("turned", *k))
                V.tensor_copy(t.bg, bank(B, 2 * HU)).then_inc(*OUT("bg_kept", *k))
                yield
                V.wait_ge(*GOT("gram", *k))

                def pair(a, lo):
                    return a.rearrange("p b (h t) -> p b h t", t=2 * P)[:, :, :, lo:lo + P]

                def per(m):
                    return con[:, m:m + 2, :].unsqueeze(2).to_broadcast([P, 2, HU, P])
                TT(t.ng.rearrange("p (m h) t -> p m h t", m=2), bank(A).unsqueeze(1).to_broadcast([P, 2, HU, P]), per(C_ND),
                   ALU.mult).then_inc(*OUT("masked", *k, 0))
                TT(t.ntb.rearrange("p (m h) t -> p m h t", m=2), pair(ps[:, C_:C_ + 2, :], 0), per(C_NDT), ALU.mult) \
                    .then_inc(*OUT("masked", *k, 1))
                TT(t.q, ps[:, C_:C_ + 2, :].rearrange("p b (h t) -> p (b h) t", t=2 * P)[:, :, P:],
                   C(C_MI).unsqueeze(1).to_broadcast([P, 2 * HU, P]), ALU.mult).then_inc(*OUT("masked", *k, 2))
                yield
                V.wait_ge(*GOT("p_nt2", *k))
                V.tensor_copy(t.b, bank(B)).then_inc(*OUT("nt2_kept", *k))
                yield
                if u == 0:
                    own = slice(s * 256, (s + 1) * 256)
                    TT(t.tok[1], t.tok[1], rep[:, 1, own], ALU.mult).then_inc(*OUT("bonus_b", l, c, s))
                    V.wait_ge(*GOT("bonus_b", l, c, s))
                    V.tensor_reduce(osb[:, c, CW + s * HS:CW + (s + 1) * HS], heads(t.tok[1], HS), AX.X, ALU.add) \
                        .then_inc(*OUT("bonus_kept", l, c, s))
                V.wait_ge(*GOT("x1b_done", *k))
                V.wait_ge(*GOT("p_nt3", *k))
                TT(t.ma, bank(C_), t.x1, ALU.add).then_inc(*OUT("x2_done", *k))
                yield
                V.wait_ge(*GOT("x2_done", *k))
                V.wait_ge(*GOT("p_x4", *k))
                TT(t.mr, bank(C_), t.ma, ALU.add).then_inc(*OUT("x4_done", *k))
                yield
                V.wait_ge(*GOT("x4_done", *k))
                V.wait_ge(*GOT("p_x8", *k))
                TT(t.xt, bank(B), t.mr, ALU.add).then_inc(*OUT("xt_done", *k))
                yield
                V.wait_ge(*GOT("p_ht", *k))
                V.tensor_copy(t.nt, bank(C_)).then_inc(*OUT("ht_kept", *k))
                yield
                yield
                V.wait_ge(*GOT("w2_done", *k))
                V.wait_ge(*GOT("p_ht3", *k))
                TT(t.nt4, bank(C_), t.nt4, ALU.add).then_inc(*OUT("w_done", *k))
                yield
                yield
                yield
                h0 = s * HS + u * HU
                s_ = state[:, h0:h0 + HU, :]
                V.wait_ge(*GOT("p_s", *k))
                TT(s_, ps[:, C_, 0:HU * HD].rearrange("p (h v) -> p h v", v=HD), s_, ALU.add).then_inc(*OUT("state_sum", *k))
                V.wait_ge(*GOT("state_sum", *k))
                V.wait_ge(*GOT("exps", l, c, s, 3))
                TT(s_, s_, t.end[:, u * HU:(u + 1) * HU].unsqueeze(2).to_broadcast([P, HU, HD]), ALU.mult) \
                    .then_inc(*OUT("state_new", *k))
                yield

            def rwkv_readout(l):
                for i in range(t0_of(l) // P, NT):
                    def spread(a):
                        return a.unsqueeze(2).to_broadcast([P, HEADS, HD])
                    a, b = heads(tok[:, 0, :]), heads(tok[:, 1, :])
                    V.wait_ge(*GOT("read", l, i))
                    if i > t0_of(l) // P:
                        V.wait_ge(*GOT("yc_turned", l, i - 1))
                    V.tensor_reduce(st[:, 8:16], heads(ps[:, 0, :]), AX.X, ALU.add).then_inc(*OUT("ro", l, i, 0))
                    V.tensor_copy(st[:, 24:32], ps[:, 1, 0:8]).then_inc(*OUT("ro", l, i, 1))
                    V.wait_ge(*GOT("ro", l, i, 1))
                    V.tensor_scalar(st[:, 8:16], st[:, 8:16], 1.0 / HD, None, ALU.mult).then_inc(*OUT("ro", l, i, 2))
                    TT(b, heads(ps[:, 2, :]), spread(st[:, 24:32]), ALU.mult).then_inc(*OUT("ro", l, i, 3))
                    V.wait_ge(*GOT("ro", l, i, 2))
                    TT(a, heads(ps[:, 0, :]), spread(st[:, 8:16]), ALU.subtract).then_inc(*OUT("ro", l, i, 4))
                    V.wait_ge(*GOT("ro", l, i, 4))
                    TT(heads(tok[:, 2, :]), a, a, ALU.mult).then_inc(*OUT("ro", l, i, 5))
                    V.wait_ge(*GOT("ro", l, i, 5))
                    V.tensor_reduce(st[:, 16:24], heads(tok[:, 2, :]), AX.X, ALU.add).then_inc(*OUT("var_done", l, i))
                    V.wait_ge(*GOT("var_rooted", l, i))
                    V.reciprocal(st[:, 16:24], st[:, 16:24]).then_inc(*OUT("ro", l, i, 6))
                    V.wait_ge(*GOT("ro", l, i, 6))
                    TT(a, a, spread(st[:, 16:24]), ALU.mult).then_inc(*OUT("ro", l, i, 7))
                    for q, (z, op) in enumerate(((rep[:, 2, :], ALU.mult), (rep[:, 3, :], ALU.add), (tok[:, 1, :], ALU.add))):
                        V.wait_ge(*GOT("ro", l, i, 7 + q))
                        TT(tok[:, 0, :], tok[:, 0, :], z, op).then_inc(*OUT("ro", l, i, 8 + q))
                    V.wait_ge(*GOT("ro", l, i, 10))
                    TT(tok[:, 0, :], ps[:, 3, :], tok[:, 0, :], ALU.mult).then_inc(*OUT("yc_done", l, i))

            def attention_inputs(l):
                t0 = t0_of(l)
                for i in range(2):
                    V.wait_ge(*GOT("zb_rooted", l, i))
                    V.reciprocal(pr[:, 0, i, :], pr[:, 0, i, :]).then_inc(*OUT("zb_inv", l, i))
                for i in range(5):
                    V.wait_ge(*GOT("zb_inv", l, 0 if i < 3 else 1))
                    V.scalar_tensor_tensor(out=zq[:, i, :], in0=zq[:, i, :], scalar=vec[:, V_QN + i:V_QN + i + 1],
                                           in1=pr[:, 0, 0 if i < 3 else 1, :], op0=ALU.mult, op1=ALU.mult) \
                        .then_inc(*OUT("zb_scaled", l, i))

                def rope(src, dst, name, *key):
                    b = rtmp[64:96, :, :, :]
                    TT(b[:, 0, 0, :], src[96:128, CTX:], cs[96:128, 1, :], ALU.mult).then_inc(*OUT("rope_sin", name, *key))
                    TT(b[:, 1, 0, :], src[64:96, CTX:], cs[64:96, 0, :], ALU.mult).then_inc(*OUT("rope_cos", name, *key))
                    V.wait_ge(*GOT("rope_cos", name, *key))
                    return TT(dst, b[:, 0, 0, :], b[:, 1, 0, :], ALU.add)

                V.wait_ge(*GOT("chunk_used", "zb", l, 5))
                V.tensor_copy(kt_[64:96, 0, 0:CTX], ps[64:96, 6, 0:CTX]).then_inc(*OUT("kr_ctx", l))
                rope(ps[:, 6, :], kt_[64:96, 0, CTX:], "k", l).then_inc(*OUT("kr_made", l))
                V.wait_ge(*GOT("kr_made", l))
                V.wait_ge(*GOT("kr_ctx", l))
                V.tensor_copy(kt_[64:96, 1:HEADS, :], kt_[64:96, 0:1, :].to_broadcast([32, HEADS - 1, TOK])) \
                    .then_inc(*OUT("kr_spread", l))
                for hh in range(HEADS):
                    V.wait_ge(*(GOT("q_made", l, hh) if hh % 2 == 0 else GOT("chunk_used", "uq", l, hh // 2)))
                    V.wait_ge(*(GOT("kr_made", l) if hh == 0 else GOT("q_roped", l, hh - 1)))
                    if t0 == 0:
                        V.tensor_copy(qt[64:96, hh, 0:CTX], ps[64:96, 4 + hh % 2, 0:CTX]).then_inc(*OUT("q_mid", l, hh))
                    rope(ps[:, 4 + hh % 2, :], qt[64:96, hh, CTX:], "q", l, hh).then_inc(*OUT("q_roped", l, hh))

            def attention(l):
                pairs = attention_pairs(l)

                def maxima(n):
                    nk = 4 if pairs[n][0] else 2
                    c0 = 32 + n % 2 * 8
                    V.wait_ge(*GOT("scores", l, n))
                    V.tensor_reduce(st[:, c0 + 4:c0 + 6], ps[:, n % 2 * 2:n % 2 * 2 + 2, 0:nk * P], AX.X, ALU.max) \
                        .then_inc(*OUT("max_raw", l, n))
                    V.wait_ge(*GOT("max_raw", l, n))
                    V.tensor_scalar(st[:, c0:c0 + 2], st[:, c0 + 4:c0 + 6], -MLA_SCALE, None, ALU.mult) \
                        .then_inc(*OUT("max_done", l, n))

                maxima(0)
                for n in range(len(pairs)):
                    nk = 4 if pairs[n][0] else 2
                    c0 = 32 + n % 2 * 8
                    if n + 1 < len(pairs):
                        maxima(n + 1)
                    V.wait_ge(*GOT("prob", l, n, 1))
                    V.reciprocal(st[:, c0 + 2:c0 + 4], st[:, c0 + 2:c0 + 4]).then_inc(*OUT("sum_inv", l, n))
                    V.wait_ge(*GOT("sum_inv", l, n))
                    for q in range(2):
                        p_ = pr[:, n % 2, q, 0:nk * P]
                        V.tensor_scalar(p_, p_, st[:, c0 + 2 + q:c0 + 3 + q], None, ALU.mult) \
                            .then_inc(*OUT("prob_scaled", l, n, q))

            def gmlp(l):
                t0 = t0_of(l)
                V.wait_ge(*GOT("v_rooted", l))
                s_ = st[:, 52 + t0 // P:56]
                V.reciprocal(s_, s_).then_inc(*OUT("v_inv", l))
                V.wait_ge(*GOT("v_inv", l))
                for t in range(t0 // P, NT):
                    V.tensor_scalar(vg[:, t, :], vg[:, t, :], st[:, 52 + t:53 + t], None, ALU.mult) \
                        .then_inc(*OUT("v_normed", l, t))
                for g in range(4):
                    V.wait_ge(*GOT("mixed", l, g))
                    o = at[:, g, t0:].rearrange("p (t i) -> p t i", i=P)
                    n = NT - t0 // P
                    V.scalar_tensor_tensor(out=o, in0=ps[:, 4 + g, t0:].rearrange("p (t i) -> p t i", i=P),
                                           scalar=vec[:, V_AVG + g:V_AVG + g + 1],
                                           in1=bs[:, g:g + 1, :].to_broadcast([P, n, P]), op0=ALU.mult, op1=ALU.add) \
                        .then_inc(*OUT("mix_biased", l, g))
                    V.wait_ge(*GOT("mix_biased", l, g))
                    TT(y[:, g, t0:], at[:, g, t0:], ut[:, g, t0:], ALU.mult).then_inc(*OUT("ya_done", l, g))

            def merge(l):
                t0 = t0_of(l)
                if l == 0:
                    V.wait_ge(*GOT("crow_ready"))
                for j in range(KT):
                    if l == 0:
                        modulation_rows(j)
                    V.wait_ge(*GOT("chunk_used", "up", l, j, 1))
                    V.wait_ge(*GOT("gated", l, j, 2))
                    o = mg[:, j, t0:]
                    for g in range(3):
                        s_ = sgm[:, j % 2, g, t0:]
                        TT(s_ if g else o, ps[:, 3 + g, t0:], s_, ALU.mult).then_inc(*OUT("merged", l, j, g))
                    for g in (1, 2):
                        V.wait_ge(*GOT("merged", l, j, g + 1))
                        TT(o, o, sgm[:, j % 2, g, t0:], ALU.add).then_inc(*OUT("merged", l, j, 2 + g))
                for j in range(KT):
                    V.wait_ge(*GOT("chunk_used", "wo", l, j))
                    for s in range(t0 // CTX, 2):
                        r = slice(s * CTX, (s + 1) * CTX)
                        ins = V.scalar_tensor_tensor(out=x[:, j, r], in0=ps[:, 6 + j % 2, r], scalar=mod[:, 16 + j, s:s + 1],
                                                     in1=x[:, j, r], op0=ALU.mult, op1=ALU.add)
                    ins.then_inc(*OUT(f"x_added{l}", j))

            def router(l):
                a = t0_of(l) // P
                n = NT - a
                G = n * NG

                def grp(t):
                    return t[:, a:, :].rearrange("p t (g e) -> p (t g) e", e=EPG)
                rank = small[:, 2 + P + NE:2 + P + NE + EPG]
                dec = rank.unsqueeze(1).to_broadcast([P, G, EPG])
                m = rt[:, 0:16 * 8].rearrange("p (m g) -> p m g", g=16)
                step = [0]

                def run(ins):
                    step[0] += 1
                    ins.then_inc(*OUT("route", l, step[0]))
                    V.wait_ge(*GOT("route", l, step[0]))

                def over(i, e=EPG):
                    return m[:, i, 0:G].unsqueeze(2).to_broadcast([P, G, e])

                def top(src, i, onehot):
                    run(V.tensor_reduce(m[:, i, 0:G], src, AX.X, ALU.max))
                    run(TT(onehot, src, over(i), ALU.is_equal))
                    run(TT(onehot, onehot, dec, ALU.mult))
                    run(V.tensor_reduce(m[:, 7, 0:G], onehot, AX.X, ALU.max))
                    run(TT(onehot, onehot, over(7), ALU.is_equal))

                V.wait_ge(*GOT("scored", l))
                run(TT(sel[:, a:, :], score[:, a:, :], rb[:, :].unsqueeze(1).to_broadcast([P, n, NE]), ALU.add))
                top(grp(sel), 0, grp(first))
                run(V.scalar_tensor_tensor(out=grp(pick), in0=grp(first), scalar=-1e30, in1=grp(sel), op0=ALU.mult, op1=ALU.add))
                top(grp(pick), 1, grp(second))
                run(TT(m[:, 2, 0:G], m[:, 0, 0:G], m[:, 1, 0:G], ALU.add))

                def rows(i):
                    return m[:, i, 0:G].rearrange("p (t g) -> p t g", g=NG)
                dg = rank.unsqueeze(1).to_broadcast([P, n, NG])

                def wide(i):
                    return m[:, i, 0:n].unsqueeze(2).to_broadcast([P, n, NG])
                run(V.tensor_reduce(m[:, 3, 0:n], rows(2), AX.X, ALU.max))
                run(TT(rows(4), rows(2), wide(3), ALU.is_equal))
                run(TT(rows(4), rows(4), dg, ALU.mult))
                run(V.tensor_reduce(m[:, 3, 0:n], rows(4), AX.X, ALU.max))
                run(TT(rows(4), rows(4), wide(3), ALU.is_equal))
                run(TT(grp(first), grp(first), grp(second), ALU.add))
                TT(grp(mask), grp(first), over(4), ALU.mult).then_inc(*OUT("mask_done", l))
                V.wait_ge(*GOT("mask_done", l))
                run(TT(first[:, a:, :], mask[:, a:, :], score[:, a:, :], ALU.mult))
                run(V.tensor_reduce(m[:, 5, 0:n], first[:, a:, :], AX.X, ALU.add))
                run(V.reciprocal(m[:, 5, 0:n], m[:, 5, 0:n]))
                run(TT(comb[:, a:, :], first[:, a:, :], m[:, 5, 0:n].unsqueeze(2).to_broadcast([P, n, NE]), ALU.mult))
                V.wait_ge(*GOT("placed", l))
                pos = ps[:, 6, 64 + a * NE:64 + NT * NE].rearrange("p (t e) -> p t e", e=NE)
                run(V.scalar_tensor_tensor(out=place[:, a:, :], in0=pos, scalar=-FAR, in1=mask[:, a:, :], op0=ALU.add, op1=ALU.mult))
                run(V.tensor_scalar(place[:, a:, :], place[:, a:, :], FAR, None, ALU.add))
                run(V.tensor_reduce(m[:, 6, 0:1], ps[:, 6, 128:128 + NE], AX.X, ALU.max))
                run(V.tensor_scalar(m[:, 6, 1:2], m[:, 6, 0:1], float(CAP), 1.0, ALU.is_gt, ALU.add))
                for i in range(2, TOK // CAP):
                    run(V.tensor_scalar(m[:, 6, 2:3], m[:, 6, 0:1], float(i * CAP), None, ALU.is_gt))
                    run(TT(m[:, 6, 1:2], m[:, 6, 1:2], m[:, 6, 2:3], ALU.add))
                run(V.tensor_scalar(slots, C(C_IOTA), -float(CAP), None, ALU.add))
                V.tensor_copy(passes[:, :], m[:, 6, 1:2]).then_inc(*OUT("passes_set", l))

            def experts(l):
                t0 = t0_of(l)
                a = t0 // P
                nt = NT - a

                def S(name):
                    return sg.sem(f"{name}{l}")
                V.wait_ge(*GOT("passes_set", l))
                V.wait_ge(*GOT("row_turned", l, NT - 1))
                n_passes = V.value_load(passes[0:1, 0:1], min_val=1, max_val=TOK // CAP)
                x_final[l, "dve"] = n_passes * (PAIRS * KT) + KT
                sl = slots.unsqueeze(1).to_broadcast([P, nt, CAP])

                def of_expert(block, e):
                    c = wsf[:, block * 64 + a * NE:][:, 0:nt * NE].rearrange("p (t e) -> p t e", e=NE)
                    return c[:, :, bass.ds(e, 1)].to_broadcast([P, nt, CAP])

                def pick_slots(u, n, e):
                    TT(pk[u][:, a:, :], sl, of_expert(7, e), ALU.is_equal).then_inc(S("picks"), 1)

                def weigh(u, n, e):
                    V.wait_ge(S("picks"), n + (u + 1))
                    TT(pkw[u][:, a:, :], pk[u][:, a:, :], of_expert(5, e), ALU.mult).then_inc(S("weighted"), 1)

                def pair(n, m, j):
                    for u in range(2):
                        V.wait_ge(S("silu_done"), n + (u + 1))
                        TT(he[u], ps[:, 4, :], sil[u], ALU.mult).then_inc(S("he_done"), 1)
                        if j is not None:
                            if u == 0:
                                for v in range(2):
                                    V.wait_ge(S("weighted"), n + (v + 1))
                                    pick_slots(v, n + 2, j * 2 + (2 + v))
                            V.wait_ge(S("turned_back"), n + (u + 1))
                            weigh(u, n + 2, j * 2 + (2 + u))
                    for d in range(KT):
                        V.wait_ge(S("scattered"), m * KT + (d + 1))
                        V.wait_ge(S("x_added"), m * KT + (d + 1))
                        for s in range(t0 // CTX, 2):
                            r = slice(s * CTX, (s + 1) * CTX)
                            ins = V.scalar_tensor_tensor(out=x[:, d, r], in0=ps[:, 3 + d % 4, r],
                                                         scalar=mod[:, 40 + d, s:s + 1], in1=x[:, d, r],
                                                         op0=ALU.mult, op1=ALU.add)
                        ins.then_inc(S("x_added"), 1)

                with V.Fori(0, n_passes, 1) as p:
                    V.wait_ge(S("x_added"), p * (PAIRS * KT) + KT)
                    V.tensor_scalar(slots, slots, float(CAP), None, ALU.add).then_inc(S("slots_moved"), 1)
                    V.wait_ge(S("slots_moved"), p + 1)
                    for u in range(2):
                        pick_slots(u, p * NE, u)
                        weigh(u, p * NE, u)
                    with V.Fori(0, PAIRS - 1, 1) as j:
                        m = V.snap(p * PAIRS + j)
                        pair(V.snap(m * 2), m, j)
                    m = V.snap(p * PAIRS + (PAIRS - 1))
                    pair(V.snap(m * 2), m, None)

            V.memset(eps[:, 0:1], EPS).then_inc(*OUT("eps_half"))
            V.memset(eps[:, 1:2], GN_EPS).then_inc(*OUT("eps_set"))
            V.wait_ge(*GOT("const_in"))
            for l in range(DEPTH):
                modulation(l)
                norm(l, 0)
                rwkv_inputs(l)
                in_turn(lambda s: rwkv_flow(l, s))
                rwkv_readout(l)
                attention_inputs(l)
                attention(l)
                gmlp(l)
                merge(l)
                norm(l, 1)
                router(l)
                experts(l)
            norm(DEPTH, 0)

        @block.gpsimd
        def _(pool):
            last = []

            def alone():
                if last:
                    pool.wait_ge(*GOT(*last[-1]))

            def run(ins, *key):
                ins.then_inc(*OUT(*key))
                last.append(key)

            def rwkv_flow(l, s):
                for c in range(STEPS):
                    yield from rwkv_step(l, c, s)
                    for u in range(HS // HU):
                        yield from rwkv_unit(l, c, s, u)

            def rwkv_step(l, c, s):
                t = units[s]
                if c == 0:
                    pool.wait_ge(*GOT("z_mixed", l, 14))
                    pool.wait_ge(*GOT("blocks_clear", l))
                else:
                    pool.wait_ge(*GOT("tokens_turned", l, c - 1, s))
                for d in range(2):
                    a = chunk_start(c, d)
                    alone()
                    run(pool.tensor_copy(t.stage[:, :, d * CH:(d + 1) * CH].rearrange("p (q f) t -> p q f t", f=2),
                                         zc[:, 0:16, a:a + CH].rearrange("p (q f) t -> p q f t", f=4)[:, :, 2 * s:2 * s + 2, :]),
                        "staged", l, c, s, d)
                yield
                yield

            def rwkv_unit(l, c, s, u):
                k = (l, c, s, u)
                t = units[s]
                prev = (l, c, s, 0) if u else (l, c - 1, s, 1)
                if c or u:
                    pool.wait_ge(*GOT("xt_done", *prev))
                for q, m, i in ((1, t.mr, 2),):
                    pool.wait_ge(*GOT("operand", l, c, s, 2 + q))
                    for d in range(2):
                        r = slice(d * CH, (d + 1) * CH)
                        alone()
                        run(pool.tensor_copy(m[r, :, d * HD:(d + 1) * HD],
                                             t.tok[i][r, u * P:(u + 1) * P].rearrange("p (h v) -> p h v", v=HD)),
                            "ar_in", *k, q, d)
                yield
                eye = C(C_ID).unsqueeze(1).to_broadcast([P, HU, P])
                pool.wait_ge(*GOT("masked", *k, 1))
                alone()
                run(pool.tensor_tensor(t.x1, t.nt, eye, ALU.add), "x1_done", *k)
                yield
                pool.wait_ge(*GOT("nt2_kept", *k))
                alone()
                run(pool.tensor_tensor(t.x1, t.x1, t.b, ALU.add), "x1b_done", *k)
                yield
                yield
                yield
                yield
                pool.wait_ge(*GOT("ht_kept", *k))
                alone()
                run(pool.tensor_tensor(t.nt4, t.nt, eye, ALU.add), "w1_done", *k)
                yield
                pool.wait_ge(*GOT("ht2_kept", *k))
                alone()
                run(pool.tensor_tensor(t.nt4, t.nt4, t.n4, ALU.add), "w2_done", *k)
                yield
                yield
                yield
                yield
                yield

            for l in range(DEPTH):
                in_turn(lambda s: rwkv_flow(l, s))

        return sg.at


def layout(i):
    def chunk(wt):
        k, n = wt.shape[-2:]
        a = np.moveaxis(wt.reshape(wt.shape[:-2] + (k // P, P, n)), -3, -2)
        return a.reshape(a.shape[:-2] + (k // P * n,))

    def chunks(wt):
        L_, k, n = wt.shape
        a = wt.reshape(L_, k // P, P, n // P, P).transpose(0, 3, 2, 1, 4)
        return a.reshape(L_, n // P, P, k)

    def cols(v):
        return v.reshape(-1, P).T

    def per(f):
        return np.stack([f(l) for l in range(DEPTH)])
    swap = np.array([a * 16 + (1 - b) * 8 + f for a in range(2) for b in range(2) for f in range(8)])
    w_in = i["w_in"]
    b_cols = QL + KVL + ROPE
    c_cols = 15 * P
    kr = w_in[:, :, QL + KVL:b_cols]
    zb = np.concatenate([w_in[:, :, :QL + KVL], kr, kr, kr, kr[:, :, swap]], -1)
    a0 = b_cols + c_cols
    uq = i["b_w_uq"].reshape(DEPTH, QL, HEADS, QK)
    uq = np.concatenate([uq, uq[..., NOPE + swap]], -1).reshape(DEPTH, 3, P, 4, 2, P).transpose(0, 3, 2, 4, 1, 5)
    ukv = i["b_w_ukv"].reshape(DEPTH, 2, P, HEADS, NOPE + VD)
    up = np.stack([i["w_up_a"], i["w_up_b"], i["w_up_c"]], 1).reshape(DEPTH, 3, 4, P, KT, P)
    zv = w_in[:, :, a0 + CW:a0 + 2 * CW].reshape(DEPTH, 4, 2, P, CW).transpose(0, 1, 3, 2, 4)
    ones = np.ones((1, P, 1), np.float32)

    def spread(v):
        return np.broadcast_to(v, (P,) + v.shape)
    xs = np.concatenate([i["ctx"][0], i["x"][0]], 0)
    d = {
        "x": xs.T.reshape(KT, P, TOK).transpose(1, 0, 2),
        "cc": np.stack([i["c_ctx"], i["c"][0]], -1).reshape(KT, P, 2).transpose(1, 0, 2),
        "con": constants(), "small": small_constants(), "cs": rope_tables()[64:],
        "rw": i["router_w"].reshape(KT, P, NE).transpose(1, 0, 2),
        "rb": spread(i["router_b"]),
        "mod": i["mod_w"][0, :, :2048].reshape(4, 2, P, 4, 512).transpose(3, 0, 2, 1, 4).reshape(16, P, SLOT),
        "mrow": np.concatenate([i["mod_w"][0].T.reshape(48, P, D)[16:], i["mod_w"][1].T.reshape(48, P, D)]),
        "crow": spread(np.stack([i["c_ctx"], i["c"][0]])),
        "zc": chunks(w_in[:, :, b_cols:a0]),
        "zb": chunks(zb),
        "uq": uq.reshape(DEPTH, 4, P, 768),
        "uk": ukv[..., :NOPE].transpose(0, 2, 3, 1, 4).reshape(DEPTH, P, SLOT),
        "uv": ukv[..., NOPE:].transpose(0, 2, 1, 3, 4).reshape(DEPTH, P, SLOT),
        "zu": chunks(w_in[:, :, a0:a0 + CW]),
        "zv": zv.reshape(DEPTH, 4, P, SLOT),
        "gate": chunks(w_in[:, :, a0 + 2 * CW:]),
        "up": up.transpose(0, 4, 3, 1, 2, 5).reshape(DEPTH, KT, P, 1536),
        "wo": chunks(i["w_o"]),
        "w13": np.concatenate([i["moe_w1"], i["moe_w3"]], -1).reshape(DEPTH, NE, KT, P, 2 * DE).transpose(0, 1, 3, 2, 4),
        "w2": i["moe_w2"].reshape(DEPTH, NE, 4, P, D).transpose(0, 1, 3, 2, 4),
        "vec": per(lambda l: np.concatenate([cols(i[n][l]) for n in ("norm1_g", "norm2_g", "mod_b", "b_q_norm", "b_kv_norm",
                                             "a_v_gain", "c_mu", "c_k_k")] + [cols(i["final_g"])], 1)),
        "rep": per(lambda l: spread(np.stack([i["c_k_a"][l], i["c_r_k"][l].reshape(-1), i["c_gn_g"][l], i["c_gn_b"][l]]))),
        "lora": per(lambda l: np.stack([i["c_w2"][l].reshape(P, CW), i["c_a2"][l].reshape(P, CW), i["c_g2"][l]], 1)),
        "bias2": per(lambda l: np.stack([i["c_w0"][l], i["c_a0"][l]], 1)),
        "bs": per(lambda l: spread(i["a_bs"][l])),
        "ws": i["a_ws"].transpose(0, 3, 1, 2),
    }
    return {k: np.ascontiguousarray(v) for k, v in d.items()}


def kernel(**inputs):
    import concourse.bacc as bacc
    from concourse.bass_utils import run_bass_kernel_spmd as run

    arrays = layout({k: np.asarray(v) for k, v in inputs.items()})
    known = None
    for _ in range(2):
        nc = bacc.Bacc("TRN2", target_bir_lowering=False, num_devices=1)
        w = {k: nc.dram_tensor(f"in_{k}", v.shape, F32, kind="ExternalInput").ap() for k, v in arrays.items()}
        out = nc.dram_tensor("out", (P, KT, LAT), F32, kind="ExternalOutput").ap()
        known = build(nc, w, out, known)
    r = run(nc, [{f"in_{k}": v for k, v in arrays.items()}], core_ids=[0])
    return r.results[0]["out"].transpose(2, 1, 0).reshape(1, LAT, D)
```
